# Optimizing a Trainium2 kernel written in Bass

```python
import jax, jax.numpy as jnp
from jax import lax
import numpy as np

D_MODEL = 2048
BATCH = 1
SEQ = 512
DEPTH = 1
DEC_BATCH = 1
DEC_SEQ = 64
PAST_LEN = 256

CHUNK = 64
N_META = 16
EPS = 1e-6

MLSTM_H = 8
MLSTM_DH = 128
MLSTM_W = MLSTM_H * MLSTM_DH
HGRN_H = 4
HGRN_DK = 128
HGRN_DV = 128
HGRN_W = HGRN_H * HGRN_DV
RWKV_H = 8
RWKV_DH = 64
RWKV_W = RWKV_H * RWKV_DH
RWKV_RANK_W = 64
RWKV_RANK_A = 64
RWKV_GN_EPS = 64e-5
N_BRANCH = 3

A_SIZES = (MLSTM_W, MLSTM_W, MLSTM_W, MLSTM_H, MLSTM_H, MLSTM_W, MLSTM_W)
B_SIZES = (HGRN_H * HGRN_DK, HGRN_H * HGRN_DK, HGRN_W, HGRN_W)
C_SIZES = (RWKV_W, RWKV_W, RWKV_W, RWKV_RANK_W, RWKV_RANK_A, RWKV_W)
G_SIZES = (D_MODEL,) * N_BRANCH
A_COLS = sum(A_SIZES)
B_COLS = sum(B_SIZES)
C_COLS = sum(C_SIZES)
G_COLS = sum(G_SIZES)
N_IN = A_COLS + B_COLS + C_COLS + G_COLS

kernel_name = 'hybrid_mlstm_hgrn2_rwkv7_stream_step'

def f32(a):
    return a.astype(jnp.float32)

def split_cols(p, sizes):
    idx = [int(i) for i in np.cumsum(sizes)[:-1]]
    return jnp.split(p, idx, axis=-1)

def rmsnorm(x, g):
    xf = f32(x)
    y = xf * lax.rsqrt(jnp.mean(xf * xf, axis=-1, keepdims=True) + EPS)
    return (y * f32(g)).astype(x.dtype)

def heads_first(a, n_heads):
    b, t, _ = a.shape
    return a.reshape(b, t, n_heads, -1).transpose(0, 2, 1, 3)

def to_chunks(a, length):
    b, h, t = a.shape[:3]
    a = a.reshape((b, h, t // length, length) + a.shape[3:])
    return jnp.moveaxis(a, 2, 0)

def from_chunks(a):
    a = jnp.moveaxis(a, 0, 2)
    return a.reshape(a.shape[:2] + (-1,) + a.shape[4:])

def run_segments(step, state, xs, segments):
    outs = []
    for t0, t1, length in segments:
        seg = tuple(to_chunks(a[:, :, t0:t1], length) for a in xs)
        state, out = lax.scan(step, state, seg)
        outs.append(from_chunks(out))
    return state, jnp.concatenate(outs, axis=2)

def mlstm_step(carry, inp):
    c, n, m = carry
    q, k, v, ig, lf = inp
    length = q.shape[2]
    causal = jnp.tril(jnp.ones((length, length), dtype=bool))
    b = jnp.cumsum(lf, axis=-1)
    d = jnp.where(causal, b[..., :, None] - b[..., None, :] + ig[..., None, :], -jnp.inf)
    inter = b + m[..., None]
    m_t = jnp.maximum(inter, jnp.max(d, axis=-1))
    w_inter = jnp.exp(inter - m_t)
    s = jnp.einsum('bhtk,bhsk->bhts', q, k) * jnp.exp(d - m_t[..., None])
    num = w_inter[..., None] * jnp.einsum('bhvk,bhtk->bhtv', c, q) + jnp.einsum('bhts,bhsv->bhtv', s, v)
    den = w_inter * jnp.einsum('bhk,bhtk->bht', n, q) + jnp.sum(s, axis=-1)
    h = num / jnp.maximum(jnp.abs(den), jnp.exp(-m_t))[..., None]
    b_end = b[..., -1]
    g = b_end[..., None] - b + ig
    m_new = jnp.maximum(b_end + m, jnp.max(g, axis=-1))
    w_old = jnp.exp(b_end + m - m_new)
    w_s = jnp.exp(g - m_new[..., None])
    c_new = w_old[..., None, None] * c + jnp.einsum('bhs,bhsv,bhsk->bhvk', w_s, v, k)
    n_new = w_old[..., None] * n + jnp.einsum('bhs,bhsk->bhk', w_s, k)
    return (c_new, n_new, m_new), h

def hgrn_step(s_state, inp):
    q, k, v, lf = inp
    length = q.shape[2]
    causal = jnp.tril(jnp.ones((length, length), dtype=bool))[:, :, None]
    a = jnp.cumsum(lf, axis=2)
    rel = jnp.where(causal, a[:, :, :, None, :] - a[:, :, None, :, :], -jnp.inf)
    scores = jnp.einsum('bhtk,bhsk,bhtsk->bhts', q, k, jnp.exp(rel))
    o = jnp.einsum('bhtk,bhkv->bhtv', q * jnp.exp(a), s_state) + jnp.einsum('bhts,bhsv->bhtv', scores, v)
    a_end = a[:, :, -1:]
    s_new = jnp.exp(a_end[:, :, 0])[..., None] * s_state + jnp.einsum('bhsk,bhsv->bhkv', k * jnp.exp(a_end - a), v)
    return s_new, o

def rwkv_step(s_state, inp):
    r, w, k, v, kk, a = inp
    sa = jnp.einsum('bhvk,bhk->bhv', s_state, -kk)
    s_new = (s_state * w[:, :, None, :] + sa[..., None] * (kk * a)[:, :, None, :]
             + v[..., None] * k[:, :, None, :])
    y = jnp.einsum('bhvk,bhk->bhv', s_new, r)
    return s_new, y

def mlstm_branch(pa, p, state, segments):
    bsz, t, _ = pa.shape
    q, k, v, ig, fg, og, z = split_cols(f32(pa), A_SIZES)
    q = heads_first(q, MLSTM_H)
    k = heads_first(k, MLSTM_H) * (MLSTM_DH ** -0.5)
    v = heads_first(v, MLSTM_H)
    ig = (ig + p['mlstm_b_i']).transpose(0, 2, 1)
    lf = jax.nn.log_sigmoid(fg + p['mlstm_b_f']).transpose(0, 2, 1)
    state, h = run_segments(mlstm_step, tuple(f32(s) for s in state), (q, k, v, ig, lf), segments)
    h = h.transpose(0, 2, 1, 3)
    mu = jnp.mean(h, axis=-1, keepdims=True)
    var = jnp.mean(jnp.square(h - mu), axis=-1, keepdims=True)
    h = ((h - mu) * lax.rsqrt(var + EPS)).reshape(bsz, t, MLSTM_W) * p['mlstm_norm']
    return h * jax.nn.sigmoid(og) * jax.nn.silu(z), state

def hgrn_branch(pb, p, lb, s_state, segments):
    bsz, t, _ = pb.shape
    q, fp, i, z = split_cols(f32(pb), B_SIZES)
    f = lb + (1.0 - lb) * jax.nn.sigmoid(fp)
    lf = heads_first(jnp.log(f), HGRN_H)
    k = heads_first((1.0 - lb) * jax.nn.sigmoid(-fp), HGRN_H)
    s_state, o = run_segments(hgrn_step, f32(s_state),
                              (heads_first(q, HGRN_H), k, heads_first(i, HGRN_H), lf), segments)
    o = o.transpose(0, 2, 1, 3)
    o = o * lax.rsqrt(jnp.mean(o * o, axis=-1, keepdims=True) + EPS)
    return o.reshape(bsz, t, HGRN_W) * p['hgrn_norm'] * jax.nn.silu(z), s_state

def rwkv_branch(pc, p, shift, s_state):
    pc = f32(pc)
    bsz, t, _ = pc.shape
    prev = jnp.concatenate([f32(shift), pc[:, :-1]], axis=1)
    xs = pc + p['rwkv_mu'] * (prev - pc)
    r, k, v, wd, ad, z = split_cols(xs, C_SIZES)
    w_logit = -jax.nn.softplus(-(p['rwkv_w0'] + jnp.tanh(wd) @ p['rwkv_w_up'])) - 0.5
    decay = jnp.exp(-jnp.exp(w_logit))
    a = jax.nn.sigmoid(p['rwkv_a0'] + ad @ p['rwkv_a_up'])

    def split_h(u):
        return u.reshape(bsz, t, RWKV_H, RWKV_DH)

    def time_major(u):
        return u.transpose(1, 0, 2, 3)

    kk = split_h(k * p['rwkv_k_k'])
    kk = kk / jnp.maximum(jnp.sqrt(jnp.sum(kk * kk, axis=-1, keepdims=True)), 1e-12)
    k = k * (1.0 + (a - 1.0) * p['rwkv_k_a'])
    r, k, v, decay, a = (split_h(u) for u in (r, k, v, decay, a))
    s_state, y = lax.scan(rwkv_step, f32(s_state), tuple(time_major(u) for u in (r, decay, k, v, kk, a)))
    y = time_major(y)
    mu = jnp.mean(y, axis=-1, keepdims=True)
    var = jnp.mean(jnp.square(y - mu), axis=-1, keepdims=True)
    y = ((y - mu) * lax.rsqrt(var + RWKV_GN_EPS) * p['rwkv_gn_g'].reshape(RWKV_H, RWKV_DH)
         + p['rwkv_gn_b'].reshape(RWKV_H, RWKV_DH))
    bonus = jnp.sum(r * k * p['rwkv_r_k'].reshape(RWKV_H, RWKV_DH), axis=-1, keepdims=True) * v
    out = (y + bonus).reshape(bsz, t, RWKV_W) * jax.nn.silu(z)
    return out, pc[:, -1:], s_state

def layer(x, p, lb, state, segments):
    c, n, m, s_h, s_r, shift = state
    h = rmsnorm(x, p['norm_pre'])
    proj = h @ p['w_in']
    pa, pb, pc, pg = split_cols(proj, (A_COLS, B_COLS, C_COLS, G_COLS))
    ya, (c, n, m) = mlstm_branch(pa, p, (c, n, m), segments)
    yb, s_h = hgrn_branch(pb, p, lb, s_h, segments)
    yc, shift, s_r = rwkv_branch(pc, p, shift, s_r)
    ga, gb, gc = split_cols(jax.nn.sigmoid(f32(pg)), G_SIZES)
    dt = h.dtype
    merged = (ga * (ya.astype(dt) @ p['w_proj_a']) + gb * (yb.astype(dt) @ p['w_proj_b'])
              + gc * (yc.astype(dt) @ p['w_proj_c']))
    y = merged.astype(dt) @ p['w_out']
    return x + rmsnorm(y, p['norm_post']), (c, n, m, s_h, s_r, shift)

def setup_inputs(seed: int = 0) -> dict:
    key = jax.random.key(seed)
    ks = jax.random.split(key, 40)

    def nrm(i, shape, scale=1.0):
        return scale * jax.random.normal(ks[i], shape, jnp.float32)

    return {
        'x_prompt': nrm(0, (BATCH, SEQ, D_MODEL)),
        'x_sample': nrm(1, (DEC_BATCH, DEC_SEQ, D_MODEL)),
        'state_mlstm_C': nrm(2, (DEPTH, DEC_BATCH, MLSTM_H, MLSTM_DH, MLSTM_DH), 0.5),
        'state_mlstm_n': nrm(3, (DEPTH, DEC_BATCH, MLSTM_H, MLSTM_DH), 0.5),
        'state_mlstm_m': nrm(4, (DEPTH, DEC_BATCH, MLSTM_H), 0.5),
        'state_hgrn_S': nrm(5, (DEPTH, DEC_BATCH, HGRN_H, HGRN_DK, HGRN_DV), 0.5),
        'state_rwkv_S': nrm(6, (DEPTH, DEC_BATCH, RWKV_H, RWKV_DH, RWKV_DH), 0.5),
        'cache_rwkv_shift': nrm(7, (DEPTH, DEC_BATCH, 1, C_COLS)),
        'meta_tokens': nrm(8, (N_META, D_MODEL)),
        'norm_pre': 1.0 + nrm(9, (DEPTH, D_MODEL), 0.05),
        'norm_post': 1.0 + nrm(10, (DEPTH, D_MODEL), 0.05),
        'w_in': nrm(11, (DEPTH, D_MODEL, N_IN), D_MODEL ** -0.5),
        'mlstm_b_i': nrm(12, (DEPTH, MLSTM_H), 0.1),
        'mlstm_b_f': 3.0 + nrm(13, (DEPTH, MLSTM_H), 0.5),
        'mlstm_norm': 1.0 + nrm(14, (DEPTH, MLSTM_W), 0.05),
        'hgrn_lb_logits': nrm(15, (DEPTH, HGRN_H * HGRN_DK), 0.5),
        'hgrn_norm': 1.0 + nrm(16, (DEPTH, HGRN_W), 0.05),
        'rwkv_mu': jax.random.uniform(ks[17], (DEPTH, C_COLS), jnp.float32),
        'rwkv_w0': -2.0 + nrm(18, (DEPTH, RWKV_W), 0.5),
        'rwkv_w_up': nrm(19, (DEPTH, RWKV_RANK_W, RWKV_W), 0.5 * RWKV_RANK_W ** -0.5),
        'rwkv_a0': nrm(20, (DEPTH, RWKV_W), 0.1),
        'rwkv_a_up': nrm(21, (DEPTH, RWKV_RANK_A, RWKV_W), 0.5 * RWKV_RANK_A ** -0.5),
        'rwkv_k_k': 0.85 + nrm(22, (DEPTH, RWKV_W), 0.05),
        'rwkv_k_a': 1.0 + nrm(23, (DEPTH, RWKV_W), 0.05),
        'rwkv_r_k': nrm(24, (DEPTH, RWKV_W), 0.1),
        'rwkv_gn_g': 1.0 + nrm(25, (DEPTH, RWKV_W), 0.05),
        'rwkv_gn_b': nrm(26, (DEPTH, RWKV_W), 0.01),
        'w_proj_a': nrm(27, (DEPTH, MLSTM_W, D_MODEL), MLSTM_W ** -0.5),
        'w_proj_b': nrm(28, (DEPTH, HGRN_W, D_MODEL), HGRN_W ** -0.5),
        'w_proj_c': nrm(29, (DEPTH, RWKV_W, D_MODEL), RWKV_W ** -0.5),
        'w_out': nrm(30, (DEPTH, D_MODEL, D_MODEL), D_MODEL ** -0.5),
    }

def reference(x_prompt, x_sample, state_mlstm_C, state_mlstm_n, state_mlstm_m, state_hgrn_S,
              state_rwkv_S, cache_rwkv_shift, meta_tokens, norm_pre, norm_post, w_in,
              mlstm_b_i, mlstm_b_f, mlstm_norm, hgrn_lb_logits, hgrn_norm, rwkv_mu, rwkv_w0,
              rwkv_w_up, rwkv_a0, rwkv_a_up, rwkv_k_k, rwkv_k_a, rwkv_r_k, rwkv_gn_g, rwkv_gn_b,
              w_proj_a, w_proj_b, w_proj_c, w_out):
    bp, t_p, _ = x_prompt.shape
    t_s = x_sample.shape[1]
    sm = jax.nn.softmax(f32(hgrn_lb_logits), axis=0)
    lb_all = jnp.cumsum(sm, axis=0) - sm[0]

    meta = jnp.broadcast_to(meta_tokens.astype(x_prompt.dtype)[None], (bp, N_META, D_MODEL))
    x_p = jnp.concatenate([meta, x_prompt], axis=1)
    x_s = x_sample
    seg_p = ((0, N_META, N_META), (N_META, N_META + t_p, CHUNK))
    seg_s = ((0, t_s, t_s),)
    init_p = (jnp.zeros((bp, MLSTM_H, MLSTM_DH, MLSTM_DH), jnp.float32),
              jnp.zeros((bp, MLSTM_H, MLSTM_DH), jnp.float32),
              jnp.zeros((bp, MLSTM_H), jnp.float32),
              jnp.zeros((bp, HGRN_H, HGRN_DK, HGRN_DV), jnp.float32),
              jnp.zeros((bp, RWKV_H, RWKV_DH, RWKV_DH), jnp.float32),
              jnp.zeros((bp, 1, C_COLS), jnp.float32))
    outs_p = []
    outs_s = []
    for l in range(DEPTH):
        p = {
            'norm_pre': norm_pre[l], 'norm_post': norm_post[l], 'w_in': w_in[l],
            'mlstm_b_i': f32(mlstm_b_i[l]), 'mlstm_b_f': f32(mlstm_b_f[l]), 'mlstm_norm': f32(mlstm_norm[l]),
            'hgrn_norm': f32(hgrn_norm[l]),
            'rwkv_mu': f32(rwkv_mu[l]), 'rwkv_w0': f32(rwkv_w0[l]), 'rwkv_w_up': f32(rwkv_w_up[l]),
            'rwkv_a0': f32(rwkv_a0[l]), 'rwkv_a_up': f32(rwkv_a_up[l]), 'rwkv_k_k': f32(rwkv_k_k[l]),
            'rwkv_k_a': f32(rwkv_k_a[l]), 'rwkv_r_k': f32(rwkv_r_k[l]), 'rwkv_gn_g': f32(rwkv_gn_g[l]),
            'rwkv_gn_b': f32(rwkv_gn_b[l]),
            'w_proj_a': w_proj_a[l], 'w_proj_b': w_proj_b[l], 'w_proj_c': w_proj_c[l], 'w_out': w_out[l],
        }
        x_p, st_p = layer(x_p, p, lb_all[l], init_p, seg_p)
        st_in = (state_mlstm_C[l], state_mlstm_n[l], state_mlstm_m[l], state_hgrn_S[l],
                 state_rwkv_S[l], cache_rwkv_shift[l])
        x_s, st_s = layer(x_s, p, lb_all[l], st_in, seg_s)
        outs_p.append(st_p)
        outs_s.append(st_s)

    mlstm_C_p, mlstm_n_p, mlstm_m_p, hgrn_S_p, rwkv_S_p, rwkv_shift_p = (
        jnp.stack([o[j] for o in outs_p]) for j in range(6))
    mlstm_C_s, mlstm_n_s, mlstm_m_s, hgrn_S_s, rwkv_S_s, rwkv_shift_s = (
        jnp.stack([o[j] for o in outs_s]) for j in range(6))
    y_prompt = x_p[:, N_META:]
    y_sample = x_s
    return (y_prompt, y_sample, mlstm_C_p, mlstm_n_p, mlstm_m_p, hgrn_S_p, rwkv_S_p, rwkv_shift_p,
            mlstm_C_s, mlstm_n_s, mlstm_m_s, hgrn_S_s, rwkv_S_s, rwkv_shift_s)


_drawn_inputs = setup_inputs


def setup_inputs(seed=0):
    import zlib

    import numpy as np

    out = dict(_drawn_inputs(seed))
    spreads = {}
    factors = {'mlstm_norm': 4.14, 'rwkv_k_k': 2.929, 'rwkv_gn_g': 2.754, 'rwkv_gn_b': 8.0}
    for name, (base, spread) in spreads.items():
        noise = np.random.default_rng([zlib.crc32(name.encode()), seed]).standard_normal(out[name].shape)
        drawn = base * np.exp(spread * noise) if base else spread * noise
        out[name] = __import__('jax').numpy.asarray(drawn.astype(out[name].dtype))
    for name, factor in factors.items():
        out[name] = (out[name] * factor).astype(out[name].dtype)
    return out
```

```python
from contextlib import ExitStack

import numpy as np

import concourse.bass as bass
from concourse import mybir

F32 = mybir.dt.float32
F32R = mybir.dt.float32r
ALU = mybir.AluOpType
ACT = mybir.ActivationFunctionType
AX = mybir.AxisListType

P = 128
D = 2048
KT = D // P
NS, NM, NP = 64, 16, 512
T = NS + NM + NP
HALF = T // 2
C0 = NS + NM
NCH = 5
START = [0] + [C0 + P * c for c in range(4)]
LEN = [C0] + [P] * 4
ENDS = [NS - 1, C0 - 1] + [C0 + P * c - 1 for c in range(1, 5)]
SPLIT = START[3]
EPS = 1e-6
GN_EPS = 64e-5
NH_A, NH_B, NP_C = 8, 4, 4
LEVELS = 7

A_TILES, C_TILES, B_TILES = 8, 8, 6
A_AT = 2
C_AT = A_AT + NH_A * A_TILES
B_AT = C_AT + NP_C * C_TILES
PROJ_AT = B_AT + NH_B * B_TILES
OUT_AT = PROJ_AT + KT
N_TILES = OUT_AT + KT
A_GATES, C_GATES, B_GATES = A_TILES - 5, C_TILES - 4, B_TILES - 4


def psum_col(c):
    return START[c] if c < 3 else 512 + START[c] - SPLIT


def part_col(c):
    return {1: 0, 2: 129, 0: 258, 3: 512, 4: 641}[c]


def level_mask(lv):
    s, t = np.arange(P)[:, None], np.arange(P)[None]
    return ((t >> (lv + 1)) == (s >> (lv + 1))) & ((t >> lv) & 1 == 1) & ((s >> lv) & 1 == 0)


def firsts(lv):
    return np.array([j for j in range(P) if not (j >> lv) & 1])


def seconds(lv):
    return np.array([j for j in range(P) if (j >> lv) & 1])


def constants():
    s, t = np.arange(P)[:, None], np.arange(P)[None]
    apart = (s < NS) == (t < NS)
    full = {"ident": np.eye(P), "blocks": s // 64 == t // 64}
    masks = {
        "causal": np.concatenate([(s <= t) & apart, s <= t], 1),
        "before": np.concatenate([(s < t) & apart, s < t], 1),
        "after": np.concatenate([(s > t) & apart, s > t], 1),
        "levels": np.concatenate([level_mask(lv) for lv in range(LEVELS)] + [s == t], 1),
        "down": np.concatenate([level_mask(lv).T[:, firsts(lv)] for lv in range(LEVELS)], 1),
        "up": np.concatenate([level_mask(lv)[:, seconds(lv)] for lv in range(LEVELS)], 1),
        "carry": np.tile(~np.isin(np.arange(T), [0, NS] + START[1:]), (P, 1)),
    }
    at = {}
    for group in (full, masks):
        cols = 0
        for name, a in group.items():
            at[name] = (cols, cols + a.shape[1])
            cols += a.shape[1]
    return [np.concatenate(list(g.values()), 1).astype(np.float32) for g in (full, masks)], at


(FULL, MASKS), CONST_AT = constants()

VEC = {"norm_pre": 0, "mlstm_norm": 16, "lb": 24, "hgrn_norm": 28, "b_i": 32, "b_f": 33, "m0": 34,
       "n0": 35, "low_mu": 43, "low_cache": 44, "pair": 45}
PAIR_VECS = 16
MU, CACHE, W0, A0, K_K, K_A, R_K, GN_G, GN_B, KA1 = 0, 4, 8, 9, 10, 11, 12, 13, 14, 15
N_VEC = VEC["pair"] + 4 * PAIR_VECS


class Num:

    def __init__(self, base, per, i, j):
        assert per % 2 == 0
        self.base, self.per, self.i, self.j = base, per, i, j

    def __add__(self, k):
        return self.i * self.per + (self.base + self.j + k)

    def __sub__(self, k):
        return self + -k


def SLOT_OF(n):
    return n % 2 if isinstance(n, int) else (n.base + n.j) % 2


def HALF_OF(n):
    return n // 2 if isinstance(n, int) else HalfOf(n)


class HalfOf:
    def __init__(self, n):
        self.n = n

    def __mul__(self, k):
        return Scaled(self.n, k)


class Scaled:
    def __init__(self, n, k):
        self.n, self.k = n, k

    def __add__(self, c):
        n = self.n
        return n.i * (n.per // 2 * self.k) + ((n.base + n.j) // 2 * self.k + c)


class Steps:

    def __init__(self, sem, names):
        self.sem, self.names, self.next = sem, names.split(), 0
        assert len(set(self.names)) == len(self.names)

    def after(self, i, step):
        return self.sem, i * len(self.names) + (self.names.index(step) + 1)

    def done(self, instruction, step):
        assert self.names[self.next % len(self.names)] == step, step
        self.next += 1
        return instruction.then_inc(self.sem, 1)

STEPS = {
    "setup_vector": """
        ones rows_clear i f f_size log_f b g m_max m m_ends ends low_mixed_step low_mixed low_1 low_2
        low_tanh scalar_args head_vectors""",
    "setup_scalar": """
        f_exp f_log m_rows low_exp low_last rows ends scalars""",
    "setup_tensor": """
        rows_turned ends_everywhere""",
    "setup_pool": """
        zeros cleared mlstm_cleared""",
    "mlstm_vector": """
        scalars head_m n0 v_rows v_weighted decay_args probs state1 state2 state3 state4 states inside
        num den_size stats den den_inv aggr den_inv2 h_var gate1 gate2 gate3 gate h_scale h_unit n_out y""",
    "mlstm_scalar": """
        k_rows decays h_log h_rstd state_out""",
    "mlstm_tensor": """
        k_turned v_turned m_everywhere scores updates inside carried h_turned states_turned""",
    "mlstm_pool": """
        masked""",
    "rwkv_vector": """
        vectors negated streams_apart ranks1 a log_decay log_sums log_decay_sums k_step k kk_raw
        k_factor k_new r_step r bonus_terms end_decays rh kk_floor v_step v kk b kkh bh kh bE kE state0
        bonus z_step z z1 z2 gate ub0 ub1 bu0 bu1 uk0 uk1 yb0 yb1 yk0 yk1 low0 inv0 w1 low1 inv1 low2
        inv2 low3 inv3 low4 inv4 low5 inv5 low6 inv6 tv u0 state1 u1 state2 u2 state3 u3 state4 u4
        state5 y_centred y_unit y_affine y_bonus y""",
    "rwkv_scalar": """
        rank_exps decay_exps kk_squares kk_log kk_rsqrt kk_rows v_rows bE_rows kE_rows z_exp tk out0
        out1 out2 out3 out4 y_squares y_log y_rstd state_out""",
    "rwkv_tensor": """
        ranks kk_lengths bonus_sums kk_turned v_turned bE_turned kE_turned ub0_ ub1_ bu0_ bu1_ uk0_ uk1_
        yb0_ yb1_ yk0_ yk1_ uk_v au1 du1 au2 du2 au3 du3 au4 du4 au5 du5 au6 du6 solved u_carried0
        y_part0 state_part0 u_carried1 state_part1 y_part1 u_carried2 state_part2 y_part2 u_carried3
        state_part3 y_part3 u_carried4 state_part4 y_part4 y_sums states_turned y_square_sums""",
    "rwkv_pool": """
        unit_blocks""",
    "hgrn_vector": """
        logit logit0 soft_inv softmax bound rest f1 f2 k f3 f log_copy log_sums end_args args0 ends khat
        meta_from_zero scaled0 args1 scaled1 masked0 args2 scaled2 masked1 args3 scaled3 masked2 args4
        scaled4 masked3 args5 scaled5 masked4 args6 scaled6 masked5 no_pairs6 masked6 masked7 state1
        state2 state3 state4 states z1 z2 gate o_unit y""",
    "hgrn_scalar": """
        soft log_f decay_exp end_exp exp0 k_rows v_rows exp1 exp2 exp3 exp4 exp5 exp6 o_sum0 o_sum1
        o_sum2 o_sum3 o_sum4 o_log o_rstd""",
    "hgrn_tensor": """
        k_turned v_turned pairs0 pairs1 pairs2 pairs3 pairs4 pairs5 pairs6 pairs7 updates outputs
        o_turned""",
    "hgrn_pool": """
        add1 add2 add3 add4 add5 add6 summed""",
    "norm_rows_tensor": """
        n_turned""",
    "norm_rows_scalar": """
        n_rows""",
    "shift_vector": """
        columns""",
    "shift_tensor": """
        shift_turned""",
    "shift_scalar": """
        shift_out""",
    "merge_vector": """
        part0_0 part1_0 sum1_0 part2_0 merged0 part0_1 part1_1 sum1_1 part2_1 merged1""",
    "merge_scalar": """
        gates0 gates1""",
    "merge_tensor": """
        proj0_0 proj1_0 proj0_1 proj1_1""",
    "out_vector": """
        rows0 rows1""",
    "out_scalar": """
        """,
    "out_tensor": """
        turned0 turned1""",
}

OUT_DMAS = [2, 3, 4, 5, 6]


def build(nc, x_all, w_stream, full_in, masks_in, vecs_in, low_in, c0_in, hgrn_s0, rwkv_s0, norm_post,
          y_prompt, y_sample, c_p, n_p, m_p, hs_p, rs_p, sh_p, c_s, n_s, m_s, hs_s, rs_s, sh_s):
    ctx = ExitStack()
    with ctx:
        def sb(name, cols, dt=F32, rows=P):
            return ctx.enter_context(nc.sbuf_tensor(name, [rows, cols], dt))

        def sem(name):
            return ctx.enter_context(nc.semaphore(name))

        def steps(name):
            return Steps(sem(name), STEPS[name])

        xh = sb("act_hi", KT * T, F32R)[:, :].rearrange("p (k t) -> p k t", k=KT)
        xl = sb("act_lo", KT * T, F32R)[:, :].rearrange("p (k t) -> p k t", k=KT)
        wraw = sb("w_raw", 2 * D)[:, :].rearrange("p (s n) -> p s n", s=2)
        whi = sb("w_hi", 2 * D, F32R)[:, :].rearrange("p (s n) -> p s n", s=2)
        wlo = sb("w_lo", 2 * D, F32R)[:, :].rearrange("p (s n) -> p s n", s=2)
        full = sb("full", FULL.shape[1])
        masks = sb("masks", MASKS.shape[1], mybir.dt.bfloat16)
        vecs = sb("vecs", N_VEC)
        low = sb("low_acts", T)
        gbuf = [sb(f"gate_out{b}", T) for b in range(2)]
        ybuf = sb("branch_out", T)
        shifts = sb("shift_rows", 34)
        ones8 = sb("ones8", P, rows=8)
        pk_all = sb("mlstm_scalars", 8 * 32)[:, :].rearrange("p (h n) -> p h n", h=8)
        pk = sb("head_scalars", 32)
        small = sb("small", 64)
        low_w = sb("rank_weights", P)
        shpad = sb("shift_columns", 64)
        shrow = low_w
        eends, bend = sb("rwkv_end_decays", 8), sb("hgrn_end_decays", 8)
        bss = sb("o_sums", 10)[:, :].rearrange("p (a b) -> p a b", a=2)
        eps, gn_eps, tenln2 = sb("eps", 1), sb("gn_eps", 1), sb("ten_ln2", 1)
        n_scr = (nc.sbuf_bytes_remaining // 4 - 8) // 8 * 8
        scr = sb("scratch", n_scr)

        acc = [ctx.enter_context(nc.psum_tensor(f"acc{k}", [P, 1024], F32)) for k in range(2)]
        br = [ctx.enter_context(nc.psum_tensor(f"branch{k}", [P, 1024], F32)) for k in range(2)]
        bra, brb = br

        ident = full[:, CONST_AT["ident"][0]:CONST_AT["ident"][1]]
        blocks = full[:, CONST_AT["blocks"][0]:CONST_AT["blocks"][1]]

        def mask(name):
            return masks[:, CONST_AT[name][0]:CONST_AT[name][1]]

        def vec(name, k=0, rows=P):
            return vecs[0:rows, VEC[name] + k:VEC[name] + k + 1]

        graw = nc.dram_tensor("gate_logits", [3 * KT, P, T], F32, kind="Internal").ap()
        yspill = nc.dram_tensor("branch_rows", [KT, P, T], F32, kind="Internal").ap()

        class Carver:
            def __init__(self, at=0):
                self.at = at

            def __call__(self, cols, *shape):
                a, self.at = self.at, self.at + cols
                assert self.at <= n_scr, (self.at, n_scr)
                v = scr[:, a:a + cols]
                if len(shape) == 2:
                    return v.rearrange("p (a b) -> p a b", a=shape[0])
                if len(shape) == 3:
                    return v.rearrange("p (a b c) -> p a b c", a=shape[0], b=shape[1])
                return v

        def halves(bank, n=HALF):
            return bank[:, :].rearrange("p (b n) -> p b n", b=2)[:, :, 0:n]

        def split2(v):
            return v.rearrange("p (b n) -> p b n", b=2)

        def shift_in(act, f, n, dst, tile_done, evac_done):
            act.wait_ge(tile_done, n + 1)
            src = acc[SLOT_OF(n)]
            f(dst[:, 1:NS + 1], src[:, 0:NS], ACT.Copy)
            f(dst[:, NS + 2:HALF + 2], src[:, NS:HALF], ACT.Copy)
            return f(dst[:, HALF + 2:T + 2], src[:, 512:512 + HALF], ACT.Copy).then_inc(evac_done, 1)

        w_here = [sem(f"weights_loaded{k}") for k in range(2)]
        hi_done, lo_done = sem("weights_hi_done"), sem("weights_lo_done")
        tile_done, evac_done = sem("tile_product_done"), sem("tile_evacuated")
        consts_here, vecs_here = sem("constants_loaded"), sem("vectors_loaded")
        gates_out = [sem(f"gate_rows_stored{b}") for b in range(2)]
        y_out = sem("branch_rows_stored")

        x_here = [sem(f"x_rows_loaded{t}") for t in range(5)]
        x_sums, x_unit = sem("x_sums_done"), sem("x_normalised")
        x_turned, x_hi, x_lo = sem("x_turned"), sem("x_hi_done"), sem("x_lo_done")
        cv = Carver()
        xt = cv(5 * D, 5, D)
        x_junk = cv(D)
        ROWS = [P] * 4 + [T - 4 * P]
        ring4 = [acc[0], acc[1], bra, brb]

        cv = Carver()
        GI, XF, AB, LF, BC, MR, MT = (cv(T) for _ in range(7))
        RR = cv(T)
        ONES = cv(T)
        LOWP = cv(T + 2)
        LOWD = cv(T + 1)
        TK = cv(5 * 96, 5, 96)
        ME = cv(56, 8, 7)
        EB = cv(56, 8, 7)
        MC = cv(7)
        mlstm_rows = MR
        a_used = cv.at
        cv = Carver(GI_END := 6 * T)
        aq, ak, av, aeo, az, aez, agz = (cv(T) for _ in range(7))
        DM = cv(T)
        ktok = cv(5 * 128, 5, 128)
        vtok = cv(5 * 129, 5, 129)
        wsv = cv(5 * 129, 5, 129)
        WW = cv(5 * 128, 5, 128)
        PP = cv(5 * 128, 5, 128)
        AST = cv(7 * 129, 7, 129)
        num = cv(5 * 129, 5, 129)
        hn = cv(5 * 128, 5, 128)
        c_in = cv(128)
        c_out = cv(256, 2, 128)
        stats = cv(30, 5, 6)
        aggr = cv(10, 5, 2)
        smA = cv(40, 8, 5)
        nout = cv(16, 2, 8)
        nrow = cv(128)
        pk3 = pk[:, :]

        cv = Carver()
        cz, cvv, bon, rh = (cv(T) for _ in range(4))
        x1 = cv.at
        PB = [cv(T + 2), cv(T + 2)]
        DD = cv(T + 1)
        cr, ck, ca, LL, kk, cb, ctmp = (cv(T) for _ in range(7))
        x2 = cv.at
        kkh, bh, kh, bE, kE = (cv(T) for _ in range(5))
        x3 = cv.at
        BM = cv(10 * 128, 10, 128)
        KM = cv(10 * 128, 10, 128)
        kkT, bET, kET, vT = (cv(5 * 128, 5, 128) for _ in range(4))
        RST = cv(7 * 64, 7, 64)
        r_in = pk_all[:, 0:4, :].rearrange("p a b -> p (a b)")
        c_end = cv.at
        cv = Carver(x1)
        AA = cv(1280, 10, 128)
        AT = cv(1280, 10, 128)
        KTm = cv(1280, 10, 128)
        UU = cv(640, 10, 64)
        VV = cv(640, 10, 64)
        W1 = cv(640, 10, 64)
        assert cv.at <= x2
        TKT = AA[:, 0:5, :]
        TV = AT[:, 0:5, :].rearrange("p a b -> p (a b)").rearrange("p (q v) -> p q v", q=10)
        ysb = UU[:, :, :].rearrange("p a b -> p (a b)")[:, 0:T]
        utok = VV[:, 0:2, :]
        r_out = VV[:, 2:4, :].rearrange("p a b -> p (a b)")
        cv = Carver(x2)
        DD1 = cv(1280, 10, 128)
        DDT = cv(1280, 10, 128)
        assert cv.at <= x3
        cv = Carver(x2)
        yc, ysq, yv = cv(T), cv(T), cv(T)
        pv = pk[:, 0:PAIR_VECS + 4]

        cv = Carver()
        bq, bk, bv, bz, bez, bef, bep, AL, qhat, khat, EE = (cv(T) for _ in range(11))
        QK = [cv(T), cv(T)]
        PS = cv(5 * 128, 5, 128)
        PT = [cv(5 * 128, 5, 128) for _ in range(2)]
        khtok = cv(5 * 128, 5, 128)
        vbtok = cv(5 * 128, 5, 128)
        BST = cv(7 * 128, 7, 128)
        on = cv(5 * 128, 5, 128)
        lbv = cv(8)
        bjunk = cv(128)

        cv = Carver()
        YIN = cv(KT * T, KT, T)
        ZF = YIN
        gin = cv(6 * T, 2, 3, T)
        gs = cv(3 * T, 3, T)
        mz = [cv(T) for _ in range(3)]
        cv = Carver()
        YT = cv(5 * D, 5, D)
        zt = [cv(T), cv(T)]
        xres = cv(2 * D, 2, D)

        state_in, rwkv_in, hgrn_in, states_out = sem("mlstm_state_loaded"), sem("rwkv_state_loaded"), sem("hgrn_state_loaded"), sem("states_stored")
        y_here = [sem(f"branch_rows_loaded{k}") for k in range(4)]
        g_here = [sem(f"gate_rows_loaded{k}") for k in range(2)]
        y_hi, y_split, z_hi, z_split = sem("branch_hi_done"), sem("branch_split"), sem("merged_hi_done"), sem("merged_split")
        post_here, res_out, res_done, r_sums = sem("norm_post_loaded"), sem("y_stored"), sem("y_rows_done"), sem("y_sums_done")
        post_done = sem("y_rows_scaled")
        res_here = [sem(f"residual_loaded{k}") for k in range(2)]
        S0 = {k: steps(k) for k in ("setup_vector", "setup_scalar", "setup_tensor", "setup_pool")}
        A_ = {k: steps(k) for k in ("mlstm_vector", "mlstm_scalar", "mlstm_tensor", "mlstm_pool")}
        C_ = {k: steps(k) for k in ("rwkv_vector", "rwkv_scalar", "rwkv_tensor", "rwkv_pool")}
        B_ = {k: steps(k) for k in ("hgrn_vector", "hgrn_scalar", "hgrn_tensor", "hgrn_pool")}
        A2 = {k: steps(k) for k in ("norm_rows_tensor", "norm_rows_scalar")}
        E_ = {k: steps(k) for k in ("shift_vector", "shift_tensor", "shift_scalar")}
        P_ = {k: steps(k) for k in ("merge_vector", "merge_scalar", "merge_tensor")}
        O_ = {k: steps(k) for k in ("out_vector", "out_scalar", "out_tensor")}

        block = ctx.enter_context(nc.Block())

        @block.sync
        def _(sp):
            def load(n, s, half):
                src = w_stream[bass.ds(n, 1)].rearrange("a p n -> (a p) n")
                return sp.dma_start(wraw[:, s, :], src).then_inc(w_here[s], 16)

            sp.dma_start(vecs[:, :], vecs_in).then_inc(vecs_here, 16)
            for t in range(5):
                sp.dma_start(xt[0:ROWS[t], t, :], x_all[P * t:P * t + ROWS[t], :]).then_inc(x_here[t], 16)
                if t == 0:
                    sp.dma_start(full[:, :], full_in).then_inc(consts_here, 16)
            for n in range(2):
                sp.dma_start(wraw[:, n, :], w_stream[n]).then_inc(w_here[n], 16)
            sp.dma_start(masks[:, :], masks_in).then_inc(consts_here, 16)

            def next_load(n):
                nxt = sp.snap(n + 2) if not isinstance(n, int) else n + 2
                sp.wait_ge(lo_done, n + 1)
                s = SLOT_OF(n)
                if isinstance(nxt, int):
                    src = w_stream[nxt]
                else:
                    src = w_stream[bass.ds(nxt, 1)].rearrange("a p n -> (a p) n")
                sp.dma_start(wraw[:, s, :], src).then_inc(w_here[s], 16)

            for n in range(A_AT):
                next_load(n)
            sp.wait_ge(*S0["setup_scalar"].after(0, "m_rows"))
            sp.dma_start(m_s, MT[0:8, NS - 1:NS]).then_inc(x_here[0], 16)
            sp.dma_start(m_p, MT[0:8, T - 1:T]).then_inc(x_here[0], 16)
            sp.wait_ge(x_here[0], 48)
            sp.wait_ge(*S0["setup_scalar"].after(0, "scalars"))
            sp.wait_ge(*S0["setup_vector"].after(0, "head_vectors"))
            with sp.Fori(0, NH_A) as i:
                for j in range(A_TILES):
                    n = Num(A_AT, A_TILES, i, j)
                    if j == 0:
                        sp.dma_start(c_in[:, :], c0_in[bass.ds(i, 1)].rearrange("a v k -> (a v) k")).then_inc(state_in, 16)
                    next_load(n)
                    if j >= 5:
                        g = j - 5
                        row = sp.snap(i * A_GATES + g)
                        sp.wait_ge(evac_done, n + 1)
                        sp.dma_start(graw[bass.ds(row, 1)].rearrange("a p t -> (a p) t"), gbuf[g % 2][:, :]).then_inc(gates_out[g % 2], 16)
                sp.wait_ge(*A_["mlstm_scalar"].after(i, "state_out"))
                sp.dma_start(c_p[bass.ds(i, 1)].rearrange("a v k -> (a v) k"), c_out[:, 0, :]).then_inc(states_out, 16)
                sp.dma_start(c_s[bass.ds(i, 1)].rearrange("a v k -> (a v) k"), c_out[:, 1, :]).then_inc(states_out, 16)
                sp.wait_ge(*A_["mlstm_vector"].after(i, "y"))
                sp.dma_start(yspill[bass.ds(i, 1)].rearrange("a p t -> (a p) t"), ybuf[:, :]).then_inc(y_out, 16)
            sp.wait_ge(*A2["norm_rows_scalar"].after(0, "n_rows"))
            sp.dma_start(n_p, nrow[0:8, :]).then_inc(states_out, 16)
            sp.dma_start(n_s, nrow[8:16, :]).then_inc(states_out, 16)
            with sp.Fori(0, NP_C) as i:
                for j in range(C_TILES):
                    n = Num(C_AT, C_TILES, i, j)
                    if j == 0:
                        sp.dma_start(low_w[:, :], low_in[bass.ds(i, 1)].rearrange("a p n -> (a p) n")).then_inc(rwkv_in, 16)
                        for h in range(2):
                            hh = sp.snap(i * 2 + h)
                            sp.dma_start(r_in[0:64, 64 * h:64 * h + 64], rwkv_s0[bass.ds(hh, 1)].rearrange("a v k -> (a v) k")).then_inc(rwkv_in, 16)
                    next_load(n)
                    if j >= 4:
                        g = j - 4
                        row = sp.snap(i * C_GATES + (NH_A * A_GATES + g))
                        sp.wait_ge(evac_done, n + 1)
                        sp.dma_start(graw[bass.ds(row, 1)].rearrange("a p t -> (a p) t"), gbuf[g % 2][:, :]).then_inc(gates_out[g % 2], 16)
                sp.wait_ge(*C_["rwkv_scalar"].after(i, "state_out"))
                for h in range(2):
                    hh = sp.snap(i * 2 + h)
                    sp.dma_start(rs_p[bass.ds(hh, 1)].rearrange("a v k -> (a v) k"), r_out[0:64, 64 * h:64 * h + 64]).then_inc(states_out, 16)
                    sp.dma_start(rs_s[bass.ds(hh, 1)].rearrange("a v k -> (a v) k"), r_out[64:128, 64 * h:64 * h + 64]).then_inc(states_out, 16)
                row = sp.snap(i + 12)
                sp.wait_ge(*C_["rwkv_vector"].after(i, "y"))
                sp.dma_start(yspill[bass.ds(row, 1)].rearrange("a p t -> (a p) t"), ybuf[:, :]).then_inc(y_out, 16)
            with sp.Fori(0, NH_B) as i:
                for j in range(B_TILES):
                    n = Num(B_AT, B_TILES, i, j)
                    if j == 0:
                        sp.dma_start(BST[:, 0, :], hgrn_s0[bass.ds(i, 1)].rearrange("a v k -> (a v) k")).then_inc(hgrn_in, 16)
                    next_load(n)
                    if j >= 4:
                        g = j - 4
                        row = sp.snap(i * B_GATES + (NH_A * A_GATES + NP_C * C_GATES + g))
                        sp.wait_ge(evac_done, n + 1)
                        sp.dma_start(graw[bass.ds(row, 1)].rearrange("a p t -> (a p) t"), gbuf[g % 2][:, :]).then_inc(gates_out[g % 2], 16)
                sp.wait_ge(*B_["hgrn_vector"].after(i, "states"))
                sp.dma_start(hs_p[bass.ds(i, 1)].rearrange("a v k -> (a v) k"), BST[:, 5, :]).then_inc(states_out, 16)
                sp.dma_start(hs_s[bass.ds(i, 1)].rearrange("a v k -> (a v) k"), BST[:, 6, :]).then_inc(states_out, 16)
                row = sp.snap(i + 8)
                sp.wait_ge(*B_["hgrn_vector"].after(i, "y"))
                sp.dma_start(yspill[bass.ds(row, 1)].rearrange("a p t -> (a p) t"), ybuf[:, :]).then_inc(y_out, 16)
            sp.wait_ge(*E_["shift_scalar"].after(0, "shift_out"))
            sp.dma_start(sh_s, shrow[0:17, :]).then_inc(states_out, 16)
            sp.dma_start(sh_p, shrow[32:49, :]).then_inc(states_out, 16)
            sp.wait_ge(y_out, 16 * KT)
            sp.wait_ge(states_out, 16 * (2 * NH_A + 2 + 4 * NP_C + 2 * NH_B + 2))
            for k in range(4):
                sp.dma_start(YIN[:, 4 * k:4 * k + 4, :], yspill[4 * k:4 * k + 4].rearrange("k p t -> p k t")).then_inc(y_here[k], 16)
            sp.wait_ge(gates_out[0], 16 * (2 * NH_A + 2 * NP_C + NH_B))
            sp.wait_ge(gates_out[1], 16 * (NH_A + 2 * NP_C + NH_B))

            def load_gates(j, s):
                for b in range(3):
                    row = sp.snap(j + KT * b) if not isinstance(j, int) else j + KT * b
                    sp.dma_start(gin[:, s, b, :], graw[bass.ds(row, 1)].rearrange("a p t -> (a p) t")).then_inc(g_here[s], 16)
            load_gates(0, 0)
            load_gates(1, 1)
            with sp.Fori(0, KT // 2 - 1) as i:
                for j in range(2):
                    next_load(Num(PROJ_AT, 2, i, j))
                    jj = sp.snap(i * 2 + (j + 2))
                    sp.wait_ge(*P_["merge_scalar"].after(i, f"gates{j}"))
                    load_gates(jj, j)
            for n in range(PROJ_AT + KT - 2, PROJ_AT + KT):
                next_load(n)
            with sp.Fori(0, KT // 2 - 1) as i:
                for j in range(2):
                    next_load(Num(OUT_AT, 2, i, j))
            sp.wait_ge(lo_done, N_TILES - 1)
            sp.dma_start(wraw[:, 0, :], norm_post.partition_broadcast(P)).then_inc(post_here, 16)
            for t in range(5):
                if t >= 2:
                    sp.wait_ge(res_out, 16 * OUT_DMAS[t - 2])
                sp.dma_start(xres[0:ROWS[t], t % 2, :], x_all[P * t:P * t + ROWS[t], :]).then_inc(res_here[t % 2], 16)
                sp.wait_ge(res_done, t + 1)
                a, b = P * t, P * t + ROWS[t]
                if a < NS:
                    sp.dma_start(y_sample, xres[0:NS, 0, :]).then_inc(res_out, 16)
                lo = max(a, C0)
                sp.dma_start(y_prompt[lo - C0:b - C0, :], xres[lo - a:b - a, t % 2, :]).then_inc(res_out, 16)
            sp.wait_ge(res_out, 16 * OUT_DMAS[4])

        @block.tensor
        def _(pe):
            mm = nc.tensor.matmul
            turn = nc.tensor.transpose

            def product(n, stages=None, first=False, unevacuated=0):
                s = SLOT_OF(n)
                stages = stages or {}
                pe.wait_ge(lo_done, n + 1)
                if not first:
                    pe.wait_ge(evac_done, n - (1 + unevacuated))
                for k in range(KT):
                    for stage in stages.get(k, ()):
                        stage()
                    w = slice(P * k, P * k + P)
                    for a, b in ((whi, xh), (whi, xl), (wlo, xh)):
                        for h in range(2):
                            last = mm(acc[s][:, 512 * h:512 * h + HALF], a[:, s, w], b[:, k, HALF * h:HALF * h + HALF],
                                      start=(k == 0 and a is whi and b is xh), stop=(k == KT - 1 and a is wlo))
                last.then_inc(tile_done, 1)

            def products(tiles, stages):
                for m, n in enumerate(tiles):
                    at = {}
                    for block, stage in stages:
                        if block // KT == m:
                            at.setdefault(block % KT, []).append(stage)
                    product(n, at)
                for block, stage in stages:
                    if block >= KT * len(tiles):
                        stage()

            pe.wait_ge(consts_here, 16)
            pe.wait_ge(x_unit, 5)
            for k in range(KT):
                if k >= 4:
                    pe.wait_ge(x_lo, k - 3)
                for t in range(5):
                    last = turn(ring4[k % 4][:, P * t:P * t + ROWS[t]], xt[0:ROWS[t], t, P * k:P * k + P], ident[0:ROWS[t], 0:ROWS[t]])
                last.then_inc(x_turned, 1)
            pe.wait_ge(x_lo, KT)
            product(0, first=True)
            product(1, first=True)
            pt, vt, at = S0["setup_tensor"], S0["setup_vector"], S0["setup_scalar"]
            pe.wait_ge(*at.after(0, "m_rows"))
            for c in range(NCH):
                last = turn(bra[0:LEN[c], 96 * c:96 * c + 96], RR[0:96, START[c]:START[c] + LEN[c]], ident[0:96, 0:96])
            pt.done(last, "rows_turned")
            pe.wait_ge(*vt.after(0, "ends"))
            pt.done(mm(brb[:, 0:56], ones8[:, :], ME[0:8, :, :].rearrange("p a b -> p (a b)"), start=True, stop=True), "ends_everywhere")

            pt, vt, at, gt = (A_[k] for k in ("mlstm_tensor", "mlstm_vector", "mlstm_scalar", "mlstm_pool"))
            with pe.Fori(0, NH_A) as i:
                def N(j):
                    return Num(A_AT, A_TILES, i, j)

                def turn_kv():
                    pe.wait_ge(evac_done, N(1) + 1)
                    for c in range(NCH):
                        last = turn(bra[0:LEN[c], P * c:P * c + P], ak[:, START[c]:START[c] + LEN[c]], ident)
                    pe.wait_ge(state_in, 16 * i + 16)
                    last = turn(bra[:, 640:768], c_in[:, :], ident)
                    pt.done(last, "k_turned")
                    for c in range(NCH):
                        last = turn(brb[0:LEN[c], P * c:P * c + P], av[:, START[c]:START[c] + LEN[c]], ident)
                    pt.done(last, "v_turned")

                def scores():
                    pe.wait_ge(*at.after(i, "k_rows"))
                    pe.wait_ge(*vt.after(i, "head_m"))
                    mm(bra[:, 0:SPLIT], ones8[:, :], DM[0:8, 0:SPLIT], start=True, stop=True)
                    pt.done(mm(bra[:, 512:512 + T - SPLIT], ones8[:, :], DM[0:8, SPLIT:T], start=True, stop=True), "m_everywhere")
                    pe.wait_ge(*vt.after(i, "v_rows"))
                    pe.wait_ge(evac_done, N(2) + 1)
                    for c in range(NCH):
                        tok = slice(START[c], START[c] + LEN[c])
                        last = mm(brb[0:LEN[c], P * c:P * c + LEN[c]], ak[:, tok], aq[:, tok], start=True, stop=True)
                    pt.done(last, "scores")

                def values():
                    pe.wait_ge(*vt.after(i, "decay_args"))
                    pe.wait_ge(*vt.after(i, "v_weighted"))
                    pe.wait_ge(*at.after(i, "k_rows"))
                    mm(bra[:, 0:129], ktok[0:NS, 0, :], wsv[0:NS, 0, :], start=True, stop=True)
                    for c in range(1, NCH):
                        o = {1: 258, 2: 512, 3: 641, 4: 770}[c]
                        last = mm(bra[:, o:o + 129], ktok[:, c, :], wsv[:, c, :], start=True, stop=True)
                    last = mm(bra[:, 129:258], ktok[NS:C0, 0, :], wsv[NS:C0, 0, :], start=True, stop=True)
                    pt.done(last, "updates")
                    pe.wait_ge(*vt.after(i, "probs"))
                    for c in range(NCH):
                        o = part_col(c)
                        last = mm(brb[0:LEN[c], o:o + 129], PP[0:LEN[c], c, 0:LEN[c]], vtok[0:LEN[c], c, :], start=True, stop=True)
                    pt.done(last, "inside")

                def carried():
                    pe.wait_ge(*vt.after(i, "states"))
                    for c in range(NCH):
                        o, n = part_col(c), (NS if c == 0 else P)
                        last = mm(bra[0:n, o:o + 129], aq[:, START[c]:START[c] + n], AST[:, c, :], start=True, stop=True)
                    pt.done(last, "carried")

                def turn_h():
                    pe.wait_ge(*vt.after(i, "h_unit"))
                    for c in range(NCH):
                        o = psum_col(c)
                        last = turn(brb[:, o:o + LEN[c]], hn[0:LEN[c], c, :], ident[0:LEN[c], 0:LEN[c]])
                    pt.done(last, "h_turned")
                    for m in range(2):
                        last = turn(bra[:, P * m:P * m + P], AST[:, 5 + m, 0:P], ident)
                    pt.done(last, "states_turned")

                product(N(0))
                product(N(1))
                product(N(2))
                turn_kv()
                product(N(3))
                scores()
                product(N(4))
                values()
                product(N(5))
                carried()
                product(N(6))
                product(N(7), {5: [turn_h]})
                pe.wait_ge(*vt.after(i, "y"))
                pe.wait_ge(*at.after(i, "state_out"))
            A2["norm_rows_tensor"].done(turn(bra[0:16, 0:P], nout[:, :, :].rearrange("p a b -> p (a b)"), ident), "n_turned")
            pe.wait_ge(*A2["norm_rows_scalar"].after(0, "n_rows"))

            pt, vt, at, gt = (C_[k] for k in ("rwkv_tensor", "rwkv_vector", "rwkv_scalar", "rwkv_pool"))
            with pe.Fori(0, NP_C) as i:
                def N(j):
                    return Num(C_AT, C_TILES, i, j)

                def ranks():
                    pe.wait_ge(rwkv_in, 48 * i + 48)
                    pe.wait_ge(states_out, 64 * i + 16 * (2 * NH_A + 2))
                    pe.wait_ge(y_out, 16 * i + 16 * NH_A)
                    for h in range(2):
                        mm(bra[:, 512 * h:512 * h + HALF], low_w[0:64, :], low[0:64, HALF * h:HALF * h + HALF], start=True, stop=True)
                    for h in range(2):
                        last = mm(brb[:, 512 * h:512 * h + HALF], low_w[64:128, :], low[64:128, HALF * h:HALF * h + HALF], start=True, stop=True)
                    pt.done(last, "ranks")

                def lengths():
                    pe.wait_ge(*at.after(i, "kk_squares"))
                    for h in range(2):
                        last = mm(bra[:, 512 * h:512 * h + HALF], blocks, ctmp[:, HALF * h:HALF * h + HALF], start=True, stop=True)
                    pt.done(last, "kk_lengths")

                def bonus():
                    pe.wait_ge(*vt.after(i, "bonus_terms"))
                    for h in range(2):
                        mm(brb[:, 512 * h:512 * h + HALF], blocks, bon[:, HALF * h:HALF * h + HALF], start=True, stop=True)
                    last = turn(brb[:, 896:960], r_in[0:64, :], ident[0:64, 0:64])
                    pt.done(last, "bonus_sums")

                def turn_to_rows(src, bank, step, ready):
                    pe.wait_ge(*vt.after(i, ready))
                    for c in range(NCH):
                        last = turn(bank[0:LEN[c], P * c:P * c + P], src[:, START[c]:START[c] + LEN[c]], ident)
                    pt.done(last, step)

                def pairs(lhs, rhs, h, bank, step, ready):
                    pe.wait_ge(*vt.after(i, ready))
                    r = slice(64 * h, 64 * h + 64)
                    for c in range(NCH):
                        tok = slice(START[c], START[c] + LEN[c])
                        last = mm(bank[0:LEN[c], P * c:P * c + LEN[c]], lhs[r, tok], rhs[r, tok], start=True, stop=True)
                    pt.done(last, step)

                def level(lv, which):
                    n0 = (C0 if lv < 4 else NS) if lv < 6 else 0
                    if which == 0:
                        pe.wait_ge(*vt.after(i, f"inv{lv - 1}"))
                        if lv == 1:
                            pe.wait_ge(*vt.after(i, "w1"))
                    else:
                        pe.wait_ge(*vt.after(i, f"low{lv}"))
                    for q in (1, 2, 3, 4, 6, 7, 8, 9, 0, 5):
                        n = P if q % 5 else n0
                        if not n:
                            continue
                        m = n // 2
                        if which == 0:
                            rhs_u = DD1[0:n, q, 0:n].rearrange("p (b two w) -> p b two w", two=2, w=1 << lv)[:, :, 0, :]
                            rhs_v = DDT[0:n, q, 0:n].rearrange("p (b two w) -> p b two w", two=2, w=1 << lv)[:, :, 1, :]
                            mm(bra[0:n, 64 * q:64 * q + m], AT[0:n, q, 0:n], rhs_u, start=True, stop=True)
                            last = mm(brb[0:n, 64 * q:64 * q + m], AA[0:n, q, 0:n], rhs_v, start=True, stop=True)
                        else:
                            mm(bra[0:n, 64 * q:64 * q + m], DDT[0:n, q, 0:n], UU[0:n, q, 0:m], start=True, stop=True)
                            last = mm(brb[0:n, 64 * q:64 * q + m], DD1[0:n, q, 0:n], VV[0:n, q, 0:m], start=True, stop=True)
                    pt.done(last, f"{'au' if which == 0 else 'du'}{lv}")

                def w1():
                    pe.wait_ge(*vt.after(i, "yk0"))
                    pe.wait_ge(*at.after(i, "v_rows"))
                    for q in range(10):
                        c, h = q % 5, q // 5
                        last = mm(bra[0:LEN[c], 64 * q:64 * q + 64], KTm[0:LEN[c], q, 0:LEN[c]], vT[0:LEN[c], c, 64 * h:64 * h + 64], start=True, stop=True)
                    pt.done(last, "uk_v")

                def solved():
                    pe.wait_ge(*vt.after(i, "inv6"))
                    for q in range(10):
                        c, h = q % 5, q // 5
                        mm(bra[0:LEN[c], 64 * q:64 * q + 64], DDT[0:LEN[c], q, 0:LEN[c]], W1[0:LEN[c], q, :], start=True, stop=True)
                    for q in range(10):
                        c, h = q % 5, q // 5
                        last = mm(brb[64 * h:64 * h + 64, P * c:P * c + LEN[c]], kkT[0:LEN[c], c, 64 * h:64 * h + 64], DDT[0:LEN[c], q, 0:LEN[c]], start=True, stop=True)
                    pt.done(last, "solved")

                def from_state(c):
                    pe.wait_ge(*vt.after(i, "tv" if c == 0 else f"state{c}"))
                    pe.wait_ge(*at.after(i, "tk"))
                    n = LEN[c]
                    for h in range(2):
                        r = slice(64 * h, 64 * h + 64)
                        last = mm(bra[0:n, 512 * h:512 * h + 64], TKT[r, c, 0:n], RST[r, c, :], start=True, stop=True)
                    pt.done(last, f"u_carried{c}")

                def to_state(c):
                    ut = utok.rearrange("p a b -> p (a b)")
                    heads = [slice(0, 64), slice(64, 128)]

                    def end_state():
                        for r in heads:
                            if c == 0:
                                mm(brb[r, 512:576], bET[0:NS, c, r], ut[0:NS, r], start=True, stop=False)
                                mm(brb[r, 512:576], kET[0:NS, c, r], vT[0:NS, c, r], start=False, stop=True)
                                mm(bra[r, 256:320], bET[NS:C0, c, r], ut[NS:C0, r], start=True, stop=False)
                                last = mm(bra[r, 256:320], kET[NS:C0, c, r], vT[NS:C0, c, r], start=False, stop=True)
                            else:
                                mm(brb[r, 512:576], bET[:, c, r], ut[:, r], start=True, stop=False)
                                last = mm(brb[r, 512:576], kET[:, c, r], vT[:, c, r], start=False, stop=True)
                        pt.done(last, f"state_part{c}")

                    def output():
                        L, n = LEN[c], (NS if c == 0 else P)
                        for h, r in enumerate(heads):
                            mm(brb[r, 0:L], vT[0:L, c, r], KM[0:L, 5 * h + c, 0:L], start=True, stop=False)
                            mm(brb[r, 0:L], ut[0:L, r], BM[0:L, 5 * h + c, 0:L], start=False, stop=False)
                            last = mm(brb[r, 0:n], RST[r, c, :], rh[r, START[c]:START[c] + n], start=False, stop=True)
                        pt.done(last, f"y_part{c}")

                    pe.wait_ge(*vt.after(i, f"u{c}"))
                    if c == 0:
                        output()
                        end_state()
                    else:
                        end_state()
                        pe.wait_ge(*at.after(i, f"out{c - 1}"))
                        output()

                def means():
                    pe.wait_ge(*at.after(i, "out4"))
                    for h in range(2):
                        last = mm(bra[:, 512 * h:512 * h + HALF], blocks, ysb[:, HALF * h:HALF * h + HALF], start=True, stop=True)
                    pt.done(last, "y_sums")

                def variances():
                    pe.wait_ge(*at.after(i, "y_squares"))
                    for h in range(2):
                        last = mm(brb[:, 512 * h:512 * h + HALF], blocks, ysq[:, HALF * h:HALF * h + HALF], start=True, stop=True)
                    pt.done(last, "y_square_sums")

                def turn_states():
                    pe.wait_ge(*vt.after(i, "y_centred"))
                    pt.done(turn(bra[:, 0:P], RST[:, 5:7, :].rearrange("p a b -> p (a b)"), ident), "states_turned")

                product(N(0))
                ranks()
                product(N(1))
                product(N(2), {8: [lengths]})
                product(N(3))
                bonus()
                turn_to_rows(kkh, bra, "kk_turned", "kkh")

                def turned_again(ready, src, bank, step, when):
                    pe.wait_ge(*at.after(i, ready))
                    turn_to_rows(src, bank, step, when)

                plan = [
                    (1, lambda: turn_to_rows(cvv, brb, "v_turned", "bonus")),
                    (2, lambda: turned_again("kk_rows", bE, bra, "bE_turned", "bE")),
                    (3, lambda: turned_again("v_rows", kE, brb, "kE_turned", "kE")),
                    (4, lambda: (pe.wait_ge(*at.after(i, "bE_rows")), pairs(kkh, bh, 0, bra, "ub0_", "kE"))),
                    (5, lambda: (pe.wait_ge(*at.after(i, "kE_rows")), pairs(kkh, bh, 1, brb, "ub1_", "kE"))),
                ]
                block = 5
                before = ("ub0", "ub1")
                for name, lhs, rhs in (("bu", bh, kkh), ("uk", kh, kkh), ("yb", bh, rh), ("yk", kh, rh)):
                    for h in range(2):
                        block += 1
                        plan.append((block, lambda name=name, lhs=lhs, rhs=rhs, h=h, ready=before[h]: pairs(lhs, rhs, h, br[h], f"{name}{h}_", ready)))
                    before = (name + "0", name + "1")
                block += 2
                plan.append((block, w1))
                for lv in range(1, LEVELS):
                    for which in range(2):
                        block += 2
                        plan.append((block, lambda lv=lv, which=which: level(lv, which)))
                block += 2
                plan.append((block, solved))
                for c in range(NCH):
                    plan += [(block + 2, lambda c=c: from_state(c)), (block + 3, lambda c=c: to_state(c))]
                    block += 3
                plan += [(block + 2, means), (block + 3, turn_states), (block + 6, variances)]
                assert block + 6 <= 4 * KT
                products([N(4), N(5), N(6), N(7)], plan)

            pt, vt, at, gt = (B_[k] for k in ("hgrn_tensor", "hgrn_vector", "hgrn_scalar", "hgrn_pool"))
            with pe.Fori(0, NH_B) as i:
                def N(j):
                    return Num(B_AT, B_TILES, i, j)

                def turn_rows(src, bank, step):
                    for c in range(NCH):
                        last = turn(bank[0:LEN[c], P * c:P * c + P], src[:, START[c]:START[c] + LEN[c]], ident)
                    pt.done(last, step)

                def level_pairs(lv):
                    bank = br[lv % 2]
                    pe.wait_ge(*vt.after(i, f"scaled{lv}" if lv < LEVELS else "k"))
                    if lv >= 2:
                        pe.wait_ge(*vt.after(i, f"masked{lv - 2}"))
                    elif lv == 0:
                        pe.wait_ge(*at.after(i, "k_rows"))
                    else:
                        pe.wait_ge(*at.after(i, "v_rows"))
                    for c in range(NCH):
                        tok = slice(START[c], START[c] + LEN[c])
                        if lv == 6 and c == 0:
                            continue
                        a, b = (QK[lv % 2], QK[lv % 2]) if lv < LEVELS else (bk, bq)
                        last = mm(bank[0:LEN[c], P * c:P * c + LEN[c]], a[:, tok], b[:, tok], start=True, stop=True)
                    pt.done(last, f"pairs{lv}")

                def updates():
                    pe.wait_ge(*vt.after(i, f"masked{LEVELS - 1}"))
                    pe.wait_ge(*at.after(i, "v_rows"))
                    mm(bra[:, 0:P], khtok[0:NS, 0, :], vbtok[0:NS, 0, :], start=True, stop=True)
                    for c in range(1, NCH):
                        last = mm(bra[:, P * c + P:P * c + 2 * P], khtok[:, c, :], vbtok[:, c, :], start=True, stop=True)
                    last = mm(bra[:, P:2 * P], khtok[NS:C0, 0, :], vbtok[NS:C0, 0, :], start=True, stop=True)
                    pt.done(last, "updates")

                def outputs():
                    pe.wait_ge(*gt.after(i, "summed"))
                    pe.wait_ge(*vt.after(i, "states"))
                    pe.wait_ge(hgrn_in, 16 * i + 16)
                    pe.wait_ge(*vt.after(i, f"masked{LEVELS}"))
                    for c in range(NCH):
                        n = LEN[c]
                        mm(brb[0:n, P * c:P * c + P], PS[0:n, c, 0:n], vbtok[0:n, c, :], start=True, stop=False)
                        last = mm(brb[0:n, P * c:P * c + P], qhat[:, START[c]:START[c] + n], BST[:, c, :], start=False, stop=True)
                    pt.done(last, "outputs")

                def turn_o():
                    pe.wait_ge(*vt.after(i, "o_unit"))
                    for c in range(NCH):
                        o = psum_col(c)
                        last = turn(bra[:, o:o + LEN[c]], on[0:LEN[c], c, :], ident[0:LEN[c], 0:LEN[c]])
                    pt.done(last, "o_turned")

                def turn_k():
                    pe.wait_ge(*vt.after(i, "khat"))
                    turn_rows(khat, bra, "k_turned")

                def turn_v():
                    pe.wait_ge(evac_done, N(2) + 1)
                    turn_rows(bv, brb, "v_turned")

                for j in range(3):
                    product(N(j))
                products([N(3), N(4), N(5)],
                         [(13, turn_k), (14, turn_v)] + [(16 + 3 * lv, lambda lv=lv: level_pairs(lv)) for lv in range(LEVELS + 1)]
                         + [(39, updates), (41, outputs), (46, turn_o)])
            pe.wait_ge(*E_["shift_vector"].after(0, "columns"))
            E_["shift_tensor"].done(turn(bra[0:64, 0:P], shpad[:, :], ident), "shift_turned")
            pe.wait_ge(*E_["shift_scalar"].after(0, "shift_out"))

            pt, vt, at = P_["merge_tensor"], P_["merge_vector"], P_["merge_scalar"]
            banks3 = [acc[0], acc[1], bra]
            RANGES = [range(0, 8), range(8, 12), range(12, 16)]

            with pe.Fori(0, KT // 2) as i:
                for j in range(2):
                    n = Num(PROJ_AT, 2, i, j)
                    s = SLOT_OF(n)
                    pe.wait_ge(lo_done, n + 1)
                    for b in range(3):
                        if j:
                            pe.wait_ge(*vt.after(i, f"part{b}_0"))
                        elif b == 2:
                            pe.wait_ge(*vt.after(i, "part0_0"))
                        ks = RANGES[b]
                        for k in ks:
                            if j == 0:
                                pe.wait_ge(y_split, k + 1)
                            w = slice(P * k, P * k + P)
                            for x, y in ((whi, xh), (whi, xl), (wlo, xh)):
                                for h in range(2):
                                    last = mm(banks3[b][:, 512 * h:512 * h + HALF], x[:, s, w], y[:, k, HALF * h:HALF * h + HALF],
                                              start=(k == ks[0] and x is whi and y is xh), stop=(k == ks[-1] and x is wlo))
                        if b == 2:
                            last.then_inc(tile_done, 1)
                        else:
                            pt.done(last, f"proj{b}_{j}")
                pe.wait_ge(*vt.after(i, "part1_1"))
            pe.wait_ge(*vt.after(KT // 2 - 1, "merged1"))

            pt, vt, at = O_["out_tensor"], O_["out_vector"], O_["out_scalar"]
            pe.wait_ge(z_split, KT)

            def turn_out(i, j):
                pe.wait_ge(evac_done, Num(OUT_AT, 2, i, j) + (1 - KT))
                for t in range(5):
                    last = turn(br[j][0:ROWS[t], P * t:P * t + P], zt[j][:, P * t:P * t + ROWS[t]], ident)
                pt.done(last, f"turned{j}")

            with pe.Fori(0, KT // 2) as i:
                product(Num(OUT_AT, 2, i, 0), unevacuated=KT)
                turn_out(i, 0)
                product(Num(OUT_AT, 2, i, 1), unevacuated=KT)
                turn_out(i, 1)
                pe.wait_ge(*vt.after(i, "rows1"))

        @block.scalar
        def _(act):
            f = nc.scalar.activation

            def split_hi(m, first=False):
                s = SLOT_OF(m)
                act.wait_ge(w_here[s], HALF_OF(m) * 16 + 16)
                if not first:
                    act.wait_ge(tile_done, m - 1)
                f(whi[:, s, :], wraw[:, s, :], ACT.Copy).then_inc(hi_done, 1)

            def source(n):
                act.wait_ge(tile_done, n + 1)
                return halves(acc[SLOT_OF(n)])

            def plain(n, dst, scale=1.0):
                f(split2(dst), source(n), ACT.Copy, scale=scale).then_inc(evac_done, 1)

            def gates(n, g, base, per, i, left):
                if left is not None:
                    act.wait_ge(gates_out[g % 2], left)
                plain(n, gbuf[g % 2][:, :])

            S = S0["setup_scalar"]
            act.wait_ge(vecs_here, 16)
            act.wait_ge(*S0["setup_pool"].after(0, "zeros"))
            for t in range(5):
                r = ROWS[t]
                act.wait_ge(x_here[t], 16)
                if t:
                    act.wait_ge(x_sums, 3 * t)
                f(x_junk[0:r, :], xt[0:r, t, :], ACT.Square, accum_out=small[0:r, t:t + 1]).then_inc(x_sums, 1)
                act.wait_ge(x_sums, 3 * t + 1)
                f(small[0:r, 8 + t:9 + t], small[0:r, t:t + 1], ACT.Ln, scale=1.0 / D, bias=eps[0:r, 0:1]).then_inc(x_sums, 1)
                act.wait_ge(x_sums, 3 * t + 2)
                f(small[0:r, 16 + t:17 + t], small[0:r, 8 + t:9 + t], ACT.Exp, scale=-0.5).then_inc(x_sums, 1)
            split_hi(0, first=True)
            split_hi(1, first=True)
            for k in range(KT):
                act.wait_ge(x_turned, k + 1)
                f(xh[:, k, :], ring4[k % 4][:, 0:T], ACT.Copy, scale=vec("norm_pre", k)).then_inc(x_hi, 1)
            split_hi(2)
            act.wait_ge(tile_done, 1)
            f(split2(GI[0:8, :]), halves(acc[0])[0:8], ACT.Copy)
            f(split2(XF[0:8, :]), halves(acc[0])[32:40], ACT.Copy).then_inc(evac_done, 1)
            V = S0["setup_vector"]
            act.wait_ge(*V.after(0, "f_size"))
            S.done(f(AB[0:8, :], AB[0:8, :], ACT.Exp, scale=-1.0), "f_exp")
            act.wait_ge(*S.after(0, "f_exp"))
            S.done(f(AB[0:8, :], AB[0:8, :], ACT.Ln, bias=1.0), "f_log")
            act.wait_ge(*V.after(0, "m"))
            f(RR[0:8, :], GI[0:8, :], ACT.Copy)
            f(RR[32:40, :], MR[0:8, :], ACT.Copy)
            S.done(f(RR[64:72, :], MT[0:8, :], ACT.Copy), "m_rows")
            shift_in(act, f, 1, LOWP, tile_done, evac_done)
            act.wait_ge(*V.after(0, "low_mixed"))
            S.done(f(low[0:64, :], low[0:64, :], ACT.Exp, scale=2.0), "low_exp")
            S.done(f(shifts[:, 32:34], LOWP[:, 64:T + 2:T + 1 - 64], ACT.Copy), "low_last")
            act.wait_ge(*S0["setup_pool"].after(0, "cleared"))
            act.wait_ge(*S0["setup_tensor"].after(0, "rows_turned"))
            f(TK[0:C0, 0, :], bra[0:C0, 0:96], ACT.Copy)
            S.done(f(TK[:, 1:5, :].rearrange("p a b -> p (a b)"), bra[:, 96:480], ACT.Copy), "rows")
            act.wait_ge(*S0["setup_tensor"].after(0, "ends_everywhere"))
            S.done(f(EB[:, :, :].rearrange("p a b -> p (a b)"), brb[:, 0:56], ACT.Copy), "ends")
            act.wait_ge(*V.after(0, "scalar_args"))
            S.done(f(pk_all[:, :, 5:25], pk_all[:, :, 5:25], ACT.Exp), "scalars")

            G, V, S, Q = (A_[k] for k in ("mlstm_tensor", "mlstm_vector", "mlstm_scalar", "mlstm_pool"))
            act.wait_ge(x_here[0], 48)
            with act.Fori(0, NH_A) as i:
                def N(j):
                    return Num(A_AT, A_TILES, i, j)

                split_hi(N(1))
                plain(N(0), ak, scale=float(P) ** -0.5)
                split_hi(N(2))
                plain(N(1), av)
                split_hi(N(3))
                plain(N(2), aq)
                split_hi(N(4))
                act.wait_ge(*G.after(i, "k_turned"))
                f(ktok[0:C0, 0, :], bra[0:C0, 0:P], ACT.Copy)
                f(ktok[:, 1:5, :].rearrange("p a b -> p (a b)"), bra[:, P:5 * P], ACT.Copy)
                S.done(f(AST[:, 0, 0:P], bra[:, 640:768], ACT.Copy), "k_rows")
                f(split2(aeo), source(N(3)), ACT.Exp, scale=-1.0).then_inc(evac_done, 1)
                split_hi(N(5))
                act.wait_ge(*V.after(i, "decay_args"))
                f(WW[0:C0, 0, 0:C0], WW[0:C0, 0, 0:C0], ACT.Exp, scale=-1.0)
                S.done(f(WW[:, 1:5, :], WW[:, 1:5, :], ACT.Exp, scale=-1.0), "decays")
                src = source(N(4))
                f(split2(az), src, ACT.Copy)
                f(split2(aez), src, ACT.Exp, scale=-1.0).then_inc(evac_done, 1)
                split_hi(N(6))
                plain(N(5), gbuf[0][:, :])
                split_hi(N(7))
                act.wait_ge(*V.after(i, "h_var"))
                S.done(f(smA[:, 4, :], smA[:, 3, :], ACT.Ln, bias=eps[:, 0:1]), "h_log")
                act.wait_ge(*S.after(i, "h_log"))
                S.done(f(smA[:, 5, :], smA[:, 4, :], ACT.Exp, scale=-0.5), "h_rstd")
                plain(N(6), gbuf[1][:, :])
                split_hi(N(8))
                act.wait_ge(*G.after(i, "states_turned"))
                S.done(f(c_out[:, :, :].rearrange("p a b -> p (a b)"), bra[:, 0:256], ACT.Copy), "state_out")
                act.wait_ge(gates_out[0], i * 32 + 16)
                plain(N(7), gbuf[0][:, :])
                act.wait_ge(gates_out[0], i * 32 + 32)
                act.wait_ge(gates_out[1], i * 16 + 16)
                act.wait_ge(states_out, i * 32 + 32)
                act.wait_ge(*V.after(i, "y"))
            act.wait_ge(*A2["norm_rows_tensor"].after(0, "n_turned"))
            A2["norm_rows_scalar"].done(f(nrow[0:16, :], bra[0:16, 0:P], ACT.Copy), "n_rows")

            G, V, S, Q = (C_[k] for k in ("rwkv_tensor", "rwkv_vector", "rwkv_scalar", "rwkv_pool"))
            act.wait_ge(states_out, 16 * (2 * NH_A + 2))
            split_hi(C_AT + 1)
            with act.Fori(0, NP_C) as i:
                def N(j):
                    return Num(C_AT, C_TILES, i, j)

                def last_rows(j, pb):
                    col = act.snap(i * 8 + 2 * j)
                    f(shifts[:, bass.ds(col, 2)], pb[:, 64:T + 2:T + 1 - 64], ACT.Copy)

                act.wait_ge(*V.after(i, "streams_apart"))
                shift_in(act, f, N(0), PB[0], tile_done, evac_done)
                split_hi(N(2))
                act.wait_ge(*G.after(i, "ranks"))
                f(split2(LL), halves(bra), ACT.Exp, scale=-1.0, bias=pv[:, 16:17])
                S.done(f(split2(ca), halves(brb), ACT.Exp, scale=-1.0, bias=pv[:, 17:18]), "rank_exps")
                act.wait_ge(*V.after(i, "log_decay_sums"))
                f(rh, LL, ACT.Exp)
                f(kkh, kkh, ACT.Exp)
                f(kh, LL, ACT.Exp, scale=-1.0)
                S.done(f(kE, kE, ACT.Exp), "decay_exps")
                shift_in(act, f, N(1), PB[1], tile_done, evac_done)
                split_hi(N(3))
                act.wait_ge(*V.after(i, "kk_raw"))
                last_rows(1, PB[0])
                S.done(f(ctmp, kk, ACT.Square), "kk_squares")
                act.wait_ge(*V.after(i, "r"))
                last_rows(0, PB[1])
                shift_in(act, f, N(2), PB[0], tile_done, evac_done)
                split_hi(N(4))
                act.wait_ge(*V.after(i, "kk_floor"))
                S.done(f(ctmp, ctmp, ACT.Ln, scale=float(2 ** 20)), "kk_log")
                act.wait_ge(*S.after(i, "kk_log"))
                S.done(f(ctmp, ctmp, ACT.Exp, scale=-0.5, bias=tenln2[:, 0:1]), "kk_rsqrt")
                act.wait_ge(*V.after(i, "v"))
                last_rows(2, PB[0])
                shift_in(act, f, N(3), PB[1], tile_done, evac_done)
                split_hi(N(5))

                def rows_of(dst, bank, after, step):
                    act.wait_ge(*G.after(i, after))
                    f(dst[0:C0, 0, :], bank[0:C0, 0:P], ACT.Copy)
                    S.done(f(dst[:, 1:5, :].rearrange("p a b -> p (a b)"), bank[:, P:5 * P], ACT.Copy), step)

                rows_of(kkT, bra, "kk_turned", "kk_rows")
                rows_of(vT, brb, "v_turned", "v_rows")
                rows_of(bET, bra, "bE_turned", "bE_rows")
                rows_of(kET, brb, "kE_turned", "kE_rows")
                act.wait_ge(*V.after(i, "z"))
                last_rows(3, PB[1])
                S.done(f(PB[0][:, 0:T], cz, ACT.Exp, scale=-1.0), "z_exp")
                act.wait_ge(gates_out[0], i * 32 + 16 * (NH_A * 2))
                plain(N(4), gbuf[0][:, :])
                split_hi(N(6))
                act.wait_ge(gates_out[1], i * 32 + 16 * NH_A)
                plain(N(5), gbuf[1][:, :])
                split_hi(N(7))
                act.wait_ge(*G.after(i, "solved"))
                f(TKT[64 * 0:128, 0, 0:C0], brb[:, 0:C0], ACT.Copy)
                S.done(f(TKT[:, 1:5, :].rearrange("p a b -> p (a b)"), brb[:, P:5 * P], ACT.Copy), "tk")
                for c in range(NCH):
                    act.wait_ge(*G.after(i, f"y_part{c}"))
                    S.done(f(ysb[:, START[c]:START[c] + LEN[c]], brb[:, 0:LEN[c]], ACT.Copy), f"out{c}")
                    if c == 3:
                        act.wait_ge(gates_out[0], i * 32 + 16 * (NH_A * 2 + 1))
                        plain(N(6), gbuf[0][:, :])
                        split_hi(N(8))
                act.wait_ge(*V.after(i, "y_centred"))
                S.done(f(ysq, yc, ACT.Square), "y_squares")
                act.wait_ge(*G.after(i, "y_square_sums"))
                S.done(f(split2(yv), halves(brb), ACT.Ln, scale=1.0 / 64, bias=gn_eps[:, 0:1]), "y_log")
                act.wait_ge(*S.after(i, "y_log"))
                S.done(f(yv, yv, ACT.Exp, scale=-0.5), "y_rstd")
                act.wait_ge(*G.after(i, "states_turned"))
                S.done(f(r_out, bra[:, 0:P], ACT.Copy), "state_out")
                split_hi(N(9))
                act.wait_ge(gates_out[1], i * 32 + 16 * (NH_A + 1))
                plain(N(7), gbuf[1][:, :])

            G, V, S, Q = (B_[k] for k in ("hgrn_tensor", "hgrn_vector", "hgrn_scalar", "hgrn_pool"))
            with act.Fori(0, NH_B) as i:
                def N(j):
                    return Num(B_AT, B_TILES, i, j)

                act.wait_ge(*V.after(i, "logit0"))
                S.done(f(lbv[:, 2:3], lbv[:, 1:2], ACT.Exp), "soft")
                src = source(N(0))
                f(split2(bef), src, ACT.Exp, scale=-1.0)
                f(split2(bep), src, ACT.Exp).then_inc(evac_done, 1)
                split_hi(N(2))
                act.wait_ge(*V.after(i, "f"))
                S.done(f(AL, bef, ACT.Ln), "log_f")
                plain(N(1), bq)
                split_hi(N(3))
                act.wait_ge(*V.after(i, "log_sums"))
                S.done(f(qhat, AL, ACT.Exp), "decay_exp")
                act.wait_ge(*V.after(i, "end_args"))
                S.done(f(khat, khat, ACT.Exp), "end_exp")
                plain(N(2), bv)
                split_hi(N(4))
                act.wait_ge(*V.after(i, "args0"))
                S.done(f(EE, EE, ACT.Exp), "exp0")

                def rows_of(dst, bank, after, step):
                    act.wait_ge(*G.after(i, after))
                    f(dst[0:C0, 0, :], bank[0:C0, 0:P], ACT.Copy)
                    S.done(f(dst[:, 1:5, :].rearrange("p a b -> p (a b)"), bank[:, P:5 * P], ACT.Copy), step)

                rows_of(khtok, bra, "k_turned", "k_rows")
                rows_of(vbtok, brb, "v_turned", "v_rows")
                src = source(N(3))
                f(split2(bz), src, ACT.Copy)
                f(split2(bez), src, ACT.Exp, scale=-1.0).then_inc(evac_done, 1)
                split_hi(N(5))
                for lv in range(1, LEVELS):
                    act.wait_ge(*V.after(i, f"args{lv}"))
                    S.done(f(EE, EE, ACT.Exp), f"exp{lv}")
                act.wait_ge(gates_out[0], i * 16 + 16 * (NH_A * 2 + NP_C * 2))
                plain(N(4), gbuf[0][:, :])
                split_hi(N(6))
                act.wait_ge(*G.after(i, "outputs"))
                for c in range(NCH):
                    last = f(bjunk[0:LEN[c], :], brb[0:LEN[c], P * c:P * c + P], ACT.Square, accum_out=bss[0:LEN[c], 0, c:c + 1])
                    S.done(last, f"o_sum{c}")
                    act.wait_ge(*S.after(i, f"o_sum{c}"))
                S.done(f(bss[:, 1, :], bss[:, 0, :], ACT.Ln, scale=1.0 / P, bias=eps[:, 0:1]), "o_log")
                act.wait_ge(*S.after(i, "o_log"))
                S.done(f(bss[:, 1, :], bss[:, 1, :], ACT.Exp, scale=-0.5), "o_rstd")
                split_hi(N(7))
                act.wait_ge(gates_out[1], i * 16 + 16 * (NH_A + NP_C * 2))
                plain(N(5), gbuf[1][:, :])
            act.wait_ge(*E_["shift_tensor"].after(0, "shift_turned"))
            E_["shift_scalar"].done(f(shrow[0:64, :], bra[0:64, 0:P], ACT.Copy), "shift_out")

            act.wait_ge(tile_done, PROJ_AT)
            for k in range(KT):
                act.wait_ge(y_here[k // 4], 16)
                f(xh[:, k, :], YIN[:, k, :], ACT.Copy).then_inc(y_hi, 1)
            G, V, S = P_["merge_tensor"], P_["merge_vector"], P_["merge_scalar"]
            with act.Fori(0, KT // 2) as i:
                for j in range(2):
                    act.wait_ge(g_here[j], i * 48 + 48)
                    S.done(f(gs[:, :, :], gin[:, j, :, :], ACT.Sigmoid), f"gates{j}")
                    split_hi(Num(PROJ_AT, 2, i, j + 2))
                    act.wait_ge(*V.after(i, f"part2_{j}"))

            act.wait_ge(tile_done, OUT_AT)
            for k in range(KT):
                act.wait_ge(*V.after(k // 2, f"merged{k % 2}"))
                f(xh[:, k, :], ZF[:, k, :], ACT.Copy).then_inc(z_hi, 1)
            G, V, S = O_["out_tensor"], O_["out_vector"], O_["out_scalar"]
            with act.Fori(0, KT // 2 - 1) as i:
                for j in range(2):
                    split_hi(Num(OUT_AT, 2, i, j + 2))
                    plain(Num(OUT_AT, 2, i, j), zt[j])
                act.wait_ge(*V.after(i, "rows1"))
            plain(N_TILES - 2, zt[0])
            plain(N_TILES - 1, zt[1])
            for t in range(5):
                r = ROWS[t]
                act.wait_ge(*V.after(KT // 2 - 1, "rows1"))
                if t:
                    act.wait_ge(r_sums, 3 * t)
                f(xh[0:r, 0:4, :].rearrange("p a b -> p (a b)")[:, 0:D], YT[0:r, t, :], ACT.Square, accum_out=small[0:r, 24 + t:25 + t]).then_inc(r_sums, 1)
                act.wait_ge(r_sums, 3 * t + 1)
                f(small[0:r, 32 + t:33 + t], small[0:r, 24 + t:25 + t], ACT.Ln, scale=1.0 / D, bias=eps[0:r, 0:1]).then_inc(r_sums, 1)
                act.wait_ge(r_sums, 3 * t + 2)
                f(small[0:r, 40 + t:41 + t], small[0:r, 32 + t:33 + t], ACT.Exp, scale=-0.5).then_inc(r_sums, 1)

        @block.vector
        def _(dve):
            v = nc.vector

            def split_lo(m):
                s = SLOT_OF(m)
                dve.wait_ge(hi_done, m + 1)
                v.tensor_tensor(wlo[:, s, :], wraw[:, s, :], whi[:, s, :].bitcast(F32), ALU.subtract).then_inc(lo_done, 1)

            def mixed(out, pb, diff, mu, S, i, name):
                S.done(v.tensor_tensor(diff[:, 0:T + 1], pb[:, 0:T + 1], pb[:, 1:T + 2], ALU.subtract), name + "_step")
                dve.wait_ge(*S.after(i, name + "_step"))
                v.scalar_tensor_tensor(out=out[:, 0:NS], in0=diff[:, 0:NS], scalar=mu, in1=pb[:, 1:NS + 1], op0=ALU.mult, op1=ALU.add)
                return S.done(v.scalar_tensor_tensor(out=out[:, NS:T], in0=diff[:, NS + 1:T + 1], scalar=mu,
                                                     in1=pb[:, NS + 2:T + 2], op0=ALU.mult, op1=ALU.add), name)

            S = S0["setup_vector"]
            dve.wait_ge(*S0["setup_pool"].after(0, "zeros"))
            dve.wait_ge(vecs_here, 16)
            for t in range(5):
                dve.wait_ge(x_sums, 3 * t + 3)
                v.tensor_scalar(xt[0:ROWS[t], t, :], xt[0:ROWS[t], t, :], small[0:ROWS[t], 16 + t:17 + t], None, ALU.mult).then_inc(x_unit, 1)
            split_lo(0)
            split_lo(1)
            for k in range(KT):
                dve.wait_ge(x_hi, k + 1)
                v.scalar_tensor_tensor(out=xl[:, k, :], in0=ring4[k % 4][:, 0:T], scalar=vec("norm_pre", k),
                                       in1=xh[:, k, :].bitcast(F32), op0=ALU.mult, op1=ALU.subtract).then_inc(x_lo, 1)
            split_lo(2)
            dve.wait_ge(evac_done, 1)
            S.done(v.memset(ONES[0:8, :], 1.0), "ones")
            S.done(v.memset(RR[0:96, :], 0.0), "rows_clear")
            S.done(v.tensor_scalar(GI[0:8, :], GI[0:8, :], vec("b_i", rows=8), None, ALU.add), "i")
            S.done(v.tensor_scalar(XF[0:8, :], XF[0:8, :], vec("b_f", rows=8), None, ALU.add), "f")
            dve.wait_ge(*S.after(0, "f"))
            S.done(v.scalar_tensor_tensor(out=AB[0:8, :], in0=XF[0:8, :], scalar=-1.0, in1=XF[0:8, :], op0=ALU.mult, op1=ALU.max), "f_size")
            dve.wait_ge(*S0["setup_scalar"].after(0, "f_log"))
            S.done(v.scalar_tensor_tensor(out=LF[0:8, :], in0=XF[0:8, :], scalar=0.0, in1=AB[0:8, :], op0=ALU.min, op1=ALU.subtract), "log_f")
            dve.wait_ge(*S.after(0, "log_f"))
            for a, b in ((0, NS), (NS, T)):
                last = v.tensor_tensor_scan(BC[0:8, a:b], ONES[0:8, a:b], LF[0:8, a:b], 0.0, ALU.mult, ALU.add)
            S.done(last, "b")
            dve.wait_ge(*S.after(0, "b"))
            S.done(v.tensor_tensor(GI[0:8, :], GI[0:8, :], BC[0:8, :], ALU.subtract), "g")
            dve.wait_ge(*S.after(0, "g"))
            v.tensor_tensor_scan(MR[0:8, 0:NS], ONES[0:8, 0:NS], GI[0:8, 0:NS], vec("m0", rows=8), ALU.mult, ALU.max)
            S.done(v.tensor_tensor_scan(MR[0:8, NS:T], ONES[0:8, NS:T], GI[0:8, NS:T], 0.0, ALU.mult, ALU.max), "m_max")
            dve.wait_ge(*S.after(0, "m_max"))
            S.done(v.tensor_tensor(MT[0:8, :], MR[0:8, :], BC[0:8, :], ALU.add), "m")
            v.tensor_copy(MC[0:8, 0:1], vec("m0", rows=8))
            v.tensor_copy(MC[0:8, 1:2], MR[0:8, NS - 1:NS])
            S.done(v.tensor_copy(MC[0:8, 2:7], MR[0:8, C0 - 1:T:P]), "m_ends")
            dve.wait_ge(*S.after(0, "m_ends"))
            dve.wait_ge(consts_here, 32)
            S.done(v.tensor_tensor(ME[0:8, :, :], ident[0:8, 0:8].unsqueeze(2).to_broadcast([8, 8, 7]),
                                   MC[0:8, :].unsqueeze(1).to_broadcast([8, 8, 7]), ALU.mult), "ends")
            dve.wait_ge(evac_done, 2)
            dve.wait_ge(*S0["setup_pool"].after(0, "cleared"))
            mixed(low, LOWP, LOWD, vec("low_mu"), S, 0, "low_mixed")
            dve.wait_ge(*S0["setup_scalar"].after(0, "low_exp"))
            S.done(v.tensor_scalar(low[0:64, :], low[0:64, :], 1.0, None, ALU.add), "low_1")
            dve.wait_ge(*S.after(0, "low_1"))
            S.done(v.reciprocal(low[0:64, :], low[0:64, :]), "low_2")
            dve.wait_ge(*S.after(0, "low_2"))
            S.done(v.tensor_scalar(low[0:64, :], low[0:64, :], -2.0, 1.0, ALU.mult, ALU.add), "low_tanh")
            dve.wait_ge(*S0["setup_scalar"].after(0, "ends"))
            TKv = TK[:, :, :].rearrange("p c n -> p n c")
            v.tensor_copy(pk_all[:, :, 0:5], TKv[:, 0:8, :])
            v.tensor_tensor(pk_all[:, :, 6:10], TKv[:, 0:8, 1:5], EB[:, :, 3:7], ALU.subtract)
            v.tensor_tensor(pk_all[0:64, :, 5:6], TKv[0:64, 0:8, 0:1], EB[0:64, :, 1:2], ALU.subtract)
            v.tensor_tensor(pk_all[64:128, :, 5:6], TKv[64:128, 0:8, 0:1], EB[64:128, :, 2:3], ALU.subtract)
            v.tensor_tensor(pk_all[:, :, 11:15], EB[:, :, 2:6], TKv[:, 32:40, 1:5], ALU.subtract)
            v.tensor_tensor(pk_all[:, :, 10:11], EB[:, :, 0:1], TKv[:, 32:40, 0:1], ALU.subtract)
            v.tensor_scalar(pk_all[:, :, 15:20], TKv[:, 64:72, :], -1.0, None, ALU.mult)
            v.tensor_tensor(pk_all[:, :, 20:21], EB[:, :, 0:1], EB[:, :, 1:2], ALU.subtract)
            S.done(v.tensor_tensor(pk_all[:, :, 21:25], EB[:, :, 2:6], EB[:, :, 3:7], ALU.subtract), "scalar_args")
            v.tensor_copy(pk_all[:, :, 25:26], vecs[:, VEC["mlstm_norm"]:VEC["mlstm_norm"] + 8].unsqueeze(2))
            S.done(v.tensor_copy(pk_all[:, :, 26:27], vecs[:, VEC["n0"]:VEC["n0"] + 8].unsqueeze(2)), "head_vectors")
            dve.wait_ge(*S0["setup_scalar"].after(0, "scalars"))

            G, V, S, Q = (A_[k] for k in ("mlstm_tensor", "mlstm_vector", "mlstm_scalar", "mlstm_pool"))
            dve.wait_ge(*S0["setup_pool"].after(0, "mlstm_cleared"))
            with dve.Fori(0, NH_A) as i:
                def N(j):
                    return Num(A_AT, A_TILES, i, j)

                def own(step):
                    dve.wait_ge(*V.after(i, step))

                split_lo(N(1))
                V.done(v.tensor_copy(pk[:, :], pk_all[:, bass.ds(i, 1), :].rearrange("p a n -> p (a n)")), "scalars")
                V.done(v.tensor_scalar(DM[0:8, :], MR[0:8, :], ident[0:8, bass.ds(i, 1)], None, ALU.mult), "head_m")
                split_lo(N(2))
                own("scalars")
                V.done(v.tensor_copy(AST[:, 0, P:P + 1], pk[:, 26:27]), "n0")
                split_lo(N(3))
                split_lo(N(4))
                dve.wait_ge(*G.after(i, "v_turned"))
                v.tensor_copy(vtok[0:C0, 0, 0:P], brb[0:C0, 0:P])
                V.done(v.tensor_copy(vtok[:, 1:5, 0:P], brb[:, P:5 * P].rearrange("p (c n) -> p c n", c=4)), "v_rows")
                own("v_rows")
                v.tensor_scalar(wsv[0:C0, 0, :], vtok[0:C0, 0, :], pk[0:C0, 5:6], None, ALU.mult)
                for c in range(1, NCH):
                    last = v.tensor_scalar(wsv[:, c, :], vtok[:, c, :], pk[:, 5 + c:6 + c], None, ALU.mult)
                V.done(last, "v_weighted")
                split_lo(N(5))
                dve.wait_ge(*G.after(i, "m_everywhere"))
                for c in range(NCH):
                    o, n = psum_col(c), LEN[c]
                    last = v.tensor_scalar(WW[0:n, c, 0:n], bra[0:n, o:o + n], pk[0:n, c:c + 1], 0.0, ALU.subtract, ALU.max)
                V.done(last, "decay_args")
                dve.wait_ge(*G.after(i, "scores"))
                dve.wait_ge(*Q.after(i, "masked"))
                v.tensor_tensor(PP[0:C0, 0, 0:C0], brb[0:C0, 0:C0], WW[0:C0, 0, 0:C0], ALU.mult)
                V.done(v.tensor_tensor(PP[:, 1:5, :].rearrange("p a b -> p (a b)"), brb[:, P:5 * P],
                                       WW[:, 1:5, :].rearrange("p a b -> p (a b)"), ALU.mult), "probs")
                split_lo(N(6))
                dve.wait_ge(*G.after(i, "updates"))
                dve.wait_ge(*S.after(i, "k_rows"))
                v.scalar_tensor_tensor(out=AST[:, 6, :], in0=AST[:, 0, :], scalar=pk[:, 20:21], in1=bra[:, 0:129], op0=ALU.mult, op1=ALU.add)
                V.done(v.tensor_copy(AST[:, 1, :], bra[:, 129:258]), "state1")
                for c in range(1, NCH):
                    o = {1: 258, 2: 512, 3: 641, 4: 770}[c]
                    own(f"state{c}")
                    V.done(v.scalar_tensor_tensor(out=AST[:, c + 1, :], in0=AST[:, c, :], scalar=pk[:, 20 + c:21 + c],
                                                  in1=bra[:, o:o + 129], op0=ALU.mult, op1=ALU.add), f"state{c + 1}" if c < 4 else "states")
                dve.wait_ge(*G.after(i, "inside"))
                v.tensor_copy(num[0:C0, 0, :], brb[0:C0, 258:387])
                v.tensor_copy(num[:, 1:3, :], brb[:, 0:258].rearrange("p (c n) -> p c n", c=2))
                V.done(v.tensor_copy(num[:, 3:5, :], brb[:, 512:770].rearrange("p (c n) -> p c n", c=2)), "inside")
                split_lo(N(7))
                dve.wait_ge(*G.after(i, "carried"))
                own("inside")
                for c in range(NCH):
                    o, n = part_col(c), (NS if c == 0 else P)
                    last = v.scalar_tensor_tensor(out=num[0:n, c, :], in0=bra[0:n, o:o + 129], scalar=pk[0:n, 10 + c:11 + c],
                                                  in1=num[0:n, c, :], op0=ALU.mult, op1=ALU.add)
                V.done(last, "num")
                own("num")
                den = num[:, :, P:P + 1].rearrange("p c n -> p (c n)")
                V.done(v.scalar_tensor_tensor(out=smA[:, 0, :], in0=den, scalar=-1.0, in1=den, op0=ALU.mult, op1=ALU.max), "den_size")
                for c in range(NCH):
                    n = LEN[c]
                    last = v.bn_stats(stats[0:n, c, :], num[0:n, c, 0:P])
                V.done(last, "stats")
                own("den_size")
                V.done(v.tensor_tensor(smA[:, 0, :], smA[:, 0, :], pk[:, 15:20], ALU.max), "den")
                own("stats")
                own("den")
                V.done(v.reciprocal(smA[:, 1, :], smA[:, 0, :]), "den_inv")
                for c in range(NCH):
                    n = LEN[c]
                    last = v.bn_aggr(aggr[0:n, c, :], stats[0:n, c, :])
                V.done(last, "aggr")
                own("den_inv")
                V.done(v.tensor_tensor(smA[:, 2, :], smA[:, 1, :], smA[:, 1, :], ALU.mult), "den_inv2")
                own("den_inv2")
                V.done(v.tensor_tensor(smA[:, 3, :], aggr[:, :, 1:2].rearrange("p c n -> p (c n)"), smA[:, 2, :], ALU.mult), "h_var")
                dve.wait_ge(evac_done, N(4) + 1)
                V.done(v.tensor_scalar(aez, aez, 1.0, None, ALU.add), "gate1")
                own("gate1")
                V.done(v.scalar_tensor_tensor(out=aez, in0=aeo, scalar=1.0, in1=aez, op0=ALU.add, op1=ALU.mult), "gate2")
                own("gate2")
                V.done(v.reciprocal(aez, aez), "gate3")
                own("gate3")
                V.done(v.scalar_tensor_tensor(out=agz, in0=az, scalar=pk[:, 25:26], in1=aez, op0=ALU.mult, op1=ALU.mult), "gate")
                dve.wait_ge(*S.after(i, "h_rstd"))
                V.done(v.tensor_tensor(smA[:, 6, :], smA[:, 5, :], smA[:, 1, :], ALU.mult), "h_scale")
                own("h_scale")
                for c in range(NCH):
                    n = LEN[c]
                    last = v.tensor_scalar(hn[0:n, c, :], num[0:n, c, 0:P], aggr[0:n, c, 0:1], smA[0:n, 6, c:c + 1], ALU.subtract, ALU.mult)
                V.done(last, "h_unit")
                V.done(v.tensor_copy(nout[:, :, bass.ds(i, 1)].rearrange("p m a -> p (m a)"), AST[:, 5:7, P:P + 1].rearrange("p m a -> p (m a)")), "n_out")
                split_lo(N(8))
                dve.wait_ge(*G.after(i, "h_turned"))
                own("gate")
                v.tensor_tensor(ybuf[:, 0:SPLIT], brb[:, 0:SPLIT], agz[:, 0:SPLIT], ALU.mult)
                V.done(v.tensor_tensor(ybuf[:, SPLIT:T], brb[:, 512:512 + T - SPLIT], agz[:, SPLIT:T], ALU.mult), "y")
                dve.wait_ge(y_out, i * 16 + 16)
                dve.wait_ge(*S.after(i, "state_out"))
                dve.wait_ge(*G.after(i, "states_turned"))

            G, V, S, Q = (C_[k] for k in ("rwkv_tensor", "rwkv_vector", "rwkv_scalar", "rwkv_pool"))
            dve.wait_ge(*A2["norm_rows_tensor"].after(0, "n_turned"))
            split_lo(C_AT + 1)
            with dve.Fori(0, NP_C) as i:
                def N(j):
                    return Num(C_AT, C_TILES, i, j)

                def own(step):
                    dve.wait_ge(*V.after(i, step))

                def tt(out, a, b, op, step=None):
                    ins = v.tensor_tensor(out, a, b, op)
                    return V.done(ins, step) if step else ins

                group = dve.snap(i * PAIR_VECS + VEC["pair"])
                V.done(v.tensor_copy(pv[:, 0:PAIR_VECS], vecs[:, bass.ds(group, PAIR_VECS)]), "vectors")
                own("vectors")
                v.tensor_scalar(pv[:, 16:18], pv[:, W0:A0 + 1], -1.0, None, ALU.mult)
                v.tensor_scalar(pv[:, KA1:KA1 + 1], pv[:, K_A:K_A + 1], -1.0, 1.0, ALU.mult, ALU.add)
                v.tensor_copy(PB[0][:, 0:1], pv[:, CACHE + 1:CACHE + 2])
                V.done(v.tensor_copy(PB[1][:, 0:1], pv[:, CACHE:CACHE + 1]), "negated")
                v.memset(PB[0][:, NS + 1:NS + 2], 0.0)
                V.done(v.memset(PB[1][:, NS + 1:NS + 2], 0.0), "streams_apart")
                split_lo(N(2))
                dve.wait_ge(*S.after(i, "rank_exps"))
                v.tensor_scalar(LL, LL, 1.0, None, ALU.add)
                V.done(v.tensor_scalar(ca, ca, 1.0, None, ALU.add), "ranks1")
                own("ranks1")
                v.reciprocal(LL, LL)
                V.done(v.reciprocal(ca, ca), "a")
                own("a")
                V.done(v.tensor_scalar(cb, LL, -float(np.exp(-0.5)), None, ALU.mult), "log_decay")
                own("log_decay")
                V.done(v.tensor_tensor_scan(LL, mask("carry"), cb, 0.0, ALU.mult, ALU.add), "log_sums")
                own("log_sums")
                tt(kkh, LL, cb, ALU.subtract)
                tt(kE[:, 0:NS], LL[:, NS - 1:NS].to_broadcast([P, NS]), LL[:, 0:NS], ALU.subtract)
                tt(kE[:, NS:C0], LL[:, C0 - 1:C0].to_broadcast([P, NM]), LL[:, NS:C0], ALU.subtract)
                tt(kE[:, C0:T].rearrange("p (c n) -> p c n", c=4), LL[:, C0 + P - 1:T:P].unsqueeze(2).to_broadcast([P, 4, P]),
                   LL[:, C0:T].rearrange("p (c n) -> p c n", c=4), ALU.subtract, "log_decay_sums")
                own("streams_apart")
                dve.wait_ge(evac_done, N(0) + 1)
                mixed(ck, PB[0], DD, pv[:, MU + 1:MU + 2], V, i, "k")
                own("k")
                dve.wait_ge(states_out, i * 64 + 16 * (2 * NH_A + 2))
                V.done(v.tensor_scalar(kk, ck, pv[:, K_K:K_K + 1], None, ALU.mult), "kk_raw")
                own("kk_raw")
                V.done(v.tensor_scalar(cb, ca, pv[:, K_A:K_A + 1], pv[:, KA1:KA1 + 1], ALU.mult, ALU.add), "k_factor")
                own("k_factor")
                tt(ck, ck, cb, ALU.mult, "k_new")
                dve.wait_ge(evac_done, N(1) + 1)
                mixed(cr, PB[1], DD, pv[:, MU:MU + 1], V, i, "r")
                own("r")
                own("k_new")
                dve.wait_ge(*S.after(i, "decay_exps"))
                dve.wait_ge(*S.after(i, "kk_squares"))
                v.tensor_copy(PB[0][:, 0:1], pv[:, CACHE + 2:CACHE + 3])
                V.done(v.scalar_tensor_tensor(out=bon, in0=cr, scalar=pv[:, R_K:R_K + 1], in1=ck, op0=ALU.mult, op1=ALU.mult), "bonus_terms")
                v.tensor_copy(eends[:, 0:2], rh[:, NS - 1:C0:NM])
                V.done(v.tensor_copy(eends[:, 2:6], rh[:, C0 + P - 1:T:P]), "end_decays")
                own("end_decays")
                tt(rh, rh, cr, ALU.mult, "rh")
                split_lo(N(3))
                dve.wait_ge(*G.after(i, "kk_lengths"))
                V.done(v.tensor_scalar(split2(ctmp), halves(bra), 1e-24, None, ALU.max), "kk_floor")
                dve.wait_ge(evac_done, N(2) + 1)
                own("bonus_terms")
                mixed(cvv, PB[0], DD, pv[:, MU + 2:MU + 3], V, i, "v")
                split_lo(N(4))
                dve.wait_ge(*S.after(i, "kk_rsqrt"))
                v.tensor_copy(PB[1][:, 0:1], pv[:, CACHE + 3:CACHE + 4])
                tt(kk, kk, ctmp, ALU.mult, "kk")
                own("kk")
                tt(cb, kk, ca, ALU.mult, "b")
                tt(kkh, kkh, kk, ALU.mult, "kkh")
                own("b")
                tt(bh, kh, cb, ALU.mult, "bh")
                own("bh")
                tt(kh, kh, ck, ALU.mult, "kh")
                tt(bE, kE, cb, ALU.mult, "bE")
                own("bE")
                tt(kE, kE, ck, ALU.mult, "kE")
                dve.wait_ge(*G.after(i, "bonus_sums"))
                own("v")
                V.done(v.tensor_copy(RST[:, 0, :], brb[:, 896:960]), "state0")
                V.done(v.tensor_tensor(split2(bon), halves(brb), split2(cvv), ALU.mult), "bonus")
                split_lo(N(5))
                dve.wait_ge(evac_done, N(3) + 1)
                own("kk")
                mixed(cz, PB[1], DD, pv[:, MU + 3:MU + 4], V, i, "z")
                dve.wait_ge(*S.after(i, "z_exp"))
                e1 = PB[0][:, 0:T]
                V.done(v.tensor_scalar(e1, e1, 1.0, None, ALU.add), "z1")
                own("z1")
                V.done(v.reciprocal(e1, e1), "z2")
                own("z2")
                tt(cz, cz, e1, ALU.mult, "gate")
                own("gate")

                def masked(dst, h, name, bank, after, step):
                    m = masks[:, CONST_AT[name][0]:CONST_AT[name][0] + 2 * P]
                    dve.wait_ge(*G.after(i, after))
                    tt(dst[0:C0, 5 * h, 0:C0], bank[0:C0, 0:C0], m[0:C0, 0:C0], ALU.mult)
                    tt(dst[:, 5 * h + 1:5 * h + 5, :], bank[:, P:5 * P].rearrange("p (c n) -> p c n", c=4),
                       m[:, P:2 * P].unsqueeze(1).to_broadcast([P, 4, P]), ALU.mult, step)

                def rows_in(lv):
                    return (C0 if lv < 4 else NS) if lv < 6 else 0

                def lower_parts(lv, down, up):
                    n0 = rows_in(lv)
                    for dst, src, name, side in ((UU, down, "down", 0), (VV, up, "up", 1)):
                        mk = masks[:, CONST_AT[name][0] + 64 * lv:CONST_AT[name][0] + 64 * lv + 64]
                        if lv == 0:
                            src = src[:, :, side::2]
                        if n0:
                            tt(dst[0:n0, 0:6:5, 0:n0 // 2], src[0:n0, 0:6:5, 0:n0 // 2],
                               mk[0:n0, 0:n0 // 2].unsqueeze(1).to_broadcast([n0, 2, n0 // 2]), ALU.mult)
                        for h in range(2):
                            last = tt(dst[:, 5 * h + 1:5 * h + 5, :], src[:, 5 * h + 1:5 * h + 5, :],
                                      mk.unsqueeze(1).to_broadcast([P, 4, 64]), ALU.mult)
                    V.done(last, f"low{lv}")

                def subtract_parts(lv, down, up):
                    n0 = rows_in(lv)
                    for dst, src, side in ((DD1, down, 0), (DDT, up, 1)):
                        for q0, q1, n in ((0, 6, n0), (1, 5, P), (6, 10, P)):
                            if not n:
                                continue
                            step = 5 if q0 == 0 else 1
                            cols = dst[0:n, q0:q1:step, 0:n].rearrange("p q (b two w) -> p q b two w", two=2, w=1 << lv)[:, :, :, side, :]
                            last = tt(cols, cols, src[0:n, q0:q1:step, 0:n // 2].rearrange("p q (b w) -> p q b w", w=1 << lv), ALU.subtract)
                    V.done(last, f"inv{lv}")

                own("kE")
                dve.wait_ge(*G.after(i, "kE_turned"))
                masked(AA, 0, "after", bra, "ub0_", "ub0")
                masked(AA, 1, "after", brb, "ub1_", "ub1")
                masked(AT, 0, "before", bra, "bu0_", "bu0")
                masked(AT, 1, "before", brb, "bu1_", "bu1")
                masked(KTm, 0, "before", bra, "uk0_", "uk0")
                masked(KTm, 1, "before", brb, "uk1_", "uk1")
                masked(BM, 0, "causal", bra, "yb0_", "yb0")
                masked(BM, 1, "causal", brb, "yb1_", "yb1")
                masked(KM, 0, "causal", bra, "yk0_", "yk0")
                masked(KM, 1, "causal", brb, "yk1_", "yk1")
                lower_parts(0, AA, AT)
                dve.wait_ge(*Q.after(i, "unit_blocks"))
                own("low0")
                subtract_parts(0, UU, VV)
                dve.wait_ge(*G.after(i, "uk_v"))
                v.tensor_copy(W1[0:C0, 0:6:5, :], bra[0:C0, 0:640].rearrange("p (q n) -> p q n", q=10)[:, 0:6:5, :])
                v.tensor_copy(W1[:, 1:5, :], bra[:, 64:320].rearrange("p (q n) -> p q n", q=4))
                V.done(v.tensor_copy(W1[:, 6:10, :], bra[:, 384:640].rearrange("p (q n) -> p q n", q=4)), "w1")
                split_lo(N(6))

                pa = bra[:, 0:640].rearrange("p (q n) -> p q n", q=10)
                pb = brb[:, 0:640].rearrange("p (q n) -> p q n", q=10)
                for lv in range(1, LEVELS):
                    dve.wait_ge(*G.after(i, f"au{lv}"))
                    lower_parts(lv, pa, pb)
                    dve.wait_ge(*G.after(i, f"du{lv}"))
                    subtract_parts(lv, pa, pb)
                    if lv == 5:
                        split_lo(N(7))
                dve.wait_ge(*G.after(i, "solved"))
                v.tensor_copy(TV[0:C0, 0:6:5, :], bra[0:C0, 0:640].rearrange("p (q n) -> p q n", q=10)[:, 0:6:5, :])
                v.tensor_copy(TV[:, 1:5, :], bra[:, 64:320].rearrange("p (q n) -> p q n", q=4))
                V.done(v.tensor_copy(TV[:, 6:10, :], bra[:, 384:640].rearrange("p (q n) -> p q n", q=4)), "tv")
                own("tv")
                ut = utok.rearrange("p a b -> p (a b)")
                for c in range(NCH):
                    n = NS if c == 0 else P
                    dve.wait_ge(*G.after(i, f"u_carried{c}"))
                    if c:
                        dve.wait_ge(*G.after(i, f"y_part{c - 1}"))
                    if c == 0:
                        v.tensor_scalar(ut[NS:C0, 0:P].rearrange("p (h n) -> p h n", h=2), TV[NS:C0, 0:6:5, :], -1.0, None, ALU.mult)
                    V.done(v.scalar_tensor_tensor(out=ut[0:n, 0:P].rearrange("p (h n) -> p h n", h=2), in0=halves(bra, 64)[0:n], scalar=-1.0,
                                                  in1=TV[0:n, c:c + 6:5, :], op0=ALU.mult, op1=ALU.subtract), f"u{c}")
                    dve.wait_ge(*G.after(i, f"state_part{c}"))
                    if c == 0:
                        v.scalar_tensor_tensor(out=RST[:, 6, :], in0=RST[:, 0, :], scalar=eends[:, 0:1], in1=brb[:, 512:576], op0=ALU.mult, op1=ALU.add)
                        V.done(v.tensor_copy(RST[:, 1, :], bra[:, 256:320]), "state1")
                    else:
                        own(f"state{c}")
                        V.done(v.scalar_tensor_tensor(out=RST[:, c + 1, :], in0=RST[:, c, :], scalar=eends[:, c + 1:c + 2],
                                                      in1=brb[:, 512:576], op0=ALU.mult, op1=ALU.add), f"state{c + 1}")
                split_lo(N(8))
                dve.wait_ge(*G.after(i, "y_sums"))
                V.done(v.scalar_tensor_tensor(out=split2(yc), in0=halves(bra), scalar=-1.0 / 64, in1=split2(ysb), op0=ALU.mult, op1=ALU.add), "y_centred")
                own("state5")
                dve.wait_ge(*S.after(i, "y_rstd"))
                tt(yc, yc, yv, ALU.mult, "y_unit")
                own("y_unit")
                V.done(v.tensor_scalar(yc, yc, pv[:, GN_G:GN_G + 1], pv[:, GN_B:GN_B + 1], ALU.mult, ALU.add), "y_affine")
                own("y_affine")
                tt(yc, yc, bon, ALU.add, "y_bonus")
                own("y_bonus")
                dve.wait_ge(y_out, i * 16 + 16 * NH_A)
                tt(ybuf[:, :], yc, cz, ALU.mult, "y")
                split_lo(N(9))

            G, V, S, Q = (B_[k] for k in ("hgrn_tensor", "hgrn_vector", "hgrn_scalar", "hgrn_pool"))
            with dve.Fori(0, NH_B) as i:
                def N(j):
                    return Num(B_AT, B_TILES, i, j)

                def own(step):
                    dve.wait_ge(*V.after(i, step))

                def regions(lv):
                    if lv < 4:
                        return [(0, T)]
                    return [(0, NS), (C0, T)] if lv < 6 else [(C0, T)]

                def level_args(lv):
                    w = 1 << lv
                    if lv:
                        own(f"scaled{lv - 1}")
                    for a, b in regions(lv):
                        A = AL[:, a:b].rearrange("p (n two w) -> p n two w", two=2, w=w)
                        E = EE[:, a:b].rearrange("p (n two w) -> p n two w", two=2, w=w)
                        nb = (b - a) // (2 * w)
                        ref = A[:, :, 0, w - 1:w].to_broadcast([P, nb, w])
                        v.tensor_tensor(E[:, :, 1, :], A[:, :, 1, :], ref, ALU.subtract)
                        last = v.tensor_tensor(E[:, :, 0, :], ref, A[:, :, 0, :], ALU.subtract)
                    V.done(last, f"args{lv}")

                col = dve.snap(i + VEC["lb"])
                col2 = dve.snap(i + VEC["hgrn_norm"])
                v.tensor_copy(lbv[:, 5:6], vecs[:, bass.ds(col2, 1)])
                V.done(v.tensor_copy(lbv[:, 0:1], vecs[:, bass.ds(col, 1)]), "logit")
                own("logit")
                V.done(v.tensor_tensor(lbv[:, 1:2], lbv[:, 0:1], lbv[:, 0:1], ALU.subtract), "logit0")
                dve.wait_ge(*S.after(i, "soft"))
                V.done(v.reciprocal(lbv[:, 3:4], lbv[:, 2:3]), "soft_inv")
                own("soft_inv")
                V.done(v.tensor_tensor(lbv[:, 6:7], lbv[:, 3:4], lbv[:, 2:3], ALU.mult), "softmax")
                own("softmax")
                V.done(v.tensor_tensor(lbv[:, 4:5], lbv[:, 6:7], lbv[:, 6:7], ALU.subtract), "bound")
                own("bound")
                V.done(v.tensor_scalar(lbv[:, 7:8], lbv[:, 4:5], -1.0, 1.0, ALU.mult, ALU.add), "rest")
                own("rest")
                dve.wait_ge(evac_done, N(0) + 1)
                v.tensor_scalar(bef, bef, 1.0, None, ALU.add)
                V.done(v.tensor_scalar(bep, bep, 1.0, None, ALU.add), "f1")
                own("f1")
                v.reciprocal(bef, bef)
                V.done(v.reciprocal(bep, bep), "f2")
                own("f2")
                V.done(v.tensor_scalar(bk, bep, lbv[:, 7:8], None, ALU.mult), "k")
                V.done(v.tensor_scalar(bef, bef, lbv[:, 7:8], lbv[:, 4:5], ALU.mult, ALU.add), "f3")
                own("f3")
                V.done(v.tensor_scalar(bef, bef, 1e-19, None, ALU.max), "f")
                split_lo(N(2))
                dve.wait_ge(*S.after(i, "log_f"))
                V.done(v.tensor_scalar(bef, AL, 1.0, None, ALU.mult), "log_copy")
                own("log_copy")
                V.done(v.tensor_tensor_scan(AL, mask("carry"), bef, 0.0, ALU.mult, ALU.add), "log_sums")
                own("log_sums")
                v.tensor_tensor(khat[:, 0:NS], AL[:, NS - 1:NS].to_broadcast([P, NS]), AL[:, 0:NS], ALU.subtract)
                v.tensor_tensor(khat[:, NS:C0], AL[:, C0 - 1:C0].to_broadcast([P, NM]), AL[:, NS:C0], ALU.subtract)
                V.done(v.tensor_tensor(khat[:, C0:T].rearrange("p (c n) -> p c n", c=4), AL[:, C0 + P - 1:T:P].unsqueeze(2).to_broadcast([P, 4, P]),
                                       AL[:, C0:T].rearrange("p (c n) -> p c n", c=4), ALU.subtract), "end_args")
                level_args(0)
                split_lo(N(3))
                dve.wait_ge(*S.after(i, "end_exp"))
                dve.wait_ge(evac_done, N(1) + 1)
                v.tensor_copy(bend[:, 0:2], qhat[:, NS - 1:C0:NM])
                V.done(v.tensor_copy(bend[:, 2:6], qhat[:, C0 + P - 1:T:P]), "ends")
                v.tensor_tensor(khat, khat, bk, ALU.mult)
                own("ends")
                V.done(v.tensor_tensor(qhat, qhat, bq, ALU.mult), "khat")
                own("khat")
                V.done(v.memset(qhat[:, NS:C0], 0.0), "meta_from_zero")
                split_lo(N(4))

                def level_scaled(lv):
                    w = 1 << lv
                    dve.wait_ge(*S.after(i, f"exp{lv}"))
                    if lv >= 2:
                        dve.wait_ge(*G.after(i, f"pairs{lv - 2}"))
                    for a, b in regions(lv):
                        def at(x, side):
                            return x[:, a:b].rearrange("p (n two w) -> p n two w", two=2, w=w)[:, :, side, :]
                        v.tensor_tensor(at(QK[lv % 2], 1), at(EE, 1), at(bq, 1), ALU.mult)
                        last = v.tensor_tensor(at(QK[lv % 2], 0), at(EE, 0), at(bk, 0), ALU.mult)
                    V.done(last, f"scaled{lv}")

                def level_masked(lv):
                    bank = br[lv % 2]
                    dve.wait_ge(*G.after(i, f"pairs{lv}"))
                    mo = CONST_AT["levels"][0] + P * lv
                    mk = masks[:, mo:mo + P]
                    dst = PT[lv % 2] if lv else PS
                    if lv >= 3:
                        dve.wait_ge(*Q.after(i, f"add{lv - 2}"))
                    if lv == 6:
                        V.done(v.memset(dst[0:C0, 0, 0:C0], 0.0), "no_pairs6")
                    else:
                        v.tensor_tensor(dst[0:C0, 0, 0:C0], bank[0:C0, 0:C0], mk[0:C0, 0:C0], ALU.mult)
                    V.done(v.tensor_tensor(dst[:, 1:5, :], bank[:, P:5 * P].rearrange("p (c n) -> p c n", c=4),
                                           mk.unsqueeze(1).to_broadcast([P, 4, P]), ALU.mult), f"masked{lv}")

                level_scaled(0)
                for lv in range(LEVELS + 1):
                    if lv + 1 < LEVELS:
                        level_args(lv + 1)
                        level_scaled(lv + 1)
                    level_masked(lv)
                    if lv == 0:
                        split_lo(N(5))
                    elif lv == LEVELS - 1:
                        split_lo(N(6))
                dve.wait_ge(states_out, i * 32 + 16 * (2 * NH_A + 2 + 4 * NP_C))
                dve.wait_ge(*G.after(i, "updates"))
                dve.wait_ge(hgrn_in, i * 16 + 16)
                v.scalar_tensor_tensor(out=BST[:, 6, :], in0=BST[:, 0, :], scalar=bend[:, 0:1], in1=bra[:, 0:P], op0=ALU.mult, op1=ALU.add)
                V.done(v.tensor_copy(BST[:, 1, :], bra[:, P:2 * P]), "state1")
                for c in range(1, NCH):
                    own(f"state{c}")
                    V.done(v.scalar_tensor_tensor(out=BST[:, c + 1, :], in0=BST[:, c, :], scalar=bend[:, c + 1:c + 2],
                                                  in1=bra[:, P * c + P:P * c + 2 * P], op0=ALU.mult, op1=ALU.add), f"state{c + 1}" if c < 4 else "states")
                dve.wait_ge(evac_done, N(3) + 1)
                V.done(v.tensor_scalar(bez, bez, 1.0, None, ALU.add), "z1")
                own("z1")
                V.done(v.reciprocal(bez, bez), "z2")
                own("z2")
                V.done(v.scalar_tensor_tensor(out=bz, in0=bz, scalar=lbv[:, 5:6], in1=bez, op0=ALU.mult, op1=ALU.mult), "gate")
                dve.wait_ge(*S.after(i, "o_rstd"))
                for c in range(NCH):
                    n = LEN[c]
                    last = v.tensor_scalar(on[0:n, c, :], brb[0:n, P * c:P * c + P], bss[0:n, 1, c:c + 1], None, ALU.mult)
                V.done(last, "o_unit")
                dve.wait_ge(*G.after(i, "o_turned"))
                own("gate")
                dve.wait_ge(y_out, i * 16 + 16 * (NH_A + NP_C))
                v.tensor_tensor(ybuf[:, 0:SPLIT], bra[:, 0:SPLIT], bz[:, 0:SPLIT], ALU.mult)
                V.done(v.tensor_tensor(ybuf[:, SPLIT:T], bra[:, 512:512 + T - SPLIT], bz[:, SPLIT:T], ALU.mult), "y")
                split_lo(N(7))

            sv = shifts[:, 0:32].rearrange("p (i j m) -> p j m i", j=4, m=2)
            pm = shpad[:, :].rearrange("p (m n) -> p m n", m=2)
            for j, at in ((0, 0), (1, 4), (2, 8), (3, 13)):
                v.tensor_copy(pm[:, :, at:at + 4], sv[:, j, :, :])
            E_["shift_vector"].done(v.tensor_copy(pm[:, :, 12:13], shifts[:, 32:34].unsqueeze(2)), "columns")

            for k in range(KT):
                dve.wait_ge(y_hi, k + 1)
                v.tensor_tensor(xl[:, k, :], YIN[:, k, :], xh[:, k, :].bitcast(F32), ALU.subtract).then_inc(y_split, 1)
            G, V, S = P_["merge_tensor"], P_["merge_vector"], P_["merge_scalar"]
            dve.wait_ge(y_split, KT)
            banks3 = [acc[0], acc[1], bra]
            with dve.Fori(0, KT // 2) as i:
                for j in range(2):
                    n = Num(PROJ_AT, 2, i, j)
                    row = dve.snap(i * 2 + j)
                    z = ZF[:, bass.ds(row, 1), :].rearrange("p a t -> p (a t)")
                    dve.wait_ge(*S.after(i, f"gates{j}"))
                    for b in range(3):
                        if b < 2:
                            dve.wait_ge(*G.after(i, f"proj{b}_{j}"))
                        else:
                            dve.wait_ge(tile_done, n + 1)
                        dst = mz[b]
                        V.done(v.tensor_tensor(split2(dst), halves(banks3[b]), split2(gs[:, b, :]), ALU.mult), f"part{b}_{j}")
                        if b == 1:
                            dve.wait_ge(*V.after(i, f"part1_{j}"))
                            V.done(v.tensor_tensor(mz[0], mz[0], mz[1], ALU.add), f"sum1_{j}")
                    dve.wait_ge(*V.after(i, f"part2_{j}"))
                    V.done(v.tensor_tensor(z, mz[0], mz[2], ALU.add), f"merged{j}")
                    split_lo(Num(PROJ_AT, 2, i, j + 2))
                    dve.wait_ge(*V.after(i, f"merged{j}"))

            for k in range(KT):
                dve.wait_ge(z_hi, k + 1)
                v.tensor_tensor(xl[:, k, :], ZF[:, k, :], xh[:, k, :].bitcast(F32), ALU.subtract).then_inc(z_split, 1)
            dve.wait_ge(z_split, KT)
            G, V, S = O_["out_tensor"], O_["out_vector"], O_["out_scalar"]

            def rows_out(i, j, col):
                dve.wait_ge(*G.after(i, f"turned{j}"))
                v.tensor_copy(YT[:, 0:4, bass.ds(col, P)], br[j][:, 0:512].rearrange("p (t n) -> p t n", t=4))
                V.done(v.tensor_copy(YT[0:ROWS[4], 4, bass.ds(col, P)], br[j][0:ROWS[4], 512:640]), f"rows{j}")

            with dve.Fori(0, KT // 2 - 1) as i:
                for j in range(2):
                    split_lo(Num(OUT_AT, 2, i, j + 2))
                    rows_out(i, j, dve.snap(i * 256 + 128 * j))
            for j in range(2):
                rows_out(KT // 2 - 1, j, 128 * (14 + j))
            dve.wait_ge(post_here, 16)
            for t in range(5):
                r = ROWS[t]
                dve.wait_ge(r_sums, 3 * t + 3)
                v.scalar_tensor_tensor(out=YT[0:r, t, :], in0=YT[0:r, t, :], scalar=small[0:r, 40 + t:41 + t], in1=wraw[0:r, 0, :],
                                       op0=ALU.mult, op1=ALU.mult).then_inc(post_done, 1)
                dve.wait_ge(post_done, t + 1)
                dve.wait_ge(res_here[t % 2], 16 * (t // 2 + 1))
                v.tensor_tensor(xres[0:r, t % 2, :], xres[0:r, t % 2, :], YT[0:r, t, :], ALU.add).then_inc(res_done, 1)

        @block.gpsimd
        def _(pool):
            g = nc.gpsimd
            S = S0["setup_pool"]
            g.memset(small[:, :], 1.0)
            g.memset(eps[:, :], EPS)
            g.memset(gn_eps[:, :], GN_EPS)
            g.memset(tenln2[:, :], 10.0 * float(np.log(2.0)))
            g.memset(shpad[:, :], 0.0)
            g.memset(pk_all[:, :, :].rearrange("p a b -> p (a b)"), 0.0)
            g.memset(bss[:, :, :], 1.0)
            S.done(g.memset(ones8[:, :], 1.0), "zeros")
            pool.wait_ge(x_turned, KT)
            g.memset(LOWP[:, NS + 1:NS + 2], 0.0)
            pool.wait_ge(vecs_here, 16)
            g.tensor_copy(LOWP[:, 0:1], vec("low_cache"))
            S.done(g.memset(TK[:, 0, :], 0.0), "cleared")
            pool.wait_ge(*S0["setup_scalar"].after(0, "scalars"))
            pool.wait_ge(*S0["setup_vector"].after(0, "head_vectors"))
            g.memset(num[:, 0, :], 1.0)
            g.memset(aggr[:, :, :], 1.0)
            g.memset(smA[:, :, :], 1.0)
            S.done(g.memset(vtok[:, :, P:P + 1], 1.0), "mlstm_cleared")

            G, V, Sc, Q = (A_[k] for k in ("mlstm_tensor", "mlstm_vector", "mlstm_scalar", "mlstm_pool"))
            pool.wait_ge(consts_here, 32)
            with pool.Fori(0, NH_A) as i:
                m = mask("causal")
                pool.wait_ge(*Sc.after(i, "decays"))
                g.tensor_tensor(WW[0:C0, 0, 0:C0], WW[0:C0, 0, 0:C0], m[0:C0, 0:C0], ALU.mult)
                Q.done(g.tensor_tensor(WW[:, 1:5, :], WW[:, 1:5, :], m[:, P:2 * P].unsqueeze(1).to_broadcast([P, 4, P]), ALU.mult), "masked")

            G, V, Sc, Q = (C_[k] for k in ("rwkv_tensor", "rwkv_vector", "rwkv_scalar", "rwkv_pool"))
            with pool.Fori(0, NP_C) as i:
                pool.wait_ge(*G.after(i, "yk1_"))
                each = ident.unsqueeze(1).to_broadcast([P, 10, P])
                g.tensor_tensor(DD1[:, :, :], each, each, ALU.mult)
                Q.done(g.tensor_copy(DDT[:, :, :], ident.unsqueeze(1).to_broadcast([P, 10, P])), "unit_blocks")

            G, V, Sc, Q = (B_[k] for k in ("hgrn_tensor", "hgrn_vector", "hgrn_scalar", "hgrn_pool"))
            with pool.Fori(0, NH_B) as i:
                for lv in range(1, LEVELS + 1):
                    pool.wait_ge(*V.after(i, f"masked{lv}"))
                    if lv > 1:
                        pool.wait_ge(*Q.after(i, f"add{lv - 1}"))
                    g.tensor_tensor(PS[0:C0, 0, 0:C0], PS[0:C0, 0, 0:C0], PT[lv % 2][0:C0, 0, 0:C0], ALU.add)
                    Q.done(g.tensor_tensor(PS[:, 1:5, :], PS[:, 1:5, :], PT[lv % 2][:, 1:5, :], ALU.add), f"add{lv}" if lv < LEVELS else "summed")


_OUTS = [
    ("y_prompt", (1, NP, D)), ("y_sample", (1, NS, D)),
    ("c_p", (1, 1, 8, P, P)), ("n_p", (1, 1, 8, P)), ("m_p", (1, 1, 8)), ("hs_p", (1, 1, 4, P, P)),
    ("rs_p", (1, 1, 8, 64, 64)), ("sh_p", (1, 1, 1, 2176)),
    ("c_s", (1, 1, 8, P, P)), ("n_s", (1, 1, 8, P)), ("m_s", (1, 1, 8)), ("hs_s", (1, 1, 4, P, P)),
    ("rs_s", (1, 1, 8, 64, 64)), ("sh_s", (1, 1, 1, 2176)),
]


def _columns():
    aq, ak, av, ao, az = 0, 1024, 2048, 3088, 4112
    b, c, g = 5136, 7184, 9360
    at, gate = [None, c + 1536], 0
    for i in range(NH_A):
        at += [x + P * i for x in (ak, av, aq, ao, az)]
        at += [g + P * (gate + k) for k in range(A_GATES)]
        gate += A_GATES
    for i in range(NP_C):
        at += [c + x + P * i for x in (512, 0, 1024, 1664)]
        at += [g + P * (gate + k) for k in range(C_GATES)]
        gate += C_GATES
    for i in range(NH_B):
        at += [b + x + P * i for x in (512, 0, 1024, 1536)]
        at += [g + P * (gate + k) for k in range(B_GATES)]
        gate += B_GATES
    assert len(at) == PROJ_AT and gate == 3 * KT
    return at


def _tile(w, at):
    return w[:, at:at + P].reshape(KT, P, P).transpose(1, 0, 2).reshape(P, D)


def kernel(**inputs):
    import concourse.bacc as _bacc
    from concourse.bass_utils import run_bass_kernel_spmd as _run

    a = {k: np.asarray(v) for k, v in inputs.items()}
    w_in = a["w_in"][0]
    gates = np.zeros((D, P), np.float32)
    gates[:, 0:8] = w_in[:, 3072:3080]
    gates[:, 32:40] = w_in[:, 3080:3088]
    w_proj = np.concatenate([a["w_proj_a"][0], a["w_proj_b"][0], a["w_proj_c"][0]], 0)
    tiles = [_tile(gates, 0) if c is None else _tile(w_in, c) for c in _columns()]
    tiles += [_tile(w_proj, P * j) for j in range(KT)] + [_tile(a["w_out"][0], P * j) for j in range(KT)]

    def cols(x):
        return x.reshape(-1, P).T

    def rows8(x):
        return np.concatenate([x.reshape(8, 1), np.zeros((P - 8, 1), np.float32)], 0)

    mu, cache = cols(a["rwkv_mu"][0]), cols(a["cache_rwkv_shift"][0, 0, 0])
    parts = [cols(a["norm_pre"][0]), cols(a["mlstm_norm"][0]), cols(a["hgrn_lb_logits"][0]), cols(a["hgrn_norm"][0]),
             rows8(a["mlstm_b_i"][0]), rows8(a["mlstm_b_f"][0]), rows8(a["state_mlstm_m"][0, 0]),
             a["state_mlstm_n"][0, 0].T, mu[:, 12:13], cache[:, 12:13]]
    for p in range(NP_C):
        parts += [x[:, t + p:t + p + 1] for x in (mu, cache) for t in (0, 4, 8, 13)]
        parts += [cols(a[k][0])[:, p:p + 1] for k in ("rwkv_w0", "rwkv_a0", "rwkv_k_k", "rwkv_k_a", "rwkv_r_k", "rwkv_gn_g", "rwkv_gn_b")]
        parts += [np.zeros((P, 1), np.float32)]
    ranks = np.concatenate([a["rwkv_w_up"][0], a["rwkv_a_up"][0]], 0)
    arrays = {
        "x_all": np.concatenate([a["x_sample"][0], a["meta_tokens"], a["x_prompt"][0]], 0),
        "w_stream": np.stack(tiles),
        "full_in": FULL,
        "masks_in": MASKS.astype(mybir.dt.np(mybir.dt.bfloat16)),
        "vecs_in": np.ascontiguousarray(np.concatenate(parts, 1)),
        "low_in": np.ascontiguousarray(ranks.reshape(P, NP_C, P).transpose(1, 0, 2)),
        "c0_in": np.ascontiguousarray(a["state_mlstm_C"][0, 0]),
        "hgrn_s0": np.ascontiguousarray(a["state_hgrn_S"][0, 0]),
        "rwkv_s0": np.ascontiguousarray(a["state_rwkv_S"][0, 0]),
        "norm_post": np.ascontiguousarray(a["norm_post"][0]),
    }
    nc = _bacc.Bacc("TRN2", target_bir_lowering=False, num_devices=1)
    args = {k: nc.dram_tensor(f"in_{k}", x.shape, mybir.dt.from_np(x.dtype), kind="ExternalInput").ap() for k, x in arrays.items()}
    outs = {k: nc.dram_tensor(f"out_{k}", s, F32, kind="ExternalOutput").ap() for k, s in _OUTS}
    views = {
        "y_prompt": outs["y_prompt"][0], "y_sample": outs["y_sample"][0],
        **{k: outs[k][0, 0] for k in outs if k[:2] in ("c_", "n_", "hs", "rs")},
        **{k: outs[k][0, 0].rearrange("(h a) -> h a", a=1) for k in ("m_p", "m_s")},
        **{k: outs[k][0, 0, 0].rearrange("(k p) -> k p", p=P) for k in ("sh_p", "sh_s")},
    }
    build(nc, **args, **views)
    r = _run(nc, [{f"in_{k}": x for k, x in arrays.items()}], core_ids=[0])
    return tuple(r.results[0][f"out_{k}"] for k, _ in _OUTS)
```

```python
from contextlib import ExitStack

import numpy as np

import concourse.bass as bass
from concourse import mybir

F32 = mybir.dt.float32
F32R = mybir.dt.float32r
ALU = mybir.AluOpType
ACT = mybir.ActivationFunctionType
AX = mybir.AxisListType

P = 128
D = 2048
KT = D // P
NS, NM, NP = 64, 16, 512
T = NS + NM + NP
HALF = T // 2
C0 = NS + NM
NCH = 5
START = [0] + [C0 + P * c for c in range(4)]
LEN = [C0] + [P] * 4
ENDS = [NS - 1, C0 - 1] + [C0 + P * c - 1 for c in range(1, 5)]
SPLIT = START[3]
EPS = 1e-6
GN_EPS = 64e-5
NH_A, NH_B, NP_C = 8, 4, 4
LEVELS = 7

A_TILES, C_TILES, B_TILES = 8, 8, 6
A_AT = 2
C_AT = A_AT + NH_A * A_TILES
B_AT = C_AT + NP_C * C_TILES
PROJ_AT = B_AT + NH_B * B_TILES
OUT_AT = PROJ_AT + KT
N_TILES = OUT_AT + KT
A_GATES, C_GATES, B_GATES = A_TILES - 5, C_TILES - 4, B_TILES - 4


def psum_col(c):
    return START[c] if c < 3 else 512 + START[c] - SPLIT


def part_col(c):
    return {1: 0, 2: 129, 0: 258, 3: 512, 4: 641}[c]


def level_mask(lv):
    s, t = np.arange(P)[:, None], np.arange(P)[None]
    return ((t >> (lv + 1)) == (s >> (lv + 1))) & ((t >> lv) & 1 == 1) & ((s >> lv) & 1 == 0)


def firsts(lv):
    return np.array([j for j in range(P) if not (j >> lv) & 1])


def seconds(lv):
    return np.array([j for j in range(P) if (j >> lv) & 1])


def constants():
    s, t = np.arange(P)[:, None], np.arange(P)[None]
    apart = (s < NS) == (t < NS)
    full = {"ident": np.eye(P), "blocks": s // 64 == t // 64}
    masks = {
        "causal": np.concatenate([(s <= t) & apart, s <= t], 1),
        "before": np.concatenate([(s < t) & apart, s < t], 1),
        "levels": np.concatenate([level_mask(lv) for lv in range(LEVELS)] + [s == t], 1),
        "down": np.concatenate([level_mask(lv).T[:, firsts(lv)] for lv in range(LEVELS)], 1),
        "up": level_mask(0)[:, seconds(0)],
        "carry": np.tile(~np.isin(np.arange(T), [0, NS] + START[1:]), (P, 1)),
    }
    at = {}
    for group in (full, masks):
        cols = 0
        for name, a in group.items():
            at[name] = (cols, cols + a.shape[1])
            cols += a.shape[1]
    return [np.concatenate(list(g.values()), 1).astype(np.float32) for g in (full, masks)], at


(FULL, MASKS), CONST_AT = constants()

VEC = {"norm_pre": 0, "mlstm_norm": 16, "lb": 24, "hgrn_norm": 28, "b_i": 32, "b_f": 33, "m0": 34,
       "n0": 35, "low_mu": 43, "low_cache": 44, "pair": 45}
PAIR_VECS = 16
MU, CACHE, W0, A0, K_K, K_A, R_K, GN_G, GN_B, KA1 = 0, 4, 8, 9, 10, 11, 12, 13, 14, 15
N_VEC = VEC["pair"] + 4 * PAIR_VECS


class Num:

    def __init__(self, base, per, i, j):
        assert per % 2 == 0
        self.base, self.per, self.i, self.j = base, per, i, j

    def __add__(self, k):
        return self.i * self.per + (self.base + self.j + k)

    def __sub__(self, k):
        return self + -k


def SLOT_OF(n):
    return n % 2 if isinstance(n, int) else (n.base + n.j) % 2


def HALF_OF(n):
    return n // 2 if isinstance(n, int) else HalfOf(n)


class HalfOf:
    def __init__(self, n):
        self.n = n

    def __mul__(self, k):
        return Scaled(self.n, k)


class Scaled:
    def __init__(self, n, k):
        self.n, self.k = n, k

    def __add__(self, c):
        n = self.n
        return n.i * (n.per // 2 * self.k) + ((n.base + n.j) // 2 * self.k + c)


class Steps:

    def __init__(self, sem, names):
        self.sem, self.names, self.next = sem, names.split(), 0
        assert len(set(self.names)) == len(self.names)

    def after(self, i, step):
        return self.sem, i * len(self.names) + (self.names.index(step) + 1)

    def done(self, instruction, step):
        assert self.names[self.next % len(self.names)] == step, step
        self.next += 1
        return instruction.then_inc(self.sem, 1)

STEPS = {
    "setup_vector": """
        ones rows_clear i f f_size log_f b g m_max m m_ends ends low_mixed_step low_mixed low_1 low_2
        low_tanh scalar_args head_vectors""",
    "setup_scalar": """
        f_exp f_log m_rows low_exp low_last rows ends scalars""",
    "setup_tensor": """
        rows_turned ends_everywhere""",
    "setup_pool": """
        zeros cleared mlstm_cleared""",
    "mlstm_vector": """
        scalars head_m n0 v_rows v_weighted decay_args probs state1 state2 state3 state4 states inside
        num den_size stats den den_inv aggr den_inv2 h_var gate1 gate2 gate3 gate h_scale h_unit n_out y""",
    "mlstm_scalar": """
        k_rows decays h_log h_rstd state_out""",
    "mlstm_tensor": """
        k_turned v_turned m_everywhere scores updates inside carried h_turned states_turned""",
    "mlstm_pool": """
        masked""",
    "rwkv_vector": """
        vectors negated streams_apart ranks1 a log_decay log_sums log_decay_sums k_step k kk_raw
        k_factor k_new r_step r bonus_terms end_decays rh kk_floor v_step v kk b kkh bh kh bE kE state0
        bonus z_step z bu0 bu1 uk0 uk1 yb0 yb1 yk0 yk1 low0 inv0 w1 z1 low1 inv1 low2 inv2 z2 low3 inv3
        gate low4 inv4 low5 inv5 low6 inv6 tv u0 state1 u1 state2 u2 state3 u3 state4 u4 state5
        y_centred y_unit y_affine y_bonus y""",
    "rwkv_scalar": """
        rank_exps decay_exps kk_squares kk_log kk_rsqrt kk_rows v_rows bE_rows kE_rows z_exp t0_0 t0_1
        t1_0 t1_1 t2_0 t2_1 t3_0 t3_1 t4_0 t4_1 t5_0 t5_1 t6_0 t6_1 tk out0 out1 out2 out3 out4
        y_squares y_log y_rstd state_out""",
    "rwkv_tensor": """
        ranks kk_lengths bonus_sums kk_turned v_turned bE_turned kE_turned bu0_ bu1_ uk0_ uk1_ yb0_ yb1_
        yk0_ yk1_ uk_v turned0_0 turned0_1 au1 du1 au2 turned1_0 turned1_1 du2 au3 turned2_0 turned2_1
        du3 au4 turned3_0 turned3_1 du4 au5 turned4_0 turned4_1 du5 au6 turned5_0 turned5_1 du6
        turned6_0 turned6_1 solved u_carried0 y_part0 state_part0 u_carried1 state_part1 y_part1
        u_carried2 state_part2 y_part2 u_carried3 state_part3 y_part3 u_carried4 state_part4 y_part4
        y_sums states_turned y_square_sums""",
    "rwkv_pool": """
        unit_blocks""",
    "hgrn_vector": """
        logit logit0 soft_inv softmax bound rest f1 f2 k f3 f log_copy log_sums end_args args0 ends khat
        meta_from_zero scaled0 args1 scaled1 args2 masked0 scaled2 args3 masked1 scaled3 args4 masked2
        scaled4 args5 masked3 scaled5 args6 masked4 scaled6 masked5 no_pairs6 masked6 masked7 state1
        state2 state3 state4 states z1 z2 gate o_unit y""",
    "hgrn_scalar": """
        soft log_f decay_exp end_exp exp0 k_rows v_rows exp1 exp2 exp3 exp4 exp5 exp6 o_sum0 o_sum1
        o_sum2 o_sum3 o_sum4 o_log o_rstd""",
    "hgrn_tensor": """
        k_turned v_turned pairs0 pairs1 pairs2 pairs3 pairs4 pairs5 pairs6 pairs7 updates outputs
        o_turned""",
    "hgrn_pool": """
        add1 add2 add3 add4 add5 add6 summed""",
    "norm_rows_tensor": """
        n_turned""",
    "norm_rows_scalar": """
        n_rows""",
    "shift_vector": """
        columns""",
    "shift_tensor": """
        shift_turned""",
    "shift_scalar": """
        shift_out""",
    "merge_vector": """
        part0_0 part1_0 sum1_0 part2_0 merged0 part0_1 part1_1 sum1_1 part2_1 merged1""",
    "merge_scalar": """
        gates0 gates1""",
    "merge_tensor": """
        proj0_0 proj1_0 proj0_1 proj1_1""",
    "out_vector": """
        rows0 rows1""",
    "out_scalar": """
        squares0 squares1""",
    "out_tensor": """
        turned0 turned1""",
    "out_pool": """
        gains0 gains1""",
}

OUT_DMAS = [2, 1, 1, 1, 1]


def build(nc, x_all, w_stream, full_in, masks_in, vecs_in, low_in, c0_in, hgrn_s0, rwkv_s0, norm_post,
          y_prompt, y_sample, c_p, n_p, m_p, hs_p, rs_p, sh_p, c_s, n_s, m_s, hs_s, rs_s, sh_s):
    ctx = ExitStack()
    with ctx:
        def sb(name, cols, dt=F32, rows=P):
            return ctx.enter_context(nc.sbuf_tensor(name, [rows, cols], dt))

        def sem(name):
            return ctx.enter_context(nc.semaphore(name))

        def steps(name):
            return Steps(sem(name), STEPS[name])

        xh = sb("act_hi", KT * T, F32R)[:, :].rearrange("p (k t) -> p k t", k=KT)
        xl = sb("act_lo", KT * T, F32R)[:, :].rearrange("p (k t) -> p k t", k=KT)
        wraw = sb("w_raw", 2 * D)[:, :].rearrange("p (s n) -> p s n", s=2)
        whi = sb("w_hi", 2 * D, F32R)[:, :].rearrange("p (s n) -> p s n", s=2)
        wlo = sb("w_lo", 2 * D, F32R)[:, :].rearrange("p (s n) -> p s n", s=2)
        full = sb("full", FULL.shape[1])
        masks = sb("masks", MASKS.shape[1], mybir.dt.bfloat16)
        vecs = sb("vecs", N_VEC)
        low = sb("low_acts", T)
        gbuf = [sb(f"gate_out{b}", T) for b in range(2)]
        ybuf = sb("branch_out", T)
        shifts = sb("shift_rows", 34)
        ones8 = sb("ones8", P, rows=8)
        pk_all = sb("mlstm_scalars", 8 * 32)[:, :].rearrange("p (h n) -> p h n", h=8)
        pk = sb("head_scalars", 32)
        small = sb("small", 64)
        low_w = sb("rank_weights", P)
        shpad = sb("shift_columns", 64)
        shrow = low_w
        eends, bend = sb("rwkv_end_decays", 8), sb("hgrn_end_decays", 8)
        bss = sb("o_sums", 10)[:, :].rearrange("p (a b) -> p a b", a=2)
        eps, gn_eps, tenln2 = sb("eps", 1), sb("gn_eps", 1), sb("ten_ln2", 1)
        n_scr = (nc.sbuf_bytes_remaining // 4 - 8) // 8 * 8
        scr = sb("scratch", n_scr)

        acc = [ctx.enter_context(nc.psum_tensor(f"acc{k}", [P, 1024], F32)) for k in range(2)]
        br = [ctx.enter_context(nc.psum_tensor(f"branch{k}", [P, 1024], F32)) for k in range(2)]
        bra, brb = br

        ident = full[:, CONST_AT["ident"][0]:CONST_AT["ident"][1]]
        blocks = full[:, CONST_AT["blocks"][0]:CONST_AT["blocks"][1]]

        def mask(name):
            return masks[:, CONST_AT[name][0]:CONST_AT[name][1]]

        def vec(name, k=0, rows=P):
            return vecs[0:rows, VEC[name] + k:VEC[name] + k + 1]

        graw = nc.dram_tensor("gate_logits", [3 * KT, P, T], F32, kind="Internal").ap()
        yspill = nc.dram_tensor("branch_rows", [KT, P, T], F32, kind="Internal").ap()

        class Carver:
            def __init__(self, at=0):
                self.at = at

            def __call__(self, cols, *shape):
                a, self.at = self.at, self.at + cols
                assert self.at <= n_scr, (self.at, n_scr)
                v = scr[:, a:a + cols]
                if len(shape) == 2:
                    return v.rearrange("p (a b) -> p a b", a=shape[0])
                if len(shape) == 3:
                    return v.rearrange("p (a b c) -> p a b c", a=shape[0], b=shape[1])
                return v

        def halves(bank, n=HALF):
            return bank[:, :].rearrange("p (b n) -> p b n", b=2)[:, :, 0:n]

        def split2(v):
            return v.rearrange("p (b n) -> p b n", b=2)

        def shift_in(act, f, n, dst, tile_done, evac_done):
            act.wait_ge(tile_done, n + 1)
            src = acc[SLOT_OF(n)]
            f(dst[:, 1:NS + 1], src[:, 0:NS], ACT.Copy)
            f(dst[:, NS + 2:HALF + 2], src[:, NS:HALF], ACT.Copy)
            return f(dst[:, HALF + 2:T + 2], src[:, 512:512 + HALF], ACT.Copy).then_inc(evac_done, 1)

        w_here = [sem(f"weights_loaded{k}") for k in range(2)]
        hi_done, lo_done = sem("weights_hi_done"), sem("weights_lo_done")
        tile_done, evac_done = sem("tile_product_done"), sem("tile_evacuated")
        consts_here, masks_here, vecs_here = sem("constants_loaded"), sem("masks_loaded"), sem("vectors_loaded")
        gates_out = [sem(f"gate_rows_stored{b}") for b in range(2)]
        y_out = sem("branch_rows_stored")

        x_here = [sem(f"x_rows_loaded{t}") for t in range(5)]
        x_sums, x_unit = sem("x_sums_done"), sem("unit_diagonals_done")
        x_turned, x_hi, x_lo = sem("x_turned"), sem("x_hi_done"), sem("x_lo_done")
        cv = Carver()
        xt = cv(5 * D, 5, D)
        x_junk = cv(D)
        unit = cv(5 * P, 5, P)
        ROWS = [P] * 4 + [T - 4 * P]
        ring4 = [acc[0], acc[1], bra, brb]

        cv = Carver()
        GI, XF, AB, LF, BC, MR, MT = (cv(T) for _ in range(7))
        RR = cv(T)
        ONES = cv(T)
        LOWP = cv(T + 2)
        LOWD = cv(T + 1)
        TK = cv(5 * 96, 5, 96)
        ME = cv(56, 8, 7)
        EB = cv(56, 8, 7)
        MC = cv(7)
        cv = Carver(6 * T)
        aq, ak, av, aeo, az, aez, agz = (cv(T) for _ in range(7))
        DM = cv(T)
        ktok = cv(5 * 128, 5, 128)
        vtok = cv(5 * 129, 5, 129)
        wsv = cv(5 * 129, 5, 129)
        WW = cv(5 * 128, 5, 128)
        PP = cv(5 * 128, 5, 128)
        AST = cv(7 * 129, 7, 129)
        num = cv(5 * 129, 5, 129)
        hn = cv(5 * 128, 5, 128)
        c_in = cv(128)
        c_out = cv(256, 2, 128)
        stats = cv(30, 5, 6)
        aggr = cv(10, 5, 2)
        smA = cv(40, 8, 5)
        nout = cv(16, 2, 8)
        nrow = cv(128)

        cv = Carver()
        cz, cvv, bon, rh = (cv(T) for _ in range(4))
        x1 = cv.at
        PB = [cv(T + 2), cv(T + 2)]
        DD = cv(T + 1)
        cr, ck, ca, LL, kk, cb, ctmp = (cv(T) for _ in range(7))
        x2 = cv.at
        kkh, bh, kh, bE, kE = (cv(T) for _ in range(5))
        x3 = cv.at
        BM = cv(10 * 128, 10, 128)
        KM = cv(10 * 128, 10, 128)
        kkT, bET, kET, vT = (cv(5 * 128, 5, 128) for _ in range(4))
        RST = cv(7 * 64, 7, 64)
        r_in = pk_all[:, 0:4, :].rearrange("p a b -> p (a b)")
        cv = Carver(x1)
        behind_k = cv(1280, 10, 128)
        AT = cv(1280, 10, 128)
        KTm = cv(1280, 10, 128)
        UU = cv(640, 10, 64)
        VV = cv(640, 10, 64)
        W1 = cv(640, 10, 64)
        assert cv.at <= x2
        TKT = behind_k[:, 0:5, :]
        TV = AT[:, 0:5, :].rearrange("p a b -> p (a b)").rearrange("p (q v) -> p q v", q=10)
        ysb = UU[:, :, :].rearrange("p a b -> p (a b)")[:, 0:T]
        utok = VV[:, 0:2, :]
        r_out = VV[:, 2:4, :].rearrange("p a b -> p (a b)")
        cv = Carver(x2)
        DD1 = cv(1280, 10, 128)
        DDT = cv(1280, 10, 128)
        assert cv.at <= x3
        cv = Carver(x2)
        yc, ysq, yv = cv(T), cv(T), cv(T)
        pv = pk[:, 0:PAIR_VECS + 4]

        cv = Carver()
        bq, bk, bv, bz, bez, bef, bep, AL, qhat, khat, EE = (cv(T) for _ in range(11))
        QK = [cv(T), cv(T)]
        PS = cv(5 * 128, 5, 128)
        PT = [cv(5 * 128, 5, 128) for _ in range(2)]
        khtok = cv(5 * 128, 5, 128)
        vbtok = cv(5 * 128, 5, 128)
        BST = cv(7 * 128, 7, 128)
        on = PT[0]
        lbv = cv(8)
        bjunk = EE[:, 0:P]

        hgrn_end = cv.at
        cv = Carver(n_scr - KT * T)
        YIN = cv(KT * T, KT, T)
        ZF = YIN
        EARLY = (n_scr - hgrn_end) // T
        place = [(k - EARLY) % KT for k in range(KT)]
        cv = Carver()
        gin = cv(6 * T, 2, 3, T)
        gs = cv(3 * T, 3, T)
        mz = [cv(T) for _ in range(3)]
        assert cv.at <= n_scr - KT * T
        cv = Carver()
        YT = cv(5 * D, 5, D)
        zt = [gbuf[0][:, :], gbuf[1][:, :]]
        gain = cv(D)
        xfirst = cv(D)
        sq_junk = cv(5 * P, 5, P)
        xrow = [xfirst, wraw[:, 0, :], wraw[:, 1, :], cv(D), xfirst]
        squares = pk_all[:, 4:8, :].rearrange("p a b -> p (a b)")[:, 0:5 * KT].rearrange("p (t n) -> p t n", t=5)

        state_in, rwkv_in, hgrn_in, states_out = sem("mlstm_state_loaded"), sem("rwkv_state_loaded"), sem("hgrn_state_loaded"), sem("states_stored")
        y_here = [sem(f"branch_rows_loaded{k}") for k in range(3)]
        g_here = [sem(f"gate_rows_loaded{k}") for k in range(2)]
        shift_out = sem("shift_rows_stored")
        y_hi, y_split, z_hi, z_split = sem("branch_hi_done"), sem("branch_split"), sem("merged_hi_done"), sem("merged_split")
        post_here, res_done, r_sums = sem("norm_post_loaded"), sem("y_rows_done"), sem("y_sums_done")
        res_out = [sem(f"y_rows_stored{t}") for t in range(5)]
        res_here = [sem(f"residual_loaded{k}") for k in range(5)]
        S0 = {k: steps(k) for k in ("setup_vector", "setup_scalar", "setup_tensor", "setup_pool")}
        A_ = {k: steps(k) for k in ("mlstm_vector", "mlstm_scalar", "mlstm_tensor", "mlstm_pool")}
        C_ = {k: steps(k) for k in ("rwkv_vector", "rwkv_scalar", "rwkv_tensor", "rwkv_pool")}
        B_ = {k: steps(k) for k in ("hgrn_vector", "hgrn_scalar", "hgrn_tensor", "hgrn_pool")}
        A2 = {k: steps(k) for k in ("norm_rows_tensor", "norm_rows_scalar")}
        E_ = {k: steps(k) for k in ("shift_vector", "shift_tensor", "shift_scalar")}
        P_ = {k: steps(k) for k in ("merge_vector", "merge_scalar", "merge_tensor")}
        O_ = {k: steps(k) for k in ("out_vector", "out_scalar", "out_tensor", "out_pool")}

        block = ctx.enter_context(nc.Block())

        @block.sync
        def _(sp):
            sp.dma_start(vecs[:, :], vecs_in).then_inc(vecs_here, 16)
            for t in range(5):
                sp.dma_start(xt[0:ROWS[t], t, :], x_all[P * t:P * t + ROWS[t], :]).then_inc(x_here[t], 16)
                if t == 0:
                    sp.dma_start(full[:, :], full_in).then_inc(consts_here, 16)
            for n in range(2):
                sp.dma_start(wraw[:, n, :], w_stream[n]).then_inc(w_here[n], 16)
            sp.dma_start(masks[:, :], masks_in).then_inc(masks_here, 16)

            def next_load(n):
                nxt = sp.snap(n + 2) if not isinstance(n, int) else n + 2
                sp.wait_ge(lo_done, n + 1)
                s = SLOT_OF(n)
                if isinstance(nxt, int):
                    src = w_stream[nxt]
                else:
                    src = w_stream[bass.ds(nxt, 1)].rearrange("a p n -> (a p) n")
                sp.dma_start(wraw[:, s, :], src).then_inc(w_here[s], 16)

            for n in range(A_AT):
                next_load(n)
            sp.wait_ge(*S0["setup_scalar"].after(0, "m_rows"))
            sp.dma_start(m_s, MT[0:8, NS - 1:NS]).then_inc(x_here[0], 16)
            sp.dma_start(m_p, MT[0:8, T - 1:T]).then_inc(x_here[0], 16)
            sp.wait_ge(x_here[0], 48)
            sp.wait_ge(*S0["setup_scalar"].after(0, "scalars"))
            sp.wait_ge(*S0["setup_vector"].after(0, "head_vectors"))
            with sp.Fori(0, NH_A) as i:
                for j in range(A_TILES):
                    n = Num(A_AT, A_TILES, i, j)
                    if j == 0:
                        sp.dma_start(c_in[:, :], c0_in[bass.ds(i, 1)].rearrange("a v k -> (a v) k")).then_inc(state_in, 16)
                    next_load(n)
                    if j >= 5:
                        g = j - 5
                        row = sp.snap(i * A_GATES + g)
                        sp.wait_ge(evac_done, n + 1)
                        sp.dma_start(graw[bass.ds(row, 1)].rearrange("a p t -> (a p) t"), gbuf[g % 2][:, :]).then_inc(gates_out[g % 2], 16)
                sp.wait_ge(*A_["mlstm_scalar"].after(i, "state_out"))
                sp.dma_start(c_p[bass.ds(i, 1)].rearrange("a v k -> (a v) k"), c_out[:, 0, :]).then_inc(states_out, 16)
                sp.dma_start(c_s[bass.ds(i, 1)].rearrange("a v k -> (a v) k"), c_out[:, 1, :]).then_inc(states_out, 16)
                sp.wait_ge(*A_["mlstm_vector"].after(i, "y"))
                sp.dma_start(yspill[bass.ds(i, 1)].rearrange("a p t -> (a p) t"), ybuf[:, :]).then_inc(y_out, 16)
            sp.wait_ge(*A2["norm_rows_scalar"].after(0, "n_rows"))
            sp.dma_start(n_p, nrow[0:8, :]).then_inc(states_out, 16)
            sp.dma_start(n_s, nrow[8:16, :]).then_inc(states_out, 16)
            with sp.Fori(0, NP_C) as i:
                for j in range(C_TILES):
                    n = Num(C_AT, C_TILES, i, j)
                    if j == 0:
                        sp.dma_start(low_w[:, :], low_in[bass.ds(i, 1)].rearrange("a p n -> (a p) n")).then_inc(rwkv_in, 16)
                        for h in range(2):
                            hh = sp.snap(i * 2 + h)
                            sp.dma_start(r_in[0:64, 64 * h:64 * h + 64], rwkv_s0[bass.ds(hh, 1)].rearrange("a v k -> (a v) k")).then_inc(rwkv_in, 16)
                    next_load(n)
                    if j >= 4:
                        g = j - 4
                        row = sp.snap(i * C_GATES + (NH_A * A_GATES + g))
                        sp.wait_ge(evac_done, n + 1)
                        sp.dma_start(graw[bass.ds(row, 1)].rearrange("a p t -> (a p) t"), gbuf[g % 2][:, :]).then_inc(gates_out[g % 2], 16)
                sp.wait_ge(*C_["rwkv_scalar"].after(i, "state_out"))
                for h in range(2):
                    hh = sp.snap(i * 2 + h)
                    sp.dma_start(rs_p[bass.ds(hh, 1)].rearrange("a v k -> (a v) k"), r_out[0:64, 64 * h:64 * h + 64]).then_inc(states_out, 16)
                    sp.dma_start(rs_s[bass.ds(hh, 1)].rearrange("a v k -> (a v) k"), r_out[64:128, 64 * h:64 * h + 64]).then_inc(states_out, 16)
                row = sp.snap(i + NH_A)
                sp.wait_ge(*C_["rwkv_vector"].after(i, "y"))
                sp.dma_start(yspill[bass.ds(row, 1)].rearrange("a p t -> (a p) t"), ybuf[:, :]).then_inc(y_out, 16)
            def load_rows(a, b, s):
                sp.dma_start(YIN[:, place[a]:place[a] + b - a, :], yspill[a:b].rearrange("k p t -> p k t")).then_inc(y_here[s], 16)

            load_rows(0, EARLY, 0)
            with sp.Fori(0, NH_B) as i:
                for j in range(B_TILES):
                    n = Num(B_AT, B_TILES, i, j)
                    if j == 0:
                        sp.dma_start(BST[:, 0, :], hgrn_s0[bass.ds(i, 1)].rearrange("a v k -> (a v) k")).then_inc(hgrn_in, 16)
                    next_load(n)
                    if j >= 4:
                        g = j - 4
                        row = sp.snap(i * B_GATES + (NH_A * A_GATES + NP_C * C_GATES + g))
                        sp.wait_ge(evac_done, n + 1)
                        sp.dma_start(graw[bass.ds(row, 1)].rearrange("a p t -> (a p) t"), gbuf[g % 2][:, :]).then_inc(gates_out[g % 2], 16)
                sp.wait_ge(*B_["hgrn_vector"].after(i, "states"))
                sp.dma_start(hs_p[bass.ds(i, 1)].rearrange("a v k -> (a v) k"), BST[:, 5, :]).then_inc(states_out, 16)
                sp.dma_start(hs_s[bass.ds(i, 1)].rearrange("a v k -> (a v) k"), BST[:, 6, :]).then_inc(states_out, 16)
                row = sp.snap(i + NH_A + NP_C)
                sp.wait_ge(*B_["hgrn_vector"].after(i, "y"))
                sp.dma_start(yspill[bass.ds(row, 1)].rearrange("a p t -> (a p) t"), ybuf[:, :]).then_inc(y_out, 16)
            load_rows(EARLY, NH_A + NP_C, 1)
            sp.wait_ge(y_out, 16 * KT)
            load_rows(NH_A + NP_C, KT, 2)
            sp.wait_ge(states_out, 16 * (2 * NH_A + 2 + 4 * NP_C + 2 * NH_B))
            sp.wait_ge(gates_out[0], 16 * (2 * NH_A + 2 * NP_C + NH_B))
            sp.wait_ge(gates_out[1], 16 * (NH_A + 2 * NP_C + NH_B))

            def load_gates(j, s):
                for b, gate in enumerate((0, 2, 1)):
                    row = sp.snap(j + KT * gate) if not isinstance(j, int) else j + KT * gate
                    sp.dma_start(gin[:, s, b, :], graw[bass.ds(row, 1)].rearrange("a p t -> (a p) t")).then_inc(g_here[s], 16)
            load_gates(0, 0)
            load_gates(1, 1)
            with sp.Fori(0, KT // 2 - 1) as i:
                for j in range(2):
                    next_load(Num(PROJ_AT, 2, i, j))
                    jj = sp.snap(i * 2 + (j + 2))
                    sp.wait_ge(*P_["merge_scalar"].after(i, f"gates{j}"))
                    load_gates(jj, j)
            for n in range(PROJ_AT + KT - 2, PROJ_AT + KT):
                next_load(n)
            sp.wait_ge(*E_["shift_scalar"].after(0, "shift_out"))
            sp.dma_start(sh_s, shrow[0:17, :]).then_inc(shift_out, 16)
            sp.dma_start(sh_p, shrow[32:49, :]).then_inc(shift_out, 16)
            sp.wait_ge(z_split, KT)
            sp.dma_start(gain, norm_post.partition_broadcast(P)).then_inc(post_here, 16)
            for t in (0, 3):
                sp.dma_start(xrow[t][0:P, :], x_all[P * t:P * t + P, :]).then_inc(res_here[t], 16)
            with sp.Fori(0, KT // 2 - 1) as i:
                for j in range(2):
                    next_load(Num(OUT_AT, 2, i, j))
            sp.wait_ge(lo_done, N_TILES)
            for t in range(5):
                if t == 0:
                    for u in range(1, 3):
                        sp.dma_start(xrow[u][0:ROWS[u], :], x_all[P * u:P * u + ROWS[u], :]).then_inc(res_here[u], 16)
                sp.wait_ge(res_done, t + 1)
                a, b = P * t, P * t + ROWS[t]
                if a < NS:
                    sp.dma_start(y_sample, xrow[t][0:NS, :]).then_inc(res_out[t], 16)
                lo = max(a, C0)
                sp.dma_start(y_prompt[lo - C0:b - C0, :], xrow[t][lo - a:b - a, :]).then_inc(res_out[t], 16)
                if t == 0:
                    sp.wait_ge(res_out[t], 16 * OUT_DMAS[t])
                    sp.dma_start(xrow[4][0:ROWS[4], :], x_all[4 * P:T, :]).then_inc(res_here[4], 16)
            for t in range(1, 5):
                sp.wait_ge(res_out[t], 16 * OUT_DMAS[t])
            sp.wait_ge(shift_out, 32)

        @block.tensor
        def _(pe):
            mm = nc.tensor.matmul
            turn = nc.tensor.transpose

            def product(n, stages=None, first=False, unevacuated=0):
                s = SLOT_OF(n)
                stages = stages or {}
                pe.wait_ge(lo_done, n + 1)
                if not first:
                    pe.wait_ge(evac_done, n - (1 + unevacuated))
                for k in range(KT):
                    for stage in stages.get(k, ()):
                        stage()
                    w = slice(P * k, P * k + P)
                    for a, b in ((whi, xh), (whi, xl), (wlo, xh)):
                        for h in range(2):
                            last = mm(acc[s][:, 512 * h:512 * h + HALF], a[:, s, w], b[:, k, HALF * h:HALF * h + HALF],
                                      start=(k == 0 and a is whi and b is xh), stop=(k == KT - 1 and a is wlo))
                last.then_inc(tile_done, 1)

            def products(tiles, stages):
                for m, n in enumerate(tiles):
                    at = {}
                    for block, stage in stages:
                        if block // KT == m:
                            at.setdefault(block % KT, []).append(stage)
                    product(n, at)
                for block, stage in stages:
                    if block >= KT * len(tiles):
                        stage()

            for k in range(KT):
                if k >= 4:
                    pe.wait_ge(x_lo, k - 3)
                for t in range(5):
                    if k == 0:
                        pe.wait_ge(x_unit, t + 1)
                    last = mm(ring4[k % 4][:, P * t:P * t + ROWS[t]], xt[0:ROWS[t], t, P * k:P * k + P], unit[0:ROWS[t], t, 0:ROWS[t]], start=True, stop=True)
                last.then_inc(x_turned, 1)
            product(0, {k: [lambda k=k: pe.wait_ge(x_lo, max(k, 12) + 1)] for k in range(0, KT)}, first=True)
            product(1, first=True)
            pt, vt, at = S0["setup_tensor"], S0["setup_vector"], S0["setup_scalar"]
            pe.wait_ge(*at.after(0, "m_rows"))
            for c in range(NCH):
                last = turn(bra[0:LEN[c], 96 * c:96 * c + 96], RR[0:96, START[c]:START[c] + LEN[c]], ident[0:96, 0:96])
            pt.done(last, "rows_turned")
            pe.wait_ge(*vt.after(0, "ends"))
            pt.done(mm(brb[:, 0:56], ones8[:, :], ME[0:8, :, :].rearrange("p a b -> p (a b)"), start=True, stop=True), "ends_everywhere")

            pt, vt, at, gt = (A_[k] for k in ("mlstm_tensor", "mlstm_vector", "mlstm_scalar", "mlstm_pool"))
            with pe.Fori(0, NH_A) as i:
                def N(j):
                    return Num(A_AT, A_TILES, i, j)

                def turn_kv():
                    pe.wait_ge(evac_done, N(1) + 1)
                    for c in range(NCH):
                        last = turn(bra[0:LEN[c], P * c:P * c + P], ak[:, START[c]:START[c] + LEN[c]], ident)
                    pe.wait_ge(state_in, 16 * i + 16)
                    last = turn(bra[:, 640:768], c_in[:, :], ident)
                    pt.done(last, "k_turned")
                    for c in range(NCH):
                        last = turn(brb[0:LEN[c], P * c:P * c + P], av[:, START[c]:START[c] + LEN[c]], ident)
                    pt.done(last, "v_turned")

                def scores():
                    pe.wait_ge(*at.after(i, "k_rows"))
                    pe.wait_ge(*vt.after(i, "head_m"))
                    mm(bra[:, 0:SPLIT], ones8[:, :], DM[0:8, 0:SPLIT], start=True, stop=True)
                    pt.done(mm(bra[:, 512:512 + T - SPLIT], ones8[:, :], DM[0:8, SPLIT:T], start=True, stop=True), "m_everywhere")
                    pe.wait_ge(*vt.after(i, "v_rows"))
                    pe.wait_ge(evac_done, N(2) + 1)
                    for c in range(NCH):
                        tok = slice(START[c], START[c] + LEN[c])
                        last = mm(brb[0:LEN[c], P * c:P * c + LEN[c]], ak[:, tok], aq[:, tok], start=True, stop=True)
                    pt.done(last, "scores")

                def values():
                    pe.wait_ge(*vt.after(i, "decay_args"))
                    pe.wait_ge(*vt.after(i, "v_weighted"))
                    pe.wait_ge(*at.after(i, "k_rows"))
                    mm(bra[:, 0:129], ktok[0:NS, 0, :], wsv[0:NS, 0, :], start=True, stop=True)
                    for c in range(1, NCH):
                        o = {1: 258, 2: 512, 3: 641, 4: 770}[c]
                        last = mm(bra[:, o:o + 129], ktok[:, c, :], wsv[:, c, :], start=True, stop=True)
                    last = mm(bra[:, 129:258], ktok[NS:C0, 0, :], wsv[NS:C0, 0, :], start=True, stop=True)
                    pt.done(last, "updates")
                    pe.wait_ge(*vt.after(i, "probs"))
                    for c in range(NCH):
                        o = part_col(c)
                        last = mm(brb[0:LEN[c], o:o + 129], PP[0:LEN[c], c, 0:LEN[c]], vtok[0:LEN[c], c, :], start=True, stop=True)
                    pt.done(last, "inside")

                def carried():
                    pe.wait_ge(*vt.after(i, "states"))
                    for c in range(NCH):
                        o, n = part_col(c), (NS if c == 0 else P)
                        last = mm(bra[0:n, o:o + 129], aq[:, START[c]:START[c] + n], AST[:, c, :], start=True, stop=True)
                    pt.done(last, "carried")

                def turn_h():
                    pe.wait_ge(*vt.after(i, "h_unit"))
                    for c in range(NCH):
                        o = psum_col(c)
                        last = turn(brb[:, o:o + LEN[c]], hn[0:LEN[c], c, :], ident[0:LEN[c], 0:LEN[c]])
                    pt.done(last, "h_turned")
                    for m in range(2):
                        last = turn(bra[:, P * m:P * m + P], AST[:, 5 + m, 0:P], ident)
                    pt.done(last, "states_turned")

                product(N(0))
                product(N(1))
                product(N(2))
                turn_kv()
                product(N(3))
                scores()
                product(N(4))
                values()
                product(N(5))
                carried()
                product(N(6))
                product(N(7), {5: [turn_h]})
                pe.wait_ge(*vt.after(i, "y"))
                pe.wait_ge(*at.after(i, "state_out"))
            A2["norm_rows_tensor"].done(turn(bra[0:16, 0:P], nout[:, :, :].rearrange("p a b -> p (a b)"), ident), "n_turned")

            pt, vt, at, gt = (C_[k] for k in ("rwkv_tensor", "rwkv_vector", "rwkv_scalar", "rwkv_pool"))
            with pe.Fori(0, NP_C) as i:
                def N(j):
                    return Num(C_AT, C_TILES, i, j)

                def ranks():
                    pe.wait_ge(rwkv_in, 48 * i + 48)
                    pe.wait_ge(states_out, 64 * i + 16 * (2 * NH_A + 2))
                    pe.wait_ge(y_out, 16 * i + 16 * NH_A)
                    for h in range(2):
                        mm(bra[:, 512 * h:512 * h + HALF], low_w[0:64, :], low[0:64, HALF * h:HALF * h + HALF], start=True, stop=True)
                    for h in range(2):
                        last = mm(brb[:, 512 * h:512 * h + HALF], low_w[64:128, :], low[64:128, HALF * h:HALF * h + HALF], start=True, stop=True)
                    pt.done(last, "ranks")

                def lengths():
                    pe.wait_ge(*at.after(i, "kk_squares"))
                    for h in range(2):
                        last = mm(bra[:, 512 * h:512 * h + HALF], blocks, ctmp[:, HALF * h:HALF * h + HALF], start=True, stop=True)
                    pt.done(last, "kk_lengths")

                def bonus():
                    pe.wait_ge(*vt.after(i, "bonus_terms"))
                    for h in range(2):
                        mm(brb[:, 512 * h:512 * h + HALF], blocks, bon[:, HALF * h:HALF * h + HALF], start=True, stop=True)
                    last = turn(brb[:, 896:960], r_in[0:64, :], ident[0:64, 0:64])
                    pt.done(last, "bonus_sums")

                def turn_to_rows(src, bank, step, ready):
                    pe.wait_ge(*vt.after(i, ready))
                    for c in range(NCH):
                        last = turn(bank[0:LEN[c], P * c:P * c + P], src[:, START[c]:START[c] + LEN[c]], ident)
                    pt.done(last, step)

                def pairs(lhs, rhs, h, bank, step, free):
                    if step in ("bu0_", "bu1_"):
                        pe.wait_ge(*vt.after(i, "kE"))
                    pe.wait_ge(*free)
                    r = slice(64 * h, 64 * h + 64)
                    for c in range(NCH):
                        tok = slice(START[c], START[c] + LEN[c])
                        last = mm(bank[0:LEN[c], P * c:P * c + LEN[c]], lhs[r, tok], rhs[r, tok], start=True, stop=True)
                    pt.done(last, step)

                def join(lv, lhs, rhs, step):
                    n0 = (C0 if lv < 4 else NS) if lv < 6 else 0
                    for q in (1, 2, 3, 4, 6, 7, 8, 9, 0, 5):
                        n = P if q % 5 else n0
                        if n:
                            last = mm(bra[0:n, 64 * q:64 * q + n // 2], lhs[0:n, q, 0:n], rhs(q, n), start=True, stop=True)
                    pt.done(last, step)

                def level_a_d(lv):
                    pe.wait_ge(*vt.after(i, f"inv{lv - 1}"))
                    if lv == 1:
                        pe.wait_ge(*vt.after(i, "w1"))
                        pe.wait_ge(*at.after(i, "t0_1"))
                    join(lv, AT, lambda q, n: DD1[0:n, q, 0:n].rearrange("p (b two w) -> p b two w", two=2, w=1 << lv)[:, :, 0, :], f"au{lv}")

                def level_d_a_d(lv):
                    pe.wait_ge(*vt.after(i, f"low{lv}"))
                    if lv > 1:
                        pe.wait_ge(*at.after(i, f"t{lv - 1}_1"))
                    join(lv, DDT, lambda q, n: UU[0:n, q, 0:n // 2], f"du{lv}")

                def turn_level(lv, h):
                    if h:
                        pe.wait_ge(*at.after(i, f"t{lv}_0"))
                    elif lv > 1:
                        pe.wait_ge(*at.after(i, f"t{lv - 1}_1"))
                    pe.wait_ge(*vt.after(i, f"inv{lv}"))
                    src = DD1 if lv else DDT
                    for c in (1, 2, 3, 4, 0):
                        n = LEN[c]
                        last = turn(brb[0:n, P * c:P * c + n], src[0:n, 5 * h + c, 0:n], ident[0:n, 0:n])
                    pt.done(last, f"turned{lv}_{h}")

                def w1():
                    pe.wait_ge(*vt.after(i, "yk0"))
                    pe.wait_ge(*at.after(i, "v_rows"))
                    for q in range(10):
                        c, h = q % 5, q // 5
                        last = mm(bra[0:LEN[c], 64 * q:64 * q + 64], KTm[0:LEN[c], q, 0:LEN[c]], vT[0:LEN[c], c, 64 * h:64 * h + 64], start=True, stop=True)
                    pt.done(last, "uk_v")

                def solved():
                    pe.wait_ge(*at.after(i, "t6_1"))
                    for q in range(10):
                        c, h = q % 5, q // 5
                        mm(bra[0:LEN[c], 64 * q:64 * q + 64], DDT[0:LEN[c], q, 0:LEN[c]], W1[0:LEN[c], q, :], start=True, stop=True)
                    for q in range(10):
                        c, h = q % 5, q // 5
                        last = mm(brb[64 * h:64 * h + 64, P * c:P * c + LEN[c]], kkT[0:LEN[c], c, 64 * h:64 * h + 64], DDT[0:LEN[c], q, 0:LEN[c]], start=True, stop=True)
                    pt.done(last, "solved")

                def from_state(c):
                    pe.wait_ge(*vt.after(i, "tv" if c == 0 else f"state{c}"))
                    pe.wait_ge(*at.after(i, "tk"))
                    n = LEN[c]
                    for h in range(2):
                        r = slice(64 * h, 64 * h + 64)
                        last = mm(bra[0:n, 512 * h:512 * h + 64], TKT[r, c, 0:n], RST[r, c, :], start=True, stop=True)
                    pt.done(last, f"u_carried{c}")

                def to_state(c):
                    ut = utok.rearrange("p a b -> p (a b)")
                    heads = [slice(0, 64), slice(64, 128)]

                    def end_state():
                        for r in heads:
                            if c == 0:
                                mm(brb[r, 512:576], bET[0:NS, c, r], ut[0:NS, r], start=True, stop=False)
                                mm(brb[r, 512:576], kET[0:NS, c, r], vT[0:NS, c, r], start=False, stop=True)
                                mm(bra[r, 256:320], bET[NS:C0, c, r], ut[NS:C0, r], start=True, stop=False)
                                last = mm(bra[r, 256:320], kET[NS:C0, c, r], vT[NS:C0, c, r], start=False, stop=True)
                            else:
                                mm(brb[r, 512:576], bET[:, c, r], ut[:, r], start=True, stop=False)
                                last = mm(brb[r, 512:576], kET[:, c, r], vT[:, c, r], start=False, stop=True)
                        pt.done(last, f"state_part{c}")

                    def output():
                        L, n = LEN[c], (NS if c == 0 else P)
                        for h, r in enumerate(heads):
                            mm(brb[r, 0:L], vT[0:L, c, r], KM[0:L, 5 * h + c, 0:L], start=True, stop=False)
                            mm(brb[r, 0:L], ut[0:L, r], BM[0:L, 5 * h + c, 0:L], start=False, stop=False)
                            last = mm(brb[r, 0:n], RST[r, c, :], rh[r, START[c]:START[c] + n], start=False, stop=True)
                        pt.done(last, f"y_part{c}")

                    pe.wait_ge(*vt.after(i, f"u{c}"))
                    if c == 0:
                        output()
                        end_state()
                    else:
                        end_state()
                        pe.wait_ge(*at.after(i, f"out{c - 1}"))
                        output()

                def means():
                    pe.wait_ge(*at.after(i, "out4"))
                    for h in range(2):
                        last = mm(bra[:, 512 * h:512 * h + HALF], blocks, ysb[:, HALF * h:HALF * h + HALF], start=True, stop=True)
                    pt.done(last, "y_sums")

                def variances():
                    pe.wait_ge(*at.after(i, "y_squares"))
                    for h in range(2):
                        last = mm(brb[:, 512 * h:512 * h + HALF], blocks, ysq[:, HALF * h:HALF * h + HALF], start=True, stop=True)
                    pt.done(last, "y_square_sums")

                def turn_states():
                    pe.wait_ge(*vt.after(i, "y_centred"))
                    pt.done(turn(bra[:, 0:P], RST[:, 5:7, :].rearrange("p a b -> p (a b)"), ident), "states_turned")

                product(N(0))
                ranks()
                product(N(1))
                product(N(2), {14: [lengths]})
                product(N(3))
                bonus()
                turn_to_rows(kkh, bra, "kk_turned", "kkh")

                def turned_again(ready, src, bank, step, when):
                    pe.wait_ge(*at.after(i, ready))
                    turn_to_rows(src, bank, step, when)

                plan = [
                    (1, lambda: turn_to_rows(cvv, brb, "v_turned", "bonus")),
                    (2, lambda: turned_again("kk_rows", bE, bra, "bE_turned", "bE")),
                    (3, lambda: turned_again("v_rows", kE, brb, "kE_turned", "kE")),
                ]
                block, free = 3, (at.after(i, "bE_rows"), at.after(i, "kE_rows"))
                for name, lhs, rhs in (("bu", bh, kkh), ("uk", kh, kkh), ("yb", bh, rh), ("yk", kh, rh)):
                    for h in range(2):
                        block += 1
                        plan.append((block, lambda name=name, lhs=lhs, rhs=rhs, h=h, free=free: pairs(lhs, rhs, h, br[h], f"{name}{h}_", free[h])))
                    free = (vt.after(i, name + "0"), vt.after(i, name + "1"))
                plan += [(block + 2, w1), (block + 4, lambda: turn_level(0, 0)), (block + 5, lambda: turn_level(0, 1))]
                block += 7
                for lv in range(1, LEVELS):
                    plan.append((block, lambda lv=lv: level_a_d(lv)))
                    if lv > 1:
                        plan += [(block, lambda lv=lv: turn_level(lv - 1, 0)), (block + 1, lambda lv=lv: turn_level(lv - 1, 1))]
                    plan.append((block + 2, lambda lv=lv: level_d_a_d(lv)))
                    block += 4
                plan += [(block, lambda: turn_level(6, 0)), (block + 1, lambda: turn_level(6, 1)), (block + 3, solved)]
                block += 4
                for c in range(NCH):
                    plan += [(block, lambda c=c: from_state(c)), (block + 1, lambda c=c: to_state(c))]
                    block += 2
                plan += [(block + 1, means), (block + 2, turn_states), (block + 5, variances)]
                assert block + 5 <= 4 * KT
                products([N(4), N(5), N(6), N(7)], plan)

            pt, vt, at, gt = (B_[k] for k in ("hgrn_tensor", "hgrn_vector", "hgrn_scalar", "hgrn_pool"))
            with pe.Fori(0, NH_B) as i:
                def N(j):
                    return Num(B_AT, B_TILES, i, j)

                def turn_rows(src, bank, step):
                    for c in range(NCH):
                        last = turn(bank[0:LEN[c], P * c:P * c + P], src[:, START[c]:START[c] + LEN[c]], ident)
                    pt.done(last, step)

                def level_pairs(lv):
                    bank = br[lv % 2]
                    pe.wait_ge(*vt.after(i, f"scaled{lv}" if lv < LEVELS else "k"))
                    if lv >= 2:
                        pe.wait_ge(*vt.after(i, f"masked{lv - 2}"))
                    elif lv == 0:
                        pe.wait_ge(*at.after(i, "k_rows"))
                    else:
                        pe.wait_ge(*at.after(i, "v_rows"))
                    for c in range(NCH):
                        tok = slice(START[c], START[c] + LEN[c])
                        if lv == 6 and c == 0:
                            continue
                        a, b = (QK[lv % 2], QK[lv % 2]) if lv < LEVELS else (bk, bq)
                        last = mm(bank[0:LEN[c], P * c:P * c + LEN[c]], a[:, tok], b[:, tok], start=True, stop=True)
                    pt.done(last, f"pairs{lv}")

                def updates():
                    pe.wait_ge(*vt.after(i, f"masked{LEVELS - 1}"))
                    pe.wait_ge(*at.after(i, "v_rows"))
                    mm(bra[:, 0:P], khtok[0:NS, 0, :], vbtok[0:NS, 0, :], start=True, stop=True)
                    for c in range(1, NCH):
                        last = mm(bra[:, P * c + P:P * c + 2 * P], khtok[:, c, :], vbtok[:, c, :], start=True, stop=True)
                    last = mm(bra[:, P:2 * P], khtok[NS:C0, 0, :], vbtok[NS:C0, 0, :], start=True, stop=True)
                    pt.done(last, "updates")

                def outputs():
                    pe.wait_ge(*gt.after(i, "summed"))
                    pe.wait_ge(*vt.after(i, "states"))
                    pe.wait_ge(hgrn_in, 16 * i + 16)
                    pe.wait_ge(*vt.after(i, f"masked{LEVELS}"))
                    for c in range(NCH):
                        n = LEN[c]
                        mm(brb[0:n, P * c:P * c + P], PS[0:n, c, 0:n], vbtok[0:n, c, :], start=True, stop=False)
                        last = mm(brb[0:n, P * c:P * c + P], qhat[:, START[c]:START[c] + n], BST[:, c, :], start=False, stop=True)
                    pt.done(last, "outputs")

                def turn_o():
                    pe.wait_ge(*vt.after(i, "o_unit"))
                    for c in range(NCH):
                        o = psum_col(c)
                        last = turn(bra[:, o:o + LEN[c]], on[0:LEN[c], c, :], ident[0:LEN[c], 0:LEN[c]])
                    pt.done(last, "o_turned")

                def turn_k():
                    pe.wait_ge(*vt.after(i, "khat"))
                    turn_rows(khat, bra, "k_turned")

                def turn_v():
                    pe.wait_ge(evac_done, N(2) + 1)
                    turn_rows(bv, brb, "v_turned")

                for j in range(3):
                    product(N(j))
                products([N(3), N(4), N(5)],
                         [(14, turn_k), (15, turn_v)]
                         + [(at, lambda lv=lv: level_pairs(lv)) for lv, at in enumerate((19, 21, 23, 26, 28, 30, 32, 34))]
                         + [(36, updates), (39, outputs), (46, turn_o)])
            pe.wait_ge(*E_["shift_vector"].after(0, "columns"))
            E_["shift_tensor"].done(turn(brb[0:64, 0:P], shpad[:, :], ident), "shift_turned")

            pt, vt, at = P_["merge_tensor"], P_["merge_vector"], P_["merge_scalar"]
            banks3 = [acc[0], acc[1], bra]
            RANGES = [range(0, 8), range(8, 12), range(12, 16)]

            with pe.Fori(0, KT // 2) as i:
                for j in range(2):
                    n = Num(PROJ_AT, 2, i, j)
                    s = SLOT_OF(n)
                    pe.wait_ge(lo_done, n + 1)
                    for b in range(3):
                        if j:
                            pe.wait_ge(*vt.after(i, f"part{b}_0"))
                        elif b == 2:
                            pe.wait_ge(*vt.after(i, "part0_0"))
                        ks = RANGES[b]
                        for k in ks:
                            if j == 0:
                                pe.wait_ge(y_split, k + 1)
                            w = slice(P * k, P * k + P)
                            for x, y in ((whi, xh), (whi, xl), (wlo, xh)):
                                for h in range(2):
                                    last = mm(banks3[b][:, 512 * h:512 * h + HALF], x[:, s, w], y[:, k, HALF * h:HALF * h + HALF],
                                              start=(k == ks[0] and x is whi and y is xh), stop=(k == ks[-1] and x is wlo))
                        if b == 2:
                            last.then_inc(tile_done, 1)
                        else:
                            pt.done(last, f"proj{b}_{j}")
                pe.wait_ge(*vt.after(i, "part1_1"))

            pt, vt, at = O_["out_tensor"], O_["out_vector"], O_["out_scalar"]

            def turn_out(i, j):
                pe.wait_ge(evac_done, Num(OUT_AT, 2, i, j) + (1 - KT))
                for t in range(5):
                    last = turn(br[j][0:ROWS[t], P * t:P * t + P], zt[j][:, P * t:P * t + ROWS[t]], ident)
                pt.done(last, f"turned{j}")

            product(OUT_AT, {k: [lambda k=k: pe.wait_ge(z_split, k + 1)] for k in range(KT)}, unevacuated=KT)
            with pe.Fori(0, KT // 2 - 1) as i:
                product(Num(OUT_AT, 2, i, 1), {3: [lambda: turn_out(i, 0)]}, unevacuated=KT)
                product(Num(OUT_AT, 2, i, 2), {3: [lambda: turn_out(i, 1)]}, unevacuated=KT)
                pe.wait_ge(*vt.after(i, "rows1"))
            product(N_TILES - 1, {3: [lambda: turn_out(KT // 2 - 1, 0)]}, unevacuated=KT)
            turn_out(KT // 2 - 1, 1)

        @block.scalar
        def _(act):
            f = nc.scalar.activation

            def split_hi(m, first=False):
                s = SLOT_OF(m)
                act.wait_ge(w_here[s], HALF_OF(m) * 16 + 16)
                if not first:
                    act.wait_ge(tile_done, m - 1)
                f(whi[:, s, :], wraw[:, s, :], ACT.Copy).then_inc(hi_done, 1)

            def source(n):
                act.wait_ge(tile_done, n + 1)
                return halves(acc[SLOT_OF(n)])

            def plain(n, dst, scale=1.0):
                f(split2(dst), source(n), ACT.Copy, scale=scale).then_inc(evac_done, 1)

            S = S0["setup_scalar"]
            act.wait_ge(vecs_here, 16)
            act.wait_ge(*S0["setup_pool"].after(0, "zeros"))
            for t in range(5):
                r = ROWS[t]
                act.wait_ge(x_here[t], 16)
                if t:
                    act.wait_ge(x_sums, t)
                f(x_junk[0:r, :], xt[0:r, t, :], ACT.Square, accum_out=small[0:r, t:t + 1]).then_inc(x_sums, 1)
            act.wait_ge(x_sums, 5)
            f(small[:, 8:13], small[:, 0:5], ACT.Ln, scale=1.0 / D, bias=eps[:, 0:1]).then_inc(x_sums, 1)
            act.wait_ge(x_sums, 6)
            f(small[:, 16:21], small[:, 8:13], ACT.Exp, scale=-0.5).then_inc(x_sums, 1)
            split_hi(0, first=True)
            split_hi(1, first=True)
            for k in range(KT):
                act.wait_ge(x_turned, k + 1)
                f(xh[:, k, :], ring4[k % 4][:, 0:T], ACT.Copy, scale=vec("norm_pre", k)).then_inc(x_hi, 1)
            split_hi(2)
            act.wait_ge(tile_done, 1)
            f(split2(GI[0:8, :]), halves(acc[0])[0:8], ACT.Copy)
            f(split2(XF[0:8, :]), halves(acc[0])[32:40], ACT.Copy).then_inc(evac_done, 1)
            V = S0["setup_vector"]
            act.wait_ge(*V.after(0, "f_size"))
            S.done(f(AB[0:8, :], AB[0:8, :], ACT.Exp, scale=-1.0), "f_exp")
            act.wait_ge(*S.after(0, "f_exp"))
            S.done(f(AB[0:8, :], AB[0:8, :], ACT.Ln, bias=1.0), "f_log")
            act.wait_ge(*V.after(0, "m"))
            f(RR[0:8, :], GI[0:8, :], ACT.Copy)
            f(RR[32:40, :], MR[0:8, :], ACT.Copy)
            S.done(f(RR[64:72, :], MT[0:8, :], ACT.Copy), "m_rows")
            shift_in(act, f, 1, LOWP, tile_done, evac_done)
            act.wait_ge(*V.after(0, "low_mixed"))
            S.done(f(low[0:64, :], low[0:64, :], ACT.Exp, scale=2.0), "low_exp")
            S.done(f(shifts[:, 32:34], LOWP[:, 64:T + 2:T + 1 - 64], ACT.Copy), "low_last")
            act.wait_ge(*S0["setup_pool"].after(0, "cleared"))
            act.wait_ge(*S0["setup_tensor"].after(0, "rows_turned"))
            f(TK[0:C0, 0, :], bra[0:C0, 0:96], ACT.Copy)
            S.done(f(TK[:, 1:5, :].rearrange("p a b -> p (a b)"), bra[:, 96:480], ACT.Copy), "rows")
            act.wait_ge(*S0["setup_tensor"].after(0, "ends_everywhere"))
            S.done(f(EB[:, :, :].rearrange("p a b -> p (a b)"), brb[:, 0:56], ACT.Copy), "ends")
            act.wait_ge(*V.after(0, "scalar_args"))
            S.done(f(pk_all[:, :, 5:25], pk_all[:, :, 5:25], ACT.Exp), "scalars")

            G, V, S, Q = (A_[k] for k in ("mlstm_tensor", "mlstm_vector", "mlstm_scalar", "mlstm_pool"))
            act.wait_ge(x_here[0], 48)
            with act.Fori(0, NH_A) as i:
                def N(j):
                    return Num(A_AT, A_TILES, i, j)

                split_hi(N(1))
                plain(N(0), ak, scale=float(P) ** -0.5)
                split_hi(N(2))
                plain(N(1), av)
                split_hi(N(3))
                plain(N(2), aq)
                split_hi(N(4))
                act.wait_ge(*G.after(i, "k_turned"))
                f(ktok[0:C0, 0, :], bra[0:C0, 0:P], ACT.Copy)
                f(ktok[:, 1:5, :].rearrange("p a b -> p (a b)"), bra[:, P:5 * P], ACT.Copy)
                S.done(f(AST[:, 0, 0:P], bra[:, 640:768], ACT.Copy), "k_rows")
                f(split2(aeo), source(N(3)), ACT.Exp, scale=-1.0).then_inc(evac_done, 1)
                split_hi(N(5))
                act.wait_ge(*V.after(i, "decay_args"))
                f(WW[0:C0, 0, 0:C0], WW[0:C0, 0, 0:C0], ACT.Exp, scale=-1.0)
                S.done(f(WW[:, 1:5, :], WW[:, 1:5, :], ACT.Exp, scale=-1.0), "decays")
                src = source(N(4))
                f(split2(az), src, ACT.Copy)
                f(split2(aez), src, ACT.Exp, scale=-1.0).then_inc(evac_done, 1)
                split_hi(N(6))
                plain(N(5), gbuf[0][:, :])
                split_hi(N(7))
                act.wait_ge(*V.after(i, "h_var"))
                S.done(f(smA[:, 4, :], smA[:, 3, :], ACT.Ln, bias=eps[:, 0:1]), "h_log")
                act.wait_ge(*S.after(i, "h_log"))
                S.done(f(smA[:, 5, :], smA[:, 4, :], ACT.Exp, scale=-0.5), "h_rstd")
                plain(N(6), gbuf[1][:, :])
                split_hi(N(8))
                act.wait_ge(*G.after(i, "states_turned"))
                S.done(f(c_out[:, :, :].rearrange("p a b -> p (a b)"), bra[:, 0:256], ACT.Copy), "state_out")
                act.wait_ge(gates_out[0], i * 32 + 16)
                plain(N(7), gbuf[0][:, :])
                act.wait_ge(gates_out[0], i * 32 + 32)
                act.wait_ge(gates_out[1], i * 16 + 16)
                act.wait_ge(states_out, i * 32 + 32)
                act.wait_ge(*V.after(i, "y"))
            act.wait_ge(*A2["norm_rows_tensor"].after(0, "n_turned"))
            A2["norm_rows_scalar"].done(f(nrow[0:16, :], bra[0:16, 0:P], ACT.Copy), "n_rows")

            G, V, S, Q = (C_[k] for k in ("rwkv_tensor", "rwkv_vector", "rwkv_scalar", "rwkv_pool"))
            act.wait_ge(states_out, 16 * (2 * NH_A + 2))
            split_hi(C_AT + 1)
            with act.Fori(0, NP_C) as i:
                def N(j):
                    return Num(C_AT, C_TILES, i, j)

                def last_rows(j, pb):
                    col = act.snap(i * 8 + 2 * j)
                    f(shifts[:, bass.ds(col, 2)], pb[:, 64:T + 2:T + 1 - 64], ACT.Copy)

                act.wait_ge(*V.after(i, "streams_apart"))
                shift_in(act, f, N(0), PB[0], tile_done, evac_done)
                split_hi(N(2))
                act.wait_ge(*G.after(i, "ranks"))
                f(split2(LL), halves(bra), ACT.Exp, scale=-1.0, bias=pv[:, 16:17])
                S.done(f(split2(ca), halves(brb), ACT.Exp, scale=-1.0, bias=pv[:, 17:18]), "rank_exps")
                act.wait_ge(*V.after(i, "log_decay_sums"))
                f(rh, LL, ACT.Exp)
                f(kkh, kkh, ACT.Exp)
                f(kh, LL, ACT.Exp, scale=-1.0)
                S.done(f(kE, kE, ACT.Exp), "decay_exps")
                shift_in(act, f, N(1), PB[1], tile_done, evac_done)
                split_hi(N(3))
                act.wait_ge(*V.after(i, "kk_raw"))
                last_rows(1, PB[0])
                S.done(f(ctmp, kk, ACT.Square), "kk_squares")
                act.wait_ge(*V.after(i, "r"))
                last_rows(0, PB[1])
                shift_in(act, f, N(2), PB[0], tile_done, evac_done)
                split_hi(N(4))
                act.wait_ge(*V.after(i, "kk_floor"))
                S.done(f(ctmp, ctmp, ACT.Ln, scale=float(2 ** 20)), "kk_log")
                act.wait_ge(*S.after(i, "kk_log"))
                S.done(f(ctmp, ctmp, ACT.Exp, scale=-0.5, bias=tenln2[:, 0:1]), "kk_rsqrt")
                act.wait_ge(*V.after(i, "v"))
                last_rows(2, PB[0])
                shift_in(act, f, N(3), PB[1], tile_done, evac_done)
                split_hi(N(5))

                def rows_of(dst, bank, after, step):
                    act.wait_ge(*G.after(i, after))
                    f(dst[0:C0, 0, :], bank[0:C0, 0:P], ACT.Copy)
                    S.done(f(dst[:, 1:5, :].rearrange("p a b -> p (a b)"), bank[:, P:5 * P], ACT.Copy), step)

                rows_of(kkT, bra, "kk_turned", "kk_rows")
                rows_of(vT, brb, "v_turned", "v_rows")
                rows_of(bET, bra, "bE_turned", "bE_rows")
                rows_of(kET, brb, "kE_turned", "kE_rows")
                act.wait_ge(*V.after(i, "z"))
                last_rows(3, PB[1])
                act.wait_ge(y_out, i * 16 + 16 * NH_A)
                S.done(f(ybuf[:, :], cz, ACT.Exp, scale=-1.0), "z_exp")

                def other_side(lv):
                    dst = DDT if lv else DD1
                    for h in range(2):
                        act.wait_ge(*G.after(i, f"turned{lv}_{h}"))
                        f(dst[0:C0, 5 * h, 0:C0], brb[0:C0, 0:C0], ACT.Copy)
                        S.done(f(dst[:, 5 * h + 1:5 * h + 5, :].rearrange("p a b -> p (a b)"), brb[:, P:5 * P], ACT.Copy), f"t{lv}_{h}")

                other_side(0)
                act.wait_ge(gates_out[0], i * 32 + 16 * (NH_A * 2))
                plain(N(4), gbuf[0][:, :])
                split_hi(N(6))
                for lv in range(1, 4):
                    other_side(lv)
                act.wait_ge(gates_out[1], i * 32 + 16 * NH_A)
                plain(N(5), gbuf[1][:, :])
                split_hi(N(7))
                for lv in range(4, LEVELS):
                    other_side(lv)
                act.wait_ge(*G.after(i, "solved"))
                f(TKT[:, 0, 0:C0], brb[:, 0:C0], ACT.Copy)
                S.done(f(TKT[:, 1:5, :].rearrange("p a b -> p (a b)"), brb[:, P:5 * P], ACT.Copy), "tk")
                for c in range(NCH):
                    act.wait_ge(*G.after(i, f"y_part{c}"))
                    S.done(f(ysb[:, START[c]:START[c] + LEN[c]], brb[:, 0:LEN[c]], ACT.Copy), f"out{c}")
                    if c == 1:
                        act.wait_ge(gates_out[0], i * 32 + 16 * (NH_A * 2 + 1))
                        plain(N(6), gbuf[0][:, :])
                        split_hi(N(8))
                act.wait_ge(*V.after(i, "y_centred"))
                S.done(f(ysq, yc, ACT.Square), "y_squares")
                act.wait_ge(*G.after(i, "y_square_sums"))
                S.done(f(split2(yv), halves(brb), ACT.Ln, scale=1.0 / 64, bias=gn_eps[:, 0:1]), "y_log")
                act.wait_ge(*S.after(i, "y_log"))
                S.done(f(yv, yv, ACT.Exp, scale=-0.5), "y_rstd")
                act.wait_ge(*G.after(i, "states_turned"))
                S.done(f(r_out, bra[:, 0:P], ACT.Copy), "state_out")
                split_hi(N(9))
                act.wait_ge(gates_out[1], i * 32 + 16 * (NH_A + 1))
                plain(N(7), gbuf[1][:, :])

            G, V, S, Q = (B_[k] for k in ("hgrn_tensor", "hgrn_vector", "hgrn_scalar", "hgrn_pool"))
            with act.Fori(0, NH_B) as i:
                def N(j):
                    return Num(B_AT, B_TILES, i, j)

                act.wait_ge(*V.after(i, "logit0"))
                S.done(f(lbv[:, 2:3], lbv[:, 1:2], ACT.Exp), "soft")
                src = source(N(0))
                f(split2(bef), src, ACT.Exp, scale=-1.0)
                f(split2(bep), src, ACT.Exp).then_inc(evac_done, 1)
                split_hi(N(2))
                act.wait_ge(*V.after(i, "f"))
                S.done(f(AL, bef, ACT.Ln), "log_f")
                plain(N(1), bq)
                split_hi(N(3))
                act.wait_ge(*V.after(i, "log_sums"))
                S.done(f(qhat, AL, ACT.Exp), "decay_exp")
                act.wait_ge(*V.after(i, "end_args"))
                S.done(f(khat, khat, ACT.Exp), "end_exp")
                plain(N(2), bv)
                split_hi(N(4))
                act.wait_ge(*V.after(i, "args0"))
                S.done(f(EE, EE, ACT.Exp), "exp0")

                def rows_of(dst, bank, after, step):
                    act.wait_ge(*G.after(i, after))
                    f(dst[0:C0, 0, :], bank[0:C0, 0:P], ACT.Copy)
                    S.done(f(dst[:, 1:5, :].rearrange("p a b -> p (a b)"), bank[:, P:5 * P], ACT.Copy), step)

                rows_of(khtok, bra, "k_turned", "k_rows")
                rows_of(vbtok, brb, "v_turned", "v_rows")
                src = source(N(3))
                f(split2(bz), src, ACT.Copy)
                f(split2(bez), src, ACT.Exp, scale=-1.0).then_inc(evac_done, 1)
                split_hi(N(5))
                for lv in range(1, LEVELS):
                    act.wait_ge(*V.after(i, f"args{lv}"))
                    S.done(f(EE, EE, ACT.Exp), f"exp{lv}")
                act.wait_ge(gates_out[0], i * 16 + 16 * (NH_A * 2 + NP_C * 2))
                plain(N(4), gbuf[0][:, :])
                split_hi(N(6))
                act.wait_ge(*G.after(i, "outputs"))
                for c in range(NCH):
                    last = f(bjunk[0:LEN[c], :], brb[0:LEN[c], P * c:P * c + P], ACT.Square, accum_out=bss[0:LEN[c], 0, c:c + 1])
                    S.done(last, f"o_sum{c}")
                    act.wait_ge(*S.after(i, f"o_sum{c}"))
                S.done(f(bss[:, 1, :], bss[:, 0, :], ACT.Ln, scale=1.0 / P, bias=eps[:, 0:1]), "o_log")
                act.wait_ge(*S.after(i, "o_log"))
                S.done(f(bss[:, 1, :], bss[:, 1, :], ACT.Exp, scale=-0.5), "o_rstd")
                split_hi(N(7))
                act.wait_ge(gates_out[1], i * 16 + 16 * (NH_A + NP_C * 2))
                plain(N(5), gbuf[1][:, :])
            act.wait_ge(tile_done, PROJ_AT)
            for k in range(KT):
                act.wait_ge(y_here[0 if k < EARLY else 1 if k < NH_A + NP_C else 2], 16)
                f(xh[:, k, :], YIN[:, place[k], :], ACT.Copy).then_inc(y_hi, 1)
            act.wait_ge(*E_["shift_tensor"].after(0, "shift_turned"))
            E_["shift_scalar"].done(f(shrow[0:64, :], brb[0:64, 0:P], ACT.Copy), "shift_out")
            G, V, S = P_["merge_tensor"], P_["merge_vector"], P_["merge_scalar"]
            with act.Fori(0, KT // 2) as i:
                for j in range(2):
                    act.wait_ge(g_here[j], i * 48 + 48)
                    S.done(f(gs[:, :, :], gin[:, j, :, :], ACT.Sigmoid), f"gates{j}")
                    split_hi(Num(PROJ_AT, 2, i, j + 2))
                    act.wait_ge(*V.after(i, f"part2_{j}"))

            act.wait_ge(tile_done, OUT_AT)
            for k in range(KT):
                act.wait_ge(*V.after(k // 2, f"merged{k % 2}"))
                f(xh[:, k, :], ZF[:, k, :], ACT.Copy).then_inc(z_hi, 1)
            G, V, S = O_["out_tensor"], O_["out_vector"], O_["out_scalar"]
            act.wait_ge(z_split, KT)

            def square_rows(i, j, tile):
                act.wait_ge(*V.after(i, f"rows{j}"))
                if j:
                    act.wait_ge(*S.after(i, "squares0"))
                col = act.snap(tile * P) if not isinstance(tile, int) else tile * P
                for t in range(5):
                    r = ROWS[t]
                    part = squares[0:r, t, bass.ds(tile, 1)]
                    last = f(sq_junk[0:r, t, :], YT[0:r, t, bass.ds(col, P)], ACT.Square, accum_out=part)
                S.done(last, f"squares{j}")

            with act.Fori(0, KT // 2 - 1) as i:
                for j in range(2):
                    plain(Num(OUT_AT, 2, i, j), zt[j])
                    split_hi(Num(OUT_AT, 2, i, j + 2))
                    square_rows(i, j, act.snap(i * 2 + j))
                act.wait_ge(*S.after(i, "squares1"))
            last = KT // 2 - 1
            plain(N_TILES - 2, zt[0])
            square_rows(last, 0, KT - 2)
            plain(N_TILES - 1, zt[1])
            square_rows(last, 1, KT - 1)
            act.wait_ge(r_sums, 1)
            for a, b, r in ((0, 4, P), (4, 5, ROWS[4])):
                f(small[0:r, 32 + a:32 + b], small[0:r, 24 + a:24 + b], ACT.Ln, scale=1.0 / D, bias=eps[0:r, 0:1]).then_inc(r_sums, 1)
            act.wait_ge(r_sums, 3)
            for a, b, r in ((0, 4, P), (4, 5, ROWS[4])):
                f(small[0:r, 40 + a:40 + b], small[0:r, 32 + a:32 + b], ACT.Exp, scale=-0.5).then_inc(r_sums, 1)

        @block.vector
        def _(dve):
            v = nc.vector

            def split_lo(m):
                s = SLOT_OF(m)
                dve.wait_ge(hi_done, m + 1)
                v.tensor_tensor(wlo[:, s, :], wraw[:, s, :], whi[:, s, :].bitcast(F32), ALU.subtract).then_inc(lo_done, 1)

            def mixed(out, pb, diff, mu, S, i, name):
                S.done(v.tensor_tensor(diff[:, 0:T + 1], pb[:, 0:T + 1], pb[:, 1:T + 2], ALU.subtract), name + "_step")
                dve.wait_ge(*S.after(i, name + "_step"))
                v.scalar_tensor_tensor(out=out[:, 0:NS], in0=diff[:, 0:NS], scalar=mu, in1=pb[:, 1:NS + 1], op0=ALU.mult, op1=ALU.add)
                return S.done(v.scalar_tensor_tensor(out=out[:, NS:T], in0=diff[:, NS + 1:T + 1], scalar=mu,
                                                     in1=pb[:, NS + 2:T + 2], op0=ALU.mult, op1=ALU.add), name)

            S = S0["setup_vector"]
            dve.wait_ge(*S0["setup_pool"].after(0, "zeros"))
            dve.wait_ge(vecs_here, 16)
            dve.wait_ge(x_sums, 7)
            dve.wait_ge(consts_here, 16)
            for t in range(5):
                v.tensor_scalar(unit[:, t, :], ident, small[:, 16 + t:17 + t], None, ALU.mult).then_inc(x_unit, 1)
            split_lo(0)
            split_lo(1)
            for k in range(KT):
                dve.wait_ge(x_hi, k + 1)
                v.scalar_tensor_tensor(out=xl[:, k, :], in0=ring4[k % 4][:, 0:T], scalar=vec("norm_pre", k),
                                       in1=xh[:, k, :].bitcast(F32), op0=ALU.mult, op1=ALU.subtract).then_inc(x_lo, 1)
            S.done(v.memset(ONES[0:8, :], 1.0), "ones")
            S.done(v.memset(RR[0:96, :], 0.0), "rows_clear")
            split_lo(2)
            dve.wait_ge(evac_done, 1)
            S.done(v.tensor_scalar(GI[0:8, :], GI[0:8, :], vec("b_i", rows=8), None, ALU.add), "i")
            S.done(v.tensor_scalar(XF[0:8, :], XF[0:8, :], vec("b_f", rows=8), None, ALU.add), "f")
            dve.wait_ge(*S.after(0, "f"))
            S.done(v.scalar_tensor_tensor(out=AB[0:8, :], in0=XF[0:8, :], scalar=-1.0, in1=XF[0:8, :], op0=ALU.mult, op1=ALU.max), "f_size")
            dve.wait_ge(*S0["setup_scalar"].after(0, "f_log"))
            S.done(v.scalar_tensor_tensor(out=LF[0:8, :], in0=XF[0:8, :], scalar=0.0, in1=AB[0:8, :], op0=ALU.min, op1=ALU.subtract), "log_f")
            dve.wait_ge(*S.after(0, "log_f"))
            for a, b in ((0, NS), (NS, T)):
                last = v.tensor_tensor_scan(BC[0:8, a:b], ONES[0:8, a:b], LF[0:8, a:b], 0.0, ALU.mult, ALU.add)
            S.done(last, "b")
            dve.wait_ge(*S.after(0, "b"))
            S.done(v.tensor_tensor(GI[0:8, :], GI[0:8, :], BC[0:8, :], ALU.subtract), "g")
            dve.wait_ge(*S.after(0, "g"))
            v.tensor_tensor_scan(MR[0:8, 0:NS], ONES[0:8, 0:NS], GI[0:8, 0:NS], vec("m0", rows=8), ALU.mult, ALU.max)
            S.done(v.tensor_tensor_scan(MR[0:8, NS:T], ONES[0:8, NS:T], GI[0:8, NS:T], 0.0, ALU.mult, ALU.max), "m_max")
            dve.wait_ge(*S.after(0, "m_max"))
            S.done(v.tensor_tensor(MT[0:8, :], MR[0:8, :], BC[0:8, :], ALU.add), "m")
            v.tensor_copy(MC[0:8, 0:1], vec("m0", rows=8))
            v.tensor_copy(MC[0:8, 1:2], MR[0:8, NS - 1:NS])
            S.done(v.tensor_copy(MC[0:8, 2:7], MR[0:8, C0 - 1:T:P]), "m_ends")
            dve.wait_ge(*S.after(0, "m_ends"))
            dve.wait_ge(masks_here, 16)
            S.done(v.tensor_tensor(ME[0:8, :, :], ident[0:8, 0:8].unsqueeze(2).to_broadcast([8, 8, 7]),
                                   MC[0:8, :].unsqueeze(1).to_broadcast([8, 8, 7]), ALU.mult), "ends")
            dve.wait_ge(evac_done, 2)
            dve.wait_ge(*S0["setup_pool"].after(0, "cleared"))
            mixed(low, LOWP, LOWD, vec("low_mu"), S, 0, "low_mixed")
            dve.wait_ge(*S0["setup_scalar"].after(0, "low_exp"))
            S.done(v.tensor_scalar(low[0:64, :], low[0:64, :], 1.0, None, ALU.add), "low_1")
            dve.wait_ge(*S.after(0, "low_1"))
            S.done(v.reciprocal(low[0:64, :], low[0:64, :]), "low_2")
            dve.wait_ge(*S.after(0, "low_2"))
            S.done(v.tensor_scalar(low[0:64, :], low[0:64, :], -2.0, 1.0, ALU.mult, ALU.add), "low_tanh")
            dve.wait_ge(*S0["setup_scalar"].after(0, "ends"))
            TKv = TK[:, :, :].rearrange("p c n -> p n c")
            v.tensor_copy(pk_all[:, :, 0:5], TKv[:, 0:8, :])
            v.tensor_tensor(pk_all[:, :, 6:10], TKv[:, 0:8, 1:5], EB[:, :, 3:7], ALU.subtract)
            v.tensor_tensor(pk_all[0:64, :, 5:6], TKv[0:64, 0:8, 0:1], EB[0:64, :, 1:2], ALU.subtract)
            v.tensor_tensor(pk_all[64:128, :, 5:6], TKv[64:128, 0:8, 0:1], EB[64:128, :, 2:3], ALU.subtract)
            v.tensor_tensor(pk_all[:, :, 11:15], EB[:, :, 2:6], TKv[:, 32:40, 1:5], ALU.subtract)
            v.tensor_tensor(pk_all[:, :, 10:11], EB[:, :, 0:1], TKv[:, 32:40, 0:1], ALU.subtract)
            v.tensor_scalar(pk_all[:, :, 15:20], TKv[:, 64:72, :], -1.0, None, ALU.mult)
            v.tensor_tensor(pk_all[:, :, 20:21], EB[:, :, 0:1], EB[:, :, 1:2], ALU.subtract)
            S.done(v.tensor_tensor(pk_all[:, :, 21:25], EB[:, :, 2:6], EB[:, :, 3:7], ALU.subtract), "scalar_args")
            v.tensor_copy(pk_all[:, :, 25:26], vecs[:, VEC["mlstm_norm"]:VEC["mlstm_norm"] + 8].unsqueeze(2))
            S.done(v.tensor_copy(pk_all[:, :, 26:27], vecs[:, VEC["n0"]:VEC["n0"] + 8].unsqueeze(2)), "head_vectors")
            dve.wait_ge(*S0["setup_scalar"].after(0, "scalars"))

            G, V, S, Q = (A_[k] for k in ("mlstm_tensor", "mlstm_vector", "mlstm_scalar", "mlstm_pool"))
            dve.wait_ge(*S0["setup_pool"].after(0, "mlstm_cleared"))
            with dve.Fori(0, NH_A) as i:
                def N(j):
                    return Num(A_AT, A_TILES, i, j)

                def own(step):
                    dve.wait_ge(*V.after(i, step))

                split_lo(N(1))
                V.done(v.tensor_copy(pk[:, :], pk_all[:, bass.ds(i, 1), :].rearrange("p a n -> p (a n)")), "scalars")
                V.done(v.tensor_scalar(DM[0:8, :], MR[0:8, :], ident[0:8, bass.ds(i, 1)], None, ALU.mult), "head_m")
                split_lo(N(2))
                own("scalars")
                V.done(v.tensor_copy(AST[:, 0, P:P + 1], pk[:, 26:27]), "n0")
                split_lo(N(3))
                split_lo(N(4))
                dve.wait_ge(*G.after(i, "v_turned"))
                v.tensor_copy(vtok[0:C0, 0, 0:P], brb[0:C0, 0:P])
                V.done(v.tensor_copy(vtok[:, 1:5, 0:P], brb[:, P:5 * P].rearrange("p (c n) -> p c n", c=4)), "v_rows")
                own("v_rows")
                v.tensor_scalar(wsv[0:C0, 0, :], vtok[0:C0, 0, :], pk[0:C0, 5:6], None, ALU.mult)
                for c in range(1, NCH):
                    last = v.tensor_scalar(wsv[:, c, :], vtok[:, c, :], pk[:, 5 + c:6 + c], None, ALU.mult)
                V.done(last, "v_weighted")
                split_lo(N(5))
                dve.wait_ge(*G.after(i, "m_everywhere"))
                for c in range(NCH):
                    o, n = psum_col(c), LEN[c]
                    last = v.tensor_scalar(WW[0:n, c, 0:n], bra[0:n, o:o + n], pk[0:n, c:c + 1], 0.0, ALU.subtract, ALU.max)
                V.done(last, "decay_args")
                dve.wait_ge(*G.after(i, "scores"))
                dve.wait_ge(*Q.after(i, "masked"))
                v.tensor_tensor(PP[0:C0, 0, 0:C0], brb[0:C0, 0:C0], WW[0:C0, 0, 0:C0], ALU.mult)
                V.done(v.tensor_tensor(PP[:, 1:5, :].rearrange("p a b -> p (a b)"), brb[:, P:5 * P],
                                       WW[:, 1:5, :].rearrange("p a b -> p (a b)"), ALU.mult), "probs")
                split_lo(N(6))
                dve.wait_ge(*G.after(i, "updates"))
                dve.wait_ge(*S.after(i, "k_rows"))
                v.scalar_tensor_tensor(out=AST[:, 6, :], in0=AST[:, 0, :], scalar=pk[:, 20:21], in1=bra[:, 0:129], op0=ALU.mult, op1=ALU.add)
                V.done(v.tensor_copy(AST[:, 1, :], bra[:, 129:258]), "state1")
                for c in range(1, NCH):
                    o = {1: 258, 2: 512, 3: 641, 4: 770}[c]
                    own(f"state{c}")
                    V.done(v.scalar_tensor_tensor(out=AST[:, c + 1, :], in0=AST[:, c, :], scalar=pk[:, 20 + c:21 + c],
                                                  in1=bra[:, o:o + 129], op0=ALU.mult, op1=ALU.add), f"state{c + 1}" if c < 4 else "states")
                dve.wait_ge(*G.after(i, "inside"))
                v.tensor_copy(num[0:C0, 0, :], brb[0:C0, 258:387])
                v.tensor_copy(num[:, 1:3, :], brb[:, 0:258].rearrange("p (c n) -> p c n", c=2))
                V.done(v.tensor_copy(num[:, 3:5, :], brb[:, 512:770].rearrange("p (c n) -> p c n", c=2)), "inside")
                split_lo(N(7))
                dve.wait_ge(*G.after(i, "carried"))
                own("inside")
                for c in range(NCH):
                    o, n = part_col(c), (NS if c == 0 else P)
                    last = v.scalar_tensor_tensor(out=num[0:n, c, :], in0=bra[0:n, o:o + 129], scalar=pk[0:n, 10 + c:11 + c],
                                                  in1=num[0:n, c, :], op0=ALU.mult, op1=ALU.add)
                V.done(last, "num")
                own("num")
                den = num[:, :, P:P + 1].rearrange("p c n -> p (c n)")
                V.done(v.scalar_tensor_tensor(out=smA[:, 0, :], in0=den, scalar=-1.0, in1=den, op0=ALU.mult, op1=ALU.max), "den_size")
                for c in range(NCH):
                    n = LEN[c]
                    last = v.bn_stats(stats[0:n, c, :], num[0:n, c, 0:P])
                V.done(last, "stats")
                own("den_size")
                V.done(v.tensor_tensor(smA[:, 0, :], smA[:, 0, :], pk[:, 15:20], ALU.max), "den")
                own("stats")
                own("den")
                V.done(v.reciprocal(smA[:, 1, :], smA[:, 0, :]), "den_inv")
                for c in range(NCH):
                    n = LEN[c]
                    last = v.bn_aggr(aggr[0:n, c, :], stats[0:n, c, :])
                V.done(last, "aggr")
                own("den_inv")
                V.done(v.tensor_tensor(smA[:, 2, :], smA[:, 1, :], smA[:, 1, :], ALU.mult), "den_inv2")
                own("den_inv2")
                V.done(v.tensor_tensor(smA[:, 3, :], aggr[:, :, 1:2].rearrange("p c n -> p (c n)"), smA[:, 2, :], ALU.mult), "h_var")
                dve.wait_ge(evac_done, N(4) + 1)
                V.done(v.tensor_scalar(aez, aez, 1.0, None, ALU.add), "gate1")
                own("gate1")
                V.done(v.scalar_tensor_tensor(out=aez, in0=aeo, scalar=1.0, in1=aez, op0=ALU.add, op1=ALU.mult), "gate2")
                own("gate2")
                V.done(v.reciprocal(aez, aez), "gate3")
                own("gate3")
                V.done(v.scalar_tensor_tensor(out=agz, in0=az, scalar=pk[:, 25:26], in1=aez, op0=ALU.mult, op1=ALU.mult), "gate")
                dve.wait_ge(*S.after(i, "h_rstd"))
                V.done(v.tensor_tensor(smA[:, 6, :], smA[:, 5, :], smA[:, 1, :], ALU.mult), "h_scale")
                own("h_scale")
                for c in range(NCH):
                    n = LEN[c]
                    last = v.tensor_scalar(hn[0:n, c, :], num[0:n, c, 0:P], aggr[0:n, c, 0:1], smA[0:n, 6, c:c + 1], ALU.subtract, ALU.mult)
                V.done(last, "h_unit")
                V.done(v.tensor_copy(nout[:, :, bass.ds(i, 1)].rearrange("p m a -> p (m a)"), AST[:, 5:7, P:P + 1].rearrange("p m a -> p (m a)")), "n_out")
                split_lo(N(8))
                dve.wait_ge(*G.after(i, "h_turned"))
                own("gate")
                v.tensor_tensor(ybuf[:, 0:SPLIT], brb[:, 0:SPLIT], agz[:, 0:SPLIT], ALU.mult)
                V.done(v.tensor_tensor(ybuf[:, SPLIT:T], brb[:, 512:512 + T - SPLIT], agz[:, SPLIT:T], ALU.mult), "y")
                dve.wait_ge(y_out, i * 16 + 16)
                dve.wait_ge(*S.after(i, "state_out"))
                dve.wait_ge(*G.after(i, "states_turned"))

            G, V, S, Q = (C_[k] for k in ("rwkv_tensor", "rwkv_vector", "rwkv_scalar", "rwkv_pool"))
            dve.wait_ge(*A2["norm_rows_tensor"].after(0, "n_turned"))
            with dve.Fori(0, NP_C) as i:
                def N(j):
                    return Num(C_AT, C_TILES, i, j)

                def own(step):
                    dve.wait_ge(*V.after(i, step))

                def tt(out, a, b, op, step=None):
                    ins = v.tensor_tensor(out, a, b, op)
                    return V.done(ins, step) if step else ins

                split_lo(N(1))
                group = dve.snap(i * PAIR_VECS + VEC["pair"])
                V.done(v.tensor_copy(pv[:, 0:PAIR_VECS], vecs[:, bass.ds(group, PAIR_VECS)]), "vectors")
                own("vectors")
                v.tensor_scalar(pv[:, 16:18], pv[:, W0:A0 + 1], -1.0, None, ALU.mult)
                v.tensor_scalar(pv[:, KA1:KA1 + 1], pv[:, K_A:K_A + 1], -1.0, 1.0, ALU.mult, ALU.add)
                v.tensor_copy(PB[0][:, 0:1], pv[:, CACHE + 1:CACHE + 2])
                V.done(v.tensor_copy(PB[1][:, 0:1], pv[:, CACHE:CACHE + 1]), "negated")
                v.memset(PB[0][:, NS + 1:NS + 2], 0.0)
                V.done(v.memset(PB[1][:, NS + 1:NS + 2], 0.0), "streams_apart")
                split_lo(N(2))
                dve.wait_ge(*S.after(i, "rank_exps"))
                v.tensor_scalar(LL, LL, 1.0, None, ALU.add)
                V.done(v.tensor_scalar(ca, ca, 1.0, None, ALU.add), "ranks1")
                own("ranks1")
                v.reciprocal(LL, LL)
                V.done(v.reciprocal(ca, ca), "a")
                own("a")
                V.done(v.tensor_scalar(cb, LL, -float(np.exp(-0.5)), None, ALU.mult), "log_decay")
                own("log_decay")
                V.done(v.tensor_tensor_scan(LL, mask("carry"), cb, 0.0, ALU.mult, ALU.add), "log_sums")
                own("log_sums")
                tt(kkh, LL, cb, ALU.subtract)
                tt(kE[:, 0:NS], LL[:, NS - 1:NS].to_broadcast([P, NS]), LL[:, 0:NS], ALU.subtract)
                tt(kE[:, NS:C0], LL[:, C0 - 1:C0].to_broadcast([P, NM]), LL[:, NS:C0], ALU.subtract)
                tt(kE[:, C0:T].rearrange("p (c n) -> p c n", c=4), LL[:, C0 + P - 1:T:P].unsqueeze(2).to_broadcast([P, 4, P]),
                   LL[:, C0:T].rearrange("p (c n) -> p c n", c=4), ALU.subtract, "log_decay_sums")
                own("streams_apart")
                dve.wait_ge(evac_done, N(0) + 1)
                mixed(ck, PB[0], DD, pv[:, MU + 1:MU + 2], V, i, "k")
                own("k")
                dve.wait_ge(states_out, i * 64 + 16 * (2 * NH_A + 2))
                V.done(v.tensor_scalar(kk, ck, pv[:, K_K:K_K + 1], None, ALU.mult), "kk_raw")
                own("kk_raw")
                V.done(v.tensor_scalar(cb, ca, pv[:, K_A:K_A + 1], pv[:, KA1:KA1 + 1], ALU.mult, ALU.add), "k_factor")
                own("k_factor")
                tt(ck, ck, cb, ALU.mult, "k_new")
                dve.wait_ge(evac_done, N(1) + 1)
                mixed(cr, PB[1], DD, pv[:, MU:MU + 1], V, i, "r")
                own("r")
                own("k_new")
                dve.wait_ge(*S.after(i, "decay_exps"))
                dve.wait_ge(*S.after(i, "kk_squares"))
                v.tensor_copy(PB[0][:, 0:1], pv[:, CACHE + 2:CACHE + 3])
                V.done(v.scalar_tensor_tensor(out=bon, in0=cr, scalar=pv[:, R_K:R_K + 1], in1=ck, op0=ALU.mult, op1=ALU.mult), "bonus_terms")
                v.tensor_copy(eends[:, 0:2], rh[:, NS - 1:C0:NM])
                V.done(v.tensor_copy(eends[:, 2:6], rh[:, C0 + P - 1:T:P]), "end_decays")
                own("end_decays")
                tt(rh, rh, cr, ALU.mult, "rh")
                split_lo(N(3))
                dve.wait_ge(*G.after(i, "kk_lengths"))
                V.done(v.tensor_scalar(split2(ctmp), halves(bra), 1e-24, None, ALU.max), "kk_floor")
                dve.wait_ge(evac_done, N(2) + 1)
                own("bonus_terms")
                mixed(cvv, PB[0], DD, pv[:, MU + 2:MU + 3], V, i, "v")
                split_lo(N(4))
                dve.wait_ge(*S.after(i, "kk_rsqrt"))
                v.tensor_copy(PB[1][:, 0:1], pv[:, CACHE + 3:CACHE + 4])
                tt(kk, kk, ctmp, ALU.mult, "kk")
                own("kk")
                tt(cb, kk, ca, ALU.mult, "b")
                tt(kkh, kkh, kk, ALU.mult, "kkh")
                own("b")
                tt(bh, kh, cb, ALU.mult, "bh")
                own("bh")
                tt(kh, kh, ck, ALU.mult, "kh")
                tt(bE, kE, cb, ALU.mult, "bE")
                own("bE")
                tt(kE, kE, ck, ALU.mult, "kE")
                dve.wait_ge(*G.after(i, "bonus_sums"))
                own("v")
                V.done(v.tensor_copy(RST[:, 0, :], brb[:, 896:960]), "state0")
                V.done(v.tensor_tensor(split2(bon), halves(brb), split2(cvv), ALU.mult), "bonus")
                dve.wait_ge(evac_done, N(3) + 1)
                own("kk")
                mixed(cz, PB[1], DD, pv[:, MU + 3:MU + 4], V, i, "z")
                def masked(dst, h, name, bank, after, step):
                    m = masks[:, CONST_AT[name][0]:CONST_AT[name][0] + 2 * P]
                    dve.wait_ge(*G.after(i, after))
                    tt(dst[0:C0, 5 * h, 0:C0], bank[0:C0, 0:C0], m[0:C0, 0:C0], ALU.mult)
                    tt(dst[:, 5 * h + 1:5 * h + 5, :], bank[:, P:5 * P].rearrange("p (c n) -> p c n", c=4),
                       m[:, P:2 * P].unsqueeze(1).to_broadcast([P, 4, P]), ALU.mult, step)

                def rows_in(lv):
                    return (C0 if lv < 4 else NS) if lv < 6 else 0

                def lower_parts(lv, src, name):
                    n0, at = rows_in(lv), CONST_AT[name][0] + (64 * lv if name == "down" else 0)
                    mk = masks[:, at:at + 64]
                    if n0:
                        tt(UU[0:n0, 0:6:5, 0:n0 // 2], src[0:n0, 0:6:5, 0:n0 // 2],
                           mk[0:n0, 0:n0 // 2].unsqueeze(1).to_broadcast([n0, 2, n0 // 2]), ALU.mult)
                    for h in range(2):
                        last = tt(UU[:, 5 * h + 1:5 * h + 5, :], src[:, 5 * h + 1:5 * h + 5, :],
                                  mk.unsqueeze(1).to_broadcast([P, 4, 64]), ALU.mult)
                    V.done(last, f"low{lv}")

                def subtract_parts(lv, dst, src, side):
                    for q0, q1, step, n in ((0, 6, 5, rows_in(lv)), (1, 5, 1, P), (6, 10, 1, P)):
                        if n:
                            cols = dst[0:n, q0:q1:step, 0:n].rearrange("p q (b two w) -> p q b two w", two=2, w=1 << lv)[:, :, :, side, :]
                            last = tt(cols, cols, src[0:n, q0:q1:step, 0:n // 2].rearrange("p q (b w) -> p q b w", w=1 << lv), ALU.subtract)
                    V.done(last, f"inv{lv}")

                own("kE")
                own("z")
                dve.wait_ge(*G.after(i, "kE_turned"))
                masked(AT, 0, "before", bra, "bu0_", "bu0")
                masked(AT, 1, "before", brb, "bu1_", "bu1")
                masked(KTm, 0, "before", bra, "uk0_", "uk0")
                masked(KTm, 1, "before", brb, "uk1_", "uk1")
                split_lo(N(5))
                masked(BM, 0, "causal", bra, "yb0_", "yb0")
                masked(BM, 1, "causal", brb, "yb1_", "yb1")
                masked(KM, 0, "causal", bra, "yk0_", "yk0")
                masked(KM, 1, "causal", brb, "yk1_", "yk1")
                lower_parts(0, AT[:, :, 1::2], "up")
                dve.wait_ge(*Q.after(i, "unit_blocks"))
                own("low0")
                subtract_parts(0, DDT, UU, 1)
                dve.wait_ge(*G.after(i, "uk_v"))
                v.tensor_copy(W1[0:C0, 0:6:5, :], bra[0:C0, 0:640].rearrange("p (q n) -> p q n", q=10)[:, 0:6:5, :])
                v.tensor_copy(W1[:, 1:5, :], bra[:, 64:320].rearrange("p (q n) -> p q n", q=4))
                V.done(v.tensor_copy(W1[:, 6:10, :], bra[:, 384:640].rearrange("p (q n) -> p q n", q=4)), "w1")

                pa = bra[:, 0:640].rearrange("p (q n) -> p q n", q=10)
                dve.wait_ge(*S.after(i, "z_exp"))
                V.done(v.tensor_scalar(ybuf[:, :], ybuf[:, :], 1.0, None, ALU.add), "z1")
                own("z1")
                for lv in range(1, LEVELS):
                    dve.wait_ge(*G.after(i, f"au{lv}"))
                    lower_parts(lv, pa, "down")
                    if lv == 1:
                        split_lo(N(6))
                    dve.wait_ge(*G.after(i, f"du{lv}"))
                    subtract_parts(lv, DD1, pa, 0)
                    if lv == 2:
                        V.done(v.reciprocal(ybuf[:, :], ybuf[:, :]), "z2")
                    elif lv == 3:
                        own("z2")
                        tt(cz, cz, ybuf[:, :], ALU.mult, "gate")
                    elif lv == 5:
                        split_lo(N(7))
                dve.wait_ge(*G.after(i, "solved"))
                v.tensor_copy(TV[0:C0, 0:6:5, :], bra[0:C0, 0:640].rearrange("p (q n) -> p q n", q=10)[:, 0:6:5, :])
                v.tensor_copy(TV[:, 1:5, :], bra[:, 64:320].rearrange("p (q n) -> p q n", q=4))
                V.done(v.tensor_copy(TV[:, 6:10, :], bra[:, 384:640].rearrange("p (q n) -> p q n", q=4)), "tv")
                own("tv")
                ut = utok.rearrange("p a b -> p (a b)")
                for c in range(NCH):
                    n = NS if c == 0 else P
                    dve.wait_ge(*G.after(i, f"u_carried{c}"))
                    if c:
                        dve.wait_ge(*G.after(i, f"y_part{c - 1}"))
                    if c == 0:
                        v.tensor_scalar(ut[NS:C0, 0:P].rearrange("p (h n) -> p h n", h=2), TV[NS:C0, 0:6:5, :], -1.0, None, ALU.mult)
                    V.done(v.scalar_tensor_tensor(out=ut[0:n, 0:P].rearrange("p (h n) -> p h n", h=2), in0=halves(bra, 64)[0:n], scalar=-1.0,
                                                  in1=TV[0:n, c:c + 6:5, :], op0=ALU.mult, op1=ALU.subtract), f"u{c}")
                    dve.wait_ge(*G.after(i, f"state_part{c}"))
                    if c == 0:
                        v.scalar_tensor_tensor(out=RST[:, 6, :], in0=RST[:, 0, :], scalar=eends[:, 0:1], in1=brb[:, 512:576], op0=ALU.mult, op1=ALU.add)
                        V.done(v.tensor_copy(RST[:, 1, :], bra[:, 256:320]), "state1")
                    else:
                        own(f"state{c}")
                        V.done(v.scalar_tensor_tensor(out=RST[:, c + 1, :], in0=RST[:, c, :], scalar=eends[:, c + 1:c + 2],
                                                      in1=brb[:, 512:576], op0=ALU.mult, op1=ALU.add), f"state{c + 1}")
                split_lo(N(8))
                dve.wait_ge(*G.after(i, "y_sums"))
                V.done(v.scalar_tensor_tensor(out=split2(yc), in0=halves(bra), scalar=-1.0 / 64, in1=split2(ysb), op0=ALU.mult, op1=ALU.add), "y_centred")
                own("state5")
                dve.wait_ge(*S.after(i, "y_rstd"))
                tt(yc, yc, yv, ALU.mult, "y_unit")
                own("y_unit")
                V.done(v.tensor_scalar(yc, yc, pv[:, GN_G:GN_G + 1], pv[:, GN_B:GN_B + 1], ALU.mult, ALU.add), "y_affine")
                own("y_affine")
                tt(yc, yc, bon, ALU.add, "y_bonus")
                own("y_bonus")
                dve.wait_ge(y_out, i * 16 + 16 * NH_A)
                tt(ybuf[:, :], yc, cz, ALU.mult, "y")

            sv = shifts[:, 0:32].rearrange("p (i j m) -> p j m i", j=4, m=2)
            pm = shpad[:, :].rearrange("p (m n) -> p m n", m=2)
            dve.wait_ge(*C_["rwkv_scalar"].after(NP_C - 1, "z_exp"))
            for j, at in ((0, 0), (1, 4), (2, 8), (3, 13)):
                v.tensor_copy(pm[:, :, at:at + 4], sv[:, j, :, :])
            E_["shift_vector"].done(v.tensor_copy(pm[:, :, 12:13], shifts[:, 32:34].unsqueeze(2)), "columns")

            G, V, S, Q = (B_[k] for k in ("hgrn_tensor", "hgrn_vector", "hgrn_scalar", "hgrn_pool"))
            with dve.Fori(0, NH_B) as i:
                def N(j):
                    return Num(B_AT, B_TILES, i, j)

                def own(step):
                    dve.wait_ge(*V.after(i, step))

                def regions(lv):
                    if lv < 4:
                        return [(0, T)]
                    return [(0, NS), (C0, T)] if lv < 6 else [(C0, T)]

                def level_args(lv):
                    w = 1 << lv
                    if lv:
                        own(f"scaled{lv - 1}")
                    for a, b in regions(lv):
                        A = AL[:, a:b].rearrange("p (n two w) -> p n two w", two=2, w=w)
                        E = EE[:, a:b].rearrange("p (n two w) -> p n two w", two=2, w=w)
                        nb = (b - a) // (2 * w)
                        ref = A[:, :, 0, w - 1:w].to_broadcast([P, nb, w])
                        v.tensor_tensor(E[:, :, 1, :], A[:, :, 1, :], ref, ALU.subtract)
                        last = v.tensor_tensor(E[:, :, 0, :], ref, A[:, :, 0, :], ALU.subtract)
                    V.done(last, f"args{lv}")

                split_lo(N(1))
                col = dve.snap(i + VEC["lb"])
                col2 = dve.snap(i + VEC["hgrn_norm"])
                v.tensor_copy(lbv[:, 5:6], vecs[:, bass.ds(col2, 1)])
                V.done(v.tensor_copy(lbv[:, 0:1], vecs[:, bass.ds(col, 1)]), "logit")
                own("logit")
                V.done(v.tensor_tensor(lbv[:, 1:2], lbv[:, 0:1], lbv[:, 0:1], ALU.subtract), "logit0")
                dve.wait_ge(*S.after(i, "soft"))
                V.done(v.reciprocal(lbv[:, 3:4], lbv[:, 2:3]), "soft_inv")
                own("soft_inv")
                V.done(v.tensor_tensor(lbv[:, 6:7], lbv[:, 3:4], lbv[:, 2:3], ALU.mult), "softmax")
                own("softmax")
                V.done(v.tensor_tensor(lbv[:, 4:5], lbv[:, 6:7], lbv[:, 6:7], ALU.subtract), "bound")
                own("bound")
                V.done(v.tensor_scalar(lbv[:, 7:8], lbv[:, 4:5], -1.0, 1.0, ALU.mult, ALU.add), "rest")
                own("rest")
                dve.wait_ge(evac_done, N(0) + 1)
                v.tensor_scalar(bef, bef, 1.0, None, ALU.add)
                V.done(v.tensor_scalar(bep, bep, 1.0, None, ALU.add), "f1")
                own("f1")
                v.reciprocal(bef, bef)
                V.done(v.reciprocal(bep, bep), "f2")
                own("f2")
                V.done(v.tensor_scalar(bk, bep, lbv[:, 7:8], None, ALU.mult), "k")
                V.done(v.tensor_scalar(bef, bef, lbv[:, 7:8], lbv[:, 4:5], ALU.mult, ALU.add), "f3")
                own("f3")
                V.done(v.tensor_scalar(bef, bef, 1e-19, None, ALU.max), "f")
                split_lo(N(2))
                dve.wait_ge(*S.after(i, "log_f"))
                V.done(v.tensor_scalar(bef, AL, 1.0, None, ALU.mult), "log_copy")
                own("log_copy")
                V.done(v.tensor_tensor_scan(AL, mask("carry"), bef, 0.0, ALU.mult, ALU.add), "log_sums")
                own("log_sums")
                v.tensor_tensor(khat[:, 0:NS], AL[:, NS - 1:NS].to_broadcast([P, NS]), AL[:, 0:NS], ALU.subtract)
                v.tensor_tensor(khat[:, NS:C0], AL[:, C0 - 1:C0].to_broadcast([P, NM]), AL[:, NS:C0], ALU.subtract)
                V.done(v.tensor_tensor(khat[:, C0:T].rearrange("p (c n) -> p c n", c=4), AL[:, C0 + P - 1:T:P].unsqueeze(2).to_broadcast([P, 4, P]),
                                       AL[:, C0:T].rearrange("p (c n) -> p c n", c=4), ALU.subtract), "end_args")
                level_args(0)
                split_lo(N(3))
                dve.wait_ge(*S.after(i, "end_exp"))
                dve.wait_ge(evac_done, N(1) + 1)
                v.tensor_copy(bend[:, 0:2], qhat[:, NS - 1:C0:NM])
                V.done(v.tensor_copy(bend[:, 2:6], qhat[:, C0 + P - 1:T:P]), "ends")
                v.tensor_tensor(khat, khat, bk, ALU.mult)
                own("ends")
                V.done(v.tensor_tensor(qhat, qhat, bq, ALU.mult), "khat")
                own("khat")
                V.done(v.memset(qhat[:, NS:C0], 0.0), "meta_from_zero")
                split_lo(N(4))

                def level_scaled(lv):
                    w = 1 << lv
                    dve.wait_ge(*S.after(i, f"exp{lv}"))
                    if lv >= 2:
                        dve.wait_ge(*G.after(i, f"pairs{lv - 2}"))
                    for a, b in regions(lv):
                        def at(x, side):
                            return x[:, a:b].rearrange("p (n two w) -> p n two w", two=2, w=w)[:, :, side, :]
                        v.tensor_tensor(at(QK[lv % 2], 1), at(EE, 1), at(bq, 1), ALU.mult)
                        last = v.tensor_tensor(at(QK[lv % 2], 0), at(EE, 0), at(bk, 0), ALU.mult)
                    V.done(last, f"scaled{lv}")

                def level_masked(lv):
                    bank = br[lv % 2]
                    dve.wait_ge(*G.after(i, f"pairs{lv}"))
                    mo = CONST_AT["levels"][0] + P * lv
                    mk = masks[:, mo:mo + P]
                    dst = PT[lv % 2] if lv else PS
                    if lv >= 3:
                        dve.wait_ge(*Q.after(i, f"add{lv - 2}"))
                    if lv == 6:
                        V.done(v.memset(dst[0:C0, 0, 0:C0], 0.0), "no_pairs6")
                    else:
                        v.tensor_tensor(dst[0:C0, 0, 0:C0], bank[0:C0, 0:C0], mk[0:C0, 0:C0], ALU.mult)
                    V.done(v.tensor_tensor(dst[:, 1:5, :], bank[:, P:5 * P].rearrange("p (c n) -> p c n", c=4),
                                           mk.unsqueeze(1).to_broadcast([P, 4, P]), ALU.mult), f"masked{lv}")

                level_scaled(0)
                level_args(1)
                level_scaled(1)
                for lv in range(LEVELS + 1):
                    if lv + 2 < LEVELS:
                        level_args(lv + 2)
                    level_masked(lv)
                    if lv + 2 < LEVELS:
                        level_scaled(lv + 2)
                    if lv == 0:
                        split_lo(N(5))
                    elif lv == LEVELS - 1:
                        split_lo(N(6))
                dve.wait_ge(states_out, i * 32 + 16 * (2 * NH_A + 2 + 4 * NP_C))
                dve.wait_ge(*G.after(i, "updates"))
                dve.wait_ge(hgrn_in, i * 16 + 16)
                v.scalar_tensor_tensor(out=BST[:, 6, :], in0=BST[:, 0, :], scalar=bend[:, 0:1], in1=bra[:, 0:P], op0=ALU.mult, op1=ALU.add)
                V.done(v.tensor_copy(BST[:, 1, :], bra[:, P:2 * P]), "state1")
                for c in range(1, NCH):
                    own(f"state{c}")
                    V.done(v.scalar_tensor_tensor(out=BST[:, c + 1, :], in0=BST[:, c, :], scalar=bend[:, c + 1:c + 2],
                                                  in1=bra[:, P * c + P:P * c + 2 * P], op0=ALU.mult, op1=ALU.add), f"state{c + 1}" if c < 4 else "states")
                dve.wait_ge(evac_done, N(3) + 1)
                V.done(v.tensor_scalar(bez, bez, 1.0, None, ALU.add), "z1")
                own("z1")
                V.done(v.reciprocal(bez, bez), "z2")
                own("z2")
                V.done(v.scalar_tensor_tensor(out=bz, in0=bz, scalar=lbv[:, 5:6], in1=bez, op0=ALU.mult, op1=ALU.mult), "gate")
                dve.wait_ge(*S.after(i, "o_rstd"))
                for c in range(NCH):
                    n = LEN[c]
                    last = v.tensor_scalar(on[0:n, c, :], brb[0:n, P * c:P * c + P], bss[0:n, 1, c:c + 1], None, ALU.mult)
                V.done(last, "o_unit")
                dve.wait_ge(*G.after(i, "o_turned"))
                own("gate")
                dve.wait_ge(y_out, i * 16 + 16 * (NH_A + NP_C))
                v.tensor_tensor(ybuf[:, 0:SPLIT], bra[:, 0:SPLIT], bz[:, 0:SPLIT], ALU.mult)
                V.done(v.tensor_tensor(ybuf[:, SPLIT:T], bra[:, 512:512 + T - SPLIT], bz[:, SPLIT:T], ALU.mult), "y")

            for k in range(KT):
                dve.wait_ge(y_hi, k + 1)
                v.tensor_tensor(xl[:, k, :], YIN[:, place[k], :], xh[:, k, :].bitcast(F32), ALU.subtract).then_inc(y_split, 1)
            G, V, S = P_["merge_tensor"], P_["merge_vector"], P_["merge_scalar"]
            dve.wait_ge(y_split, KT)
            banks3 = [acc[0], acc[1], bra]
            with dve.Fori(0, KT // 2) as i:
                for j in range(2):
                    n = Num(PROJ_AT, 2, i, j)
                    split_lo(Num(PROJ_AT, 2, i, j + 1))
                    row = dve.snap(i * 2 + j)
                    z = ZF[:, bass.ds(row, 1), :].rearrange("p a t -> p (a t)")
                    dve.wait_ge(*S.after(i, f"gates{j}"))
                    for b in range(3):
                        if b < 2:
                            dve.wait_ge(*G.after(i, f"proj{b}_{j}"))
                        else:
                            dve.wait_ge(tile_done, n + 1)
                        dst = mz[b]
                        V.done(v.tensor_tensor(split2(dst), halves(banks3[b]), split2(gs[:, b, :]), ALU.mult), f"part{b}_{j}")
                        if b == 1:
                            dve.wait_ge(*V.after(i, f"part1_{j}"))
                            V.done(v.tensor_tensor(mz[0], mz[0], mz[1], ALU.add), f"sum1_{j}")
                    dve.wait_ge(*V.after(i, f"part2_{j}"))
                    V.done(v.tensor_tensor(z, mz[0], mz[2], ALU.add), f"merged{j}")
                    dve.wait_ge(*V.after(i, f"merged{j}"))

            for k in range(KT):
                dve.wait_ge(z_hi, k + 1)
                v.tensor_tensor(xl[:, k, :], ZF[:, k, :], xh[:, k, :].bitcast(F32), ALU.subtract).then_inc(z_split, 1)
            dve.wait_ge(z_split, KT)
            split_lo(OUT_AT + 1)
            G, V, S = O_["out_tensor"], O_["out_vector"], O_["out_scalar"]

            def rows_out(i, j, col):
                dve.wait_ge(*G.after(i, f"turned{j}"))
                v.tensor_copy(YT[:, 0:4, bass.ds(col, P)], br[j][:, 0:512].rearrange("p (t n) -> p t n", t=4))
                V.done(v.tensor_copy(YT[0:ROWS[4], 4, bass.ds(col, P)], br[j][0:ROWS[4], 512:640]), f"rows{j}")

            with dve.Fori(0, KT // 2 - 1) as i:
                for j in range(2):
                    split_lo(Num(OUT_AT, 2, i, j + 2))
                    rows_out(i, j, dve.snap(i * 256 + 128 * j))
            for j in range(2):
                rows_out(KT // 2 - 1, j, 128 * (14 + j))
            dve.wait_ge(*S.after(KT // 2 - 1, "squares1"))
            v.tensor_reduce(out=small[:, 24:28], in_=squares[:, 0:4, :], axis=AX.X, op=ALU.add)
            v.tensor_reduce(out=small[0:ROWS[4], 28:29], in_=squares[0:ROWS[4], 4:5, :], axis=AX.X, op=ALU.add).then_inc(r_sums, 1)
            dve.wait_ge(r_sums, 5)
            dve.wait_ge(*O_["out_pool"].after(KT // 2 - 1, "gains1"))
            for t in range(5):
                r = ROWS[t]
                dve.wait_ge(res_here[t], 16)
                v.scalar_tensor_tensor(out=xrow[t][0:r, :], in0=YT[0:r, t, :], scalar=small[0:r, 40 + t:41 + t], in1=xrow[t][0:r, :],
                                       op0=ALU.mult, op1=ALU.add).then_inc(res_done, 1)

        @block.gpsimd
        def _(pool):
            g = nc.gpsimd
            S = S0["setup_pool"]
            g.memset(small[:, :], 1.0)
            g.memset(eps[:, :], EPS)
            g.memset(gn_eps[:, :], GN_EPS)
            g.memset(tenln2[:, :], 10.0 * float(np.log(2.0)))
            g.memset(shpad[:, :], 0.0)
            g.memset(pk_all[:, :, :].rearrange("p a b -> p (a b)"), 0.0)
            g.memset(bss[:, :, :], 1.0)
            S.done(g.memset(ones8[:, :], 1.0), "zeros")
            pool.wait_ge(x_turned, KT)
            g.memset(LOWP[:, NS + 1:NS + 2], 0.0)
            pool.wait_ge(vecs_here, 16)
            g.tensor_copy(LOWP[:, 0:1], vec("low_cache"))
            S.done(g.memset(TK[:, 0, :], 0.0), "cleared")
            pool.wait_ge(*S0["setup_scalar"].after(0, "scalars"))
            pool.wait_ge(*S0["setup_vector"].after(0, "head_vectors"))
            g.memset(num[:, 0, :], 1.0)
            g.memset(aggr[:, :, :], 1.0)
            g.memset(smA[:, :, :], 1.0)
            S.done(g.memset(vtok[:, :, P:P + 1], 1.0), "mlstm_cleared")

            G, V, Sc, Q = (A_[k] for k in ("mlstm_tensor", "mlstm_vector", "mlstm_scalar", "mlstm_pool"))
            pool.wait_ge(consts_here, 16)
            pool.wait_ge(masks_here, 16)
            with pool.Fori(0, NH_A) as i:
                m = mask("causal")
                pool.wait_ge(*Sc.after(i, "decays"))
                g.tensor_tensor(WW[0:C0, 0, 0:C0], WW[0:C0, 0, 0:C0], m[0:C0, 0:C0], ALU.mult)
                Q.done(g.tensor_tensor(WW[:, 1:5, :], WW[:, 1:5, :], m[:, P:2 * P].unsqueeze(1).to_broadcast([P, 4, P]), ALU.mult), "masked")

            G, V, Sc, Q = (C_[k] for k in ("rwkv_tensor", "rwkv_vector", "rwkv_scalar", "rwkv_pool"))
            with pool.Fori(0, NP_C) as i:
                pool.wait_ge(*G.after(i, "yk1_"))
                each = ident.unsqueeze(1).to_broadcast([P, 10, P])
                Q.done(g.tensor_tensor(DDT[:, :, :], each, each, ALU.mult), "unit_blocks")

            G, V, Sc, Q = (B_[k] for k in ("hgrn_tensor", "hgrn_vector", "hgrn_scalar", "hgrn_pool"))
            with pool.Fori(0, NH_B) as i:
                for lv in range(1, LEVELS + 1):
                    pool.wait_ge(*V.after(i, f"masked{lv}"))
                    if lv > 1:
                        pool.wait_ge(*Q.after(i, f"add{lv - 1}"))
                    g.tensor_tensor(PS[0:C0, 0, 0:C0], PS[0:C0, 0, 0:C0], PT[lv % 2][0:C0, 0, 0:C0], ALU.add)
                    Q.done(g.tensor_tensor(PS[:, 1:5, :], PS[:, 1:5, :], PT[lv % 2][:, 1:5, :], ALU.add), f"add{lv}" if lv < LEVELS else "summed")

            S, Q = O_["out_scalar"], O_["out_pool"]
            pool.wait_ge(post_here, 16)

            def gained(i, j, col):
                pool.wait_ge(*S.after(i, f"squares{j}"))
                part = gain[:, bass.ds(col, P)]
                y4 = YT[:, 0:4, bass.ds(col, P)]
                g.tensor_tensor(y4, y4, part.unsqueeze(1).to_broadcast([P, 4, P]), ALU.mult)
                y1 = YT[0:ROWS[4], 4, bass.ds(col, P)]
                Q.done(g.tensor_tensor(y1, y1, part[0:ROWS[4]], ALU.mult), f"gains{j}")

            with pool.Fori(0, KT // 2 - 1) as i:
                for j in range(2):
                    gained(i, j, pool.snap(i * (2 * P) + P * j))
            for j in range(2):
                gained(KT // 2 - 1, j, P * (KT - 2 + j))


_OUTS = [
    ("y_prompt", (1, NP, D)), ("y_sample", (1, NS, D)),
    ("c_p", (1, 1, 8, P, P)), ("n_p", (1, 1, 8, P)), ("m_p", (1, 1, 8)), ("hs_p", (1, 1, 4, P, P)),
    ("rs_p", (1, 1, 8, 64, 64)), ("sh_p", (1, 1, 1, 2176)),
    ("c_s", (1, 1, 8, P, P)), ("n_s", (1, 1, 8, P)), ("m_s", (1, 1, 8)), ("hs_s", (1, 1, 4, P, P)),
    ("rs_s", (1, 1, 8, 64, 64)), ("sh_s", (1, 1, 1, 2176)),
]


def _columns():
    aq, ak, av, ao, az = 0, 1024, 2048, 3088, 4112
    b, c, g = 5136, 7184, 9360
    at, gate = [None, c + 1536], 0
    for i in range(NH_A):
        at += [x + P * i for x in (ak, av, aq, ao, az)]
        at += [g + P * (gate + k) for k in range(A_GATES)]
        gate += A_GATES
    for i in range(NP_C):
        at += [c + x + P * i for x in (512, 0, 1024, 1664)]
        at += [g + P * (gate + k) for k in range(C_GATES)]
        gate += C_GATES
    for i in range(NH_B):
        at += [b + x + P * i for x in (512, 0, 1024, 1536)]
        at += [g + P * (gate + k) for k in range(B_GATES)]
        gate += B_GATES
    assert len(at) == PROJ_AT and gate == 3 * KT
    return at


def _tile(w, at):
    return w[:, at:at + P].reshape(KT, P, P).transpose(1, 0, 2).reshape(P, D)


def kernel(**inputs):
    import concourse.bacc as _bacc
    from concourse.bass_utils import run_bass_kernel_spmd as _run

    a = {k: np.asarray(v) for k, v in inputs.items()}
    w_in = a["w_in"][0]
    gates = np.zeros((D, P), np.float32)
    gates[:, 0:8] = w_in[:, 3072:3080]
    gates[:, 32:40] = w_in[:, 3080:3088]
    w_proj = np.concatenate([a["w_proj_a"][0], a["w_proj_c"][0], a["w_proj_b"][0]], 0)
    tiles = [_tile(gates, 0) if c is None else _tile(w_in, c) for c in _columns()]
    tiles += [_tile(w_proj, P * j) for j in range(KT)] + [_tile(a["w_out"][0], P * j) for j in range(KT)]

    def cols(x):
        return x.reshape(-1, P).T

    def rows8(x):
        return np.concatenate([x.reshape(8, 1), np.zeros((P - 8, 1), np.float32)], 0)

    mu, cache = cols(a["rwkv_mu"][0]), cols(a["cache_rwkv_shift"][0, 0, 0])
    parts = [cols(a["norm_pre"][0]), cols(a["mlstm_norm"][0]), cols(a["hgrn_lb_logits"][0]), cols(a["hgrn_norm"][0]),
             rows8(a["mlstm_b_i"][0]), rows8(a["mlstm_b_f"][0]), rows8(a["state_mlstm_m"][0, 0]),
             a["state_mlstm_n"][0, 0].T, mu[:, 12:13], cache[:, 12:13]]
    for p in range(NP_C):
        parts += [x[:, t + p:t + p + 1] for x in (mu, cache) for t in (0, 4, 8, 13)]
        parts += [cols(a[k][0])[:, p:p + 1] for k in ("rwkv_w0", "rwkv_a0", "rwkv_k_k", "rwkv_k_a", "rwkv_r_k", "rwkv_gn_g", "rwkv_gn_b")]
        parts += [np.zeros((P, 1), np.float32)]
    ranks = np.concatenate([a["rwkv_w_up"][0], a["rwkv_a_up"][0]], 0)
    arrays = {
        "x_all": np.concatenate([a["x_sample"][0], a["meta_tokens"], a["x_prompt"][0]], 0),
        "w_stream": np.stack(tiles),
        "full_in": FULL,
        "masks_in": MASKS.astype(mybir.dt.np(mybir.dt.bfloat16)),
        "vecs_in": np.ascontiguousarray(np.concatenate(parts, 1)),
        "low_in": np.ascontiguousarray(ranks.reshape(P, NP_C, P).transpose(1, 0, 2)),
        "c0_in": np.ascontiguousarray(a["state_mlstm_C"][0, 0]),
        "hgrn_s0": np.ascontiguousarray(a["state_hgrn_S"][0, 0]),
        "rwkv_s0": np.ascontiguousarray(a["state_rwkv_S"][0, 0]),
        "norm_post": np.ascontiguousarray(a["norm_post"][0]),
    }
    nc = _bacc.Bacc("TRN2", target_bir_lowering=False, num_devices=1)
    args = {k: nc.dram_tensor(f"in_{k}", x.shape, mybir.dt.from_np(x.dtype), kind="ExternalInput").ap() for k, x in arrays.items()}
    outs = {k: nc.dram_tensor(f"out_{k}", s, F32, kind="ExternalOutput").ap() for k, s in _OUTS}
    views = {
        "y_prompt": outs["y_prompt"][0], "y_sample": outs["y_sample"][0],
        **{k: outs[k][0, 0] for k in outs if k[:2] in ("c_", "n_", "hs", "rs")},
        **{k: outs[k][0, 0].rearrange("(h a) -> h a", a=1) for k in ("m_p", "m_s")},
        **{k: outs[k][0, 0, 0].rearrange("(k p) -> k p", p=P) for k in ("sh_p", "sh_s")},
    }
    build(nc, **args, **views)
    r = _run(nc, [{f"in_{k}": x for k, x in arrays.items()}], core_ids=[0])
    return tuple(r.results[0][f"out_{k}"] for k, _ in _OUTS)
```
